# Optimizing a Trainium2 kernel written in Bass

```python
import math
import jax
import jax.numpy as jnp
from jax import lax
import numpy as np

D_MODEL = 2048
BATCH = 1
SEQ = 256
DEPTH = 2

GRID_W = 64
CTX_LEN = 256
HEAD_DIM = 128
A_Q_HEADS = 8
A_KV_HEADS = 2
B_Q_HEADS = 8
B_KV_HEADS = 2
WINDOW = 128
ATTN_BLOCK = 128
ROPE_THETA = 10000.0
AXIS_DIM = HEAD_DIM // 2
Q_WIDTH = (A_Q_HEADS + B_Q_HEADS) * HEAD_DIM
KV_WIDTH = (A_KV_HEADS + B_KV_HEADS) * HEAD_DIM
ATTN_IN_WIDTH = Q_WIDTH + 2 * KV_WIDTH
HYENA_ORDER = 2
HYENA_IN_WIDTH = (HYENA_ORDER + 1) * D_MODEL
SHORT_CONV = 3
FILTER_EMB = 33
FILTER_HIDDEN = 64
DECAY_TARGET = 1e-2
FAST_DECAY_PCT = 0.3
SLOW_DECAY_PCT = 1.5
MAX_DECAY = math.log(DECAY_TARGET) / FAST_DECAY_PCT
MIN_DECAY = math.log(DECAY_TARGET) / SLOW_DECAY_PCT
D_FF = 4 * D_MODEL
N_MOD = 6
N_ATTN_LAYERS = (DEPTH + 1) // 2
N_HYENA_LAYERS = DEPTH // 2
EPS = 1e-6

kernel_name = 'hybrid_swa_axial_hyena_dit_block'

def rms_norm(x, g):
    x32 = x.astype(jnp.float32)
    y = x32 * lax.rsqrt(jnp.mean(x32 * x32, axis=-1, keepdims=True) + EPS)
    return y.astype(x.dtype) * g

def modulate(h, shift, scale):
    return h * (1 + scale) + shift

def axial_rope_tables(n_tok):
    rows = n_tok // GRID_W
    row = jnp.repeat(jnp.arange(rows, dtype=jnp.float32), GRID_W)
    col = jnp.tile(jnp.arange(GRID_W, dtype=jnp.float32), rows)
    inv = ROPE_THETA ** (-jnp.arange(0, AXIS_DIM, 2, dtype=jnp.float32) / AXIS_DIM)
    ang_r = row[:, None] * inv[None]
    ang_c = col[:, None] * inv[None]
    return (jnp.cos(ang_r), jnp.sin(ang_r), jnp.cos(ang_c), jnp.sin(ang_c))

def _rotate(x, cos, sin):
    x1, x2 = jnp.split(x, 2, axis=-1)
    cos = cos[:, None, :].astype(x.dtype)
    sin = sin[:, None, :].astype(x.dtype)
    return jnp.concatenate([x1 * cos - x2 * sin, x2 * cos + x1 * sin], axis=-1)

def apply_axial_rope(x, rope):
    cos_r, sin_r, cos_c, sin_c = rope
    xr, xc = jnp.split(x, 2, axis=-1)
    return jnp.concatenate([_rotate(xr, cos_r, sin_r), _rotate(xc, cos_c, sin_c)], axis=-1)

def _split_cols(t, sizes):
    idx = [int(v) for v in np.cumsum(sizes)[:-1]]
    return jnp.split(t, idx, axis=-1)

def _heads(t):
    return t.reshape(t.shape[0], t.shape[1], -1, HEAD_DIM)

def _gqa(q, n_kv):
    b, s, hq, dh = q.shape
    return q.reshape(b, s, n_kv, hq // n_kv, dh)

def window_attention(q, k, v, k_ctx, v_ctx, sink):
    b, s, hkv, g, dh = q.shape
    nb = s // ATTN_BLOCK
    nw = -(-WINDOW // ATTN_BLOCK)
    kw_len = (2 * nw + 1) * ATTN_BLOCK
    n_ctx = k_ctx.shape[1]
    qb = q.reshape(b, nb, ATTN_BLOCK, hkv, g, dh)
    pad = ((0, 0), (nw * ATTN_BLOCK, nw * ATTN_BLOCK), (0, 0), (0, 0))
    kp = jnp.pad(k, pad).reshape(b, nb + 2 * nw, ATTN_BLOCK, hkv, dh)
    vp = jnp.pad(v, pad).reshape(b, nb + 2 * nw, ATTN_BLOCK, hkv, dh)
    kw = jnp.concatenate([kp[:, o:o + nb] for o in range(2 * nw + 1)], axis=2)
    vw = jnp.concatenate([vp[:, o:o + nb] for o in range(2 * nw + 1)], axis=2)
    blk = jnp.arange(nb)[:, None] * ATTN_BLOCK
    q_pos = blk + jnp.arange(ATTN_BLOCK)[None]
    k_pos = blk - nw * ATTN_BLOCK + jnp.arange(kw_len)[None]
    valid = (jnp.abs(k_pos[:, None, :] - q_pos[:, :, None]) <= WINDOW) & ((k_pos >= 0) & (k_pos < s))[:, None, :]
    s_loc = jnp.einsum('bnqhgd,bnkhd->bnhgqk', qb, kw).astype(jnp.float32)
    s_loc = jnp.where(valid[None, :, None, None], s_loc, -jnp.inf)
    s_ctx = jnp.einsum('bnqhgd,bchd->bnhgqc', qb, k_ctx).astype(jnp.float32)
    s_sink = jnp.broadcast_to(sink.astype(jnp.float32).reshape(hkv, g)[None, None, :, :, None, None], s_loc.shape[:-1] + (1,))
    p = jax.nn.softmax(jnp.concatenate([s_loc, s_ctx, s_sink], axis=-1), axis=-1).astype(v.dtype)
    o = (jnp.einsum('bnhgqk,bnkhd->bnqhgd', p[..., :kw_len], vw)
         + jnp.einsum('bnhgqc,bchd->bnqhgd', p[..., kw_len:kw_len + n_ctx], v_ctx))
    return o.reshape(b, s, hkv * g, dh)

def global_attention(q, k_all, v_all):
    b, s, hkv, g, dh = q.shape
    nb = s // ATTN_BLOCK
    qb = jnp.moveaxis(q.reshape(b, nb, ATTN_BLOCK, hkv, g, dh), 1, 0)

    def one_block(q_blk):
        sc = jnp.einsum('bqhgd,bkhd->bhgqk', q_blk, k_all).astype(jnp.float32)
        p = jax.nn.softmax(sc, axis=-1).astype(v_all.dtype)
        return jnp.einsum('bhgqk,bkhd->bqhgd', p, v_all)

    o = lax.map(one_block, qb)
    return jnp.moveaxis(o, 0, 1).reshape(b, s, hkv * g, dh)

def context_attention(q, k, v, sink=None):
    b, n, hkv, g, dh = q.shape
    sc = jnp.einsum('bqhgd,bkhd->bhgqk', q, k).astype(jnp.float32)
    if sink is not None:
        s_sink = jnp.broadcast_to(sink.astype(jnp.float32).reshape(hkv, g)[None, :, :, None, None], sc.shape[:-1] + (1,))
        p = jax.nn.softmax(jnp.concatenate([sc, s_sink], axis=-1), axis=-1)[..., :-1]
    else:
        p = jax.nn.softmax(sc, axis=-1)
    o = jnp.einsum('bhgqk,bkhd->bqhgd', p.astype(v.dtype), v)
    return o.reshape(b, n, hkv * g, dh)

def attention_mixer(h_lat, h_ctx, w_in, w_out, sink, q_norm, k_norm, rope, ctx_out):
    b, s, _ = h_lat.shape
    n_ctx = h_ctx.shape[1]
    scale = HEAD_DIM ** -0.5
    kv_sizes = [A_KV_HEADS * HEAD_DIM, B_KV_HEADS * HEAD_DIM, A_KV_HEADS * HEAD_DIM, B_KV_HEADS * HEAD_DIM]
    q_sizes = [A_Q_HEADS * HEAD_DIM, B_Q_HEADS * HEAD_DIM]
    qa, qb, ka, kb, va, vb = [_heads(t) for t in _split_cols(h_lat @ w_in, q_sizes + kv_sizes)]
    qb = rms_norm(qb, q_norm)
    kb = rms_norm(kb, k_norm)
    qa, ka, qb, kb = [apply_axial_rope(t, rope) for t in (qa, ka, qb, kb)]
    ka_c, kb_c, va_c, vb_c = [_heads(t) for t in _split_cols(h_ctx @ w_in[:, Q_WIDTH:], kv_sizes)]
    kb_c = rms_norm(kb_c, k_norm)
    o_a = window_attention(_gqa(qa * scale, A_KV_HEADS), ka, va, ka_c, va_c, sink)
    o_b = global_attention(_gqa(qb * scale, B_KV_HEADS),
                           jnp.concatenate([kb_c, kb], axis=1), jnp.concatenate([vb_c, vb], axis=1))
    y_lat = jnp.concatenate([o_a, o_b], axis=2).reshape(b, s, Q_WIDTH) @ w_out
    if not ctx_out:
        return y_lat, None
    qa_c, qb_c = [_heads(t) for t in _split_cols(h_ctx @ w_in[:, :Q_WIDTH], q_sizes)]
    qb_c = rms_norm(qb_c, q_norm)
    o_ac = context_attention(_gqa(qa_c * scale, A_KV_HEADS), ka_c, va_c, sink)
    o_bc = context_attention(_gqa(qb_c * scale, B_KV_HEADS), kb_c, vb_c)
    y_ctx = jnp.concatenate([o_ac, o_bc], axis=2).reshape(b, n_ctx, Q_WIDTH) @ w_out
    return y_lat, y_ctx

def hyena_filters(n_tok, w1, b1, fr1, w2, b2, fr2, w3):
    f32 = jnp.float32
    bands = (FILTER_EMB - 1) // 2
    t = jnp.linspace(0.0, 1.0, n_tok, dtype=f32)[:, None]
    w = 2.0 * math.pi * jnp.arange(n_tok, dtype=f32)[:, None] / n_tok
    f = jnp.linspace(1e-4, bands - 1, bands, dtype=f32)[None]
    feats = jnp.concatenate([t, jnp.cos(f * w), -jnp.sin(f * w)], axis=-1)
    hid = jnp.sin(fr1.astype(f32) * (feats @ w1.astype(f32) + b1.astype(f32)))
    hid = jnp.sin(fr2.astype(f32) * (hid @ w2.astype(f32) + b2.astype(f32)))
    h = (hid @ w3.astype(f32)).reshape(n_tok, HYENA_ORDER, D_MODEL)
    offs = jnp.abs(jnp.arange(n_tok) - n_tok // 2).astype(f32) * (2.0 / n_tok)
    deltas = jnp.abs(jnp.linspace(MIN_DECAY, MAX_DECAY, D_MODEL, dtype=f32))
    h = h * jnp.exp(-offs[:, None, None] * deltas[None, None, :])
    return h * lax.rsqrt(jnp.sum(h * h, axis=0, keepdims=True) + EPS)

def centred_long_conv(z, h):
    n_tok = z.shape[1]
    n_fft = 2 * n_tok
    zf = jnp.fft.rfft(z.astype(jnp.float32), n=n_fft, axis=1)
    hf = jnp.fft.rfft(h, n=n_fft, axis=0)
    y = jnp.fft.irfft(zf * hf[None], n=n_fft, axis=1)[:, n_tok // 2:n_tok // 2 + n_tok]
    return y.astype(z.dtype)

def centred_short_conv(u, w, b):
    n_tok = u.shape[1]
    half = SHORT_CONV // 2
    up = jnp.pad(u, ((0, 0), (half, half), (0, 0)))
    return sum(up[:, k:k + n_tok] * w[k] for k in range(SHORT_CONV)) + b

def hyena_mixer(h, w_in, b_in, conv_w, conv_b, filt, skip, w_out, b_out):
    u = centred_short_conv(h @ w_in + b_in, conv_w, conv_b)
    x1, x2, v = jnp.split(u, HYENA_ORDER + 1, axis=-1)
    z = x1 * (centred_long_conv(v, filt[:, 0]) + v * skip[0])
    z = x2 * (centred_long_conv(z, filt[:, 1]) + z * skip[1])
    return z @ w_out + b_out

def sq_relu_mlp(h, w1, w2):
    return jnp.square(jax.nn.relu(h @ w1)) @ w2

def setup_inputs(seed: int = 0) -> dict:
    key = jax.random.key(seed)
    ks = iter(jax.random.split(key, 40))

    def nrm(shape, scale):
        return scale * jax.random.normal(next(ks), shape, jnp.float32)

    D = D_MODEL
    NA = N_ATTN_LAYERS
    NH = N_HYENA_LAYERS
    return {
        'x': nrm((BATCH, SEQ, D), 1.0),
        'c': nrm((BATCH, D), 1.0),
        'ctx': nrm((BATCH, CTX_LEN, D), 1.0),
        'c_ctx': nrm((D,), 1.0),
        'mod_w': nrm((DEPTH, D, N_MOD * D), 0.5 * D ** -0.5),
        'mod_b': nrm((DEPTH, N_MOD * D), 0.01),
        'norm_mix_g': 1.0 + nrm((DEPTH, D), 0.02),
        'norm_mlp_g': 1.0 + nrm((DEPTH, D), 0.02),
        'attn_w_in': nrm((NA, D, ATTN_IN_WIDTH), D ** -0.5),
        'attn_w_out': nrm((NA, Q_WIDTH, D), Q_WIDTH ** -0.5),
        'attn_sink': nrm((NA, A_Q_HEADS), 1.0),
        'attn_q_norm': 1.0 + nrm((NA, HEAD_DIM), 0.02),
        'attn_k_norm': 1.0 + nrm((NA, HEAD_DIM), 0.02),
        'hy_w_in': nrm((NH, D, HYENA_IN_WIDTH), D ** -0.5),
        'hy_b_in': nrm((NH, HYENA_IN_WIDTH), 0.01),
        'hy_conv_w': nrm((NH, SHORT_CONV, HYENA_IN_WIDTH), SHORT_CONV ** -0.5),
        'hy_conv_b': nrm((NH, HYENA_IN_WIDTH), 0.01),
        'hy_f_w1': nrm((NH, FILTER_EMB, FILTER_HIDDEN), FILTER_EMB ** -0.5),
        'hy_f_b1': nrm((NH, FILTER_HIDDEN), 0.1),
        'hy_f_freq1': 1.0 + nrm((NH, FILTER_HIDDEN), 0.02),
        'hy_f_w2': nrm((NH, FILTER_HIDDEN, FILTER_HIDDEN), FILTER_HIDDEN ** -0.5),
        'hy_f_b2': nrm((NH, FILTER_HIDDEN), 0.1),
        'hy_f_freq2': 1.0 + nrm((NH, FILTER_HIDDEN), 0.02),
        'hy_f_w3': nrm((NH, FILTER_HIDDEN, HYENA_ORDER * D), FILTER_HIDDEN ** -0.5),
        'hy_skip': nrm((NH, HYENA_ORDER, D), 0.5),
        'hy_w_out': nrm((NH, D, D), D ** -0.5),
        'hy_b_out': nrm((NH, D), 0.01),
        'mlp_w1': nrm((DEPTH, D, D_FF), D ** -0.5),
        'mlp_w2': nrm((DEPTH, D_FF, D), D_FF ** -0.5),
        'final_g': 1.0 + nrm((D,), 0.02),
    }

def reference(x, c, ctx, c_ctx, mod_w, mod_b, norm_mix_g, norm_mlp_g,
              attn_w_in, attn_w_out, attn_sink, attn_q_norm, attn_k_norm,
              hy_w_in, hy_b_in, hy_conv_w, hy_conv_b, hy_f_w1, hy_f_b1, hy_f_freq1,
              hy_f_w2, hy_f_b2, hy_f_freq2, hy_f_w3, hy_skip, hy_w_out, hy_b_out,
              mlp_w1, mlp_w2, final_g):
    n_lat = x.shape[1]
    n_ctx = ctx.shape[1]
    rope = axial_rope_tables(n_lat)
    last_ctx_layer = 2 * ((DEPTH - 1) // 2)
    c_act = jax.nn.silu(c)
    cc_act = jax.nn.silu(c_ctx)
    ctx_s = ctx
    for i in range(DEPTH):
        j = i // 2
        is_attn = (i % 2 == 0)
        ctx_updated = i < last_ctx_layer
        mod = (c_act @ mod_w[i] + mod_b[i])[:, None, :]
        sh1, sc1, g1, sh2, sc2, g2 = jnp.split(mod, N_MOD, axis=-1)
        h_lat = modulate(rms_norm(x, norm_mix_g[i]), sh1, sc1)
        if is_attn or ctx_updated:
            mod_c = cc_act @ mod_w[i] + mod_b[i]
            csh1, csc1, cg1, csh2, csc2, cg2 = jnp.split(mod_c, N_MOD, axis=-1)
            h_ctx = modulate(rms_norm(ctx_s, norm_mix_g[i]), csh1, csc1)
        if is_attn:
            y_lat, y_ctx = attention_mixer(h_lat, h_ctx, attn_w_in[j], attn_w_out[j], attn_sink[j],
                                           attn_q_norm[j], attn_k_norm[j], rope, ctx_updated)
        else:
            fparams = (hy_f_w1[j], hy_f_b1[j], hy_f_freq1[j], hy_f_w2[j], hy_f_b2[j], hy_f_freq2[j], hy_f_w3[j])
            y_lat = hyena_mixer(h_lat, hy_w_in[j], hy_b_in[j], hy_conv_w[j], hy_conv_b[j],
                                hyena_filters(n_lat, *fparams), hy_skip[j], hy_w_out[j], hy_b_out[j])
            if ctx_updated:
                y_ctx = hyena_mixer(h_ctx, hy_w_in[j], hy_b_in[j], hy_conv_w[j], hy_conv_b[j],
                                    hyena_filters(n_ctx, *fparams), hy_skip[j], hy_w_out[j], hy_b_out[j])
        x = x + g1 * y_lat
        x = x + g2 * sq_relu_mlp(modulate(rms_norm(x, norm_mlp_g[i]), sh2, sc2), mlp_w1[i], mlp_w2[i])
        if ctx_updated:
            ctx_s = ctx_s + cg1 * y_ctx
            ctx_s = ctx_s + cg2 * sq_relu_mlp(modulate(rms_norm(ctx_s, norm_mlp_g[i]), csh2, csc2), mlp_w1[i], mlp_w2[i])
    return rms_norm(x, final_g)


_drawn_inputs = setup_inputs


def setup_inputs(seed=0):
    import zlib

    import numpy as np

    out = dict(_drawn_inputs(seed))
    spreads = {}
    factors = {'norm_mix_g': 2.884,
     'norm_mlp_g': 4.523,
     'attn_sink': 64.0,
     'attn_q_norm': 8.0,
     'attn_k_norm': 8.0,
     'hy_b_in': 12.164,
     'hy_conv_b': 12.977,
     'hy_f_freq1': 4.704,
     'hy_f_freq2': 5.087,
     'hy_b_out': 200.0,
     'final_g': 24.79}
    for name, (base, spread) in spreads.items():
        noise = np.random.default_rng([zlib.crc32(name.encode()), seed]).standard_normal(out[name].shape)
        drawn = base * np.exp(spread * noise) if base else spread * noise
        out[name] = jnp.asarray(drawn.astype(out[name].dtype))
    for name, factor in factors.items():
        out[name] = (out[name] * factor).astype(out[name].dtype)
    return out
```

```python
import math
from contextlib import ExitStack

import numpy as np

import concourse.bass as bass
from concourse import mybir

P = 128
D = 2048
TOK = 256
KB = D // P
D_FF = 4 * D
GRID_W = 64
HEAD = 128
THETA = 10000.0
WINDOW = 128
EPS = 1e-6
QSCALE = HEAD ** -0.5
HEADS = 16
A_HEADS = 8
KV_HEADS = 4
KV_COL = HEADS * HEAD
FILTER_EMB = 33
HID = 64
TARGET = 1e-2
MAX_DECAY = math.log(TARGET) / 0.3
MIN_DECAY = math.log(TARGET) / 1.5
NFREQ = 256
N_MOD = 6

UNIT_KB = 4
UNIT_COLS = 256
SLAB = 1024
RING = 4
MAGIC = 1.5 * 2.0 ** 23

F32 = mybir.dt.float32
F32R = mybir.dt.float32r
ACT = mybir.ActivationFunctionType
ALU = mybir.AluOpType
AX = mybir.AxisListType
ds = bass.ds

VECS = {}
_at = 0
for _name, _n in (("c", KB), ("c_ctx", KB), ("mod_b", 2 * N_MOD * KB), ("mix_g", 2 * KB), ("mlp_g", 2 * KB),
                  ("final_g", KB), ("b_in", 3 * KB), ("conv_w", 9 * KB), ("conv_b", 3 * KB), ("skip", 2 * KB),
                  ("b_out", KB), ("q_norm", 1), ("k_norm", 1), ("sink", A_HEADS)):
    VECS[_name] = _at
    _at += _n
N_VECS = _at
IDENT, SWAP, N_CONST = 0, P, 2 * P
COS, SIN, MASK, N_ROPE = 0, TOK, 2 * TOK, 3 * TOK


def constants():
    f32 = np.float32
    ident = np.eye(P, dtype=f32)
    swap = np.zeros((P, P), f32)
    for m in range(P):
        swap[m ^ 32, m] = 1.0
    tok = np.arange(TOK)
    inv = THETA ** (-np.arange(0, HEAD // 2, 2, dtype=f32) / f32(HEAD // 2))
    ang = np.empty((P, TOK), f32)
    for m in range(P):
        pos = (tok // GRID_W if m < HEAD // 2 else tok % GRID_W).astype(f32)
        ang[m] = pos * f32(inv[m % 32])
    sign = np.where((np.arange(P) // 32) % 2 == 0, -1.0, 1.0)[:, None]
    q = np.arange(P)[:, None]
    k = np.arange(P)[None]
    mask = np.stack([np.where(k + P - q <= WINDOW, 0.0, -1e30), np.where(q + P - k <= WINDOW, 0.0, -1e30)], 1)
    const = np.concatenate([ident, swap], 1)
    rope = np.concatenate([np.cos(ang), np.sin(ang) * sign, mask.reshape(P, 2 * P)], 1)
    t = np.arange(TOK)[:, None]
    f = np.arange(NFREQ)[None] + 0.5
    th = np.pi * f * t / TOK
    fwd = np.concatenate([np.cos(th), -np.sin(th)], 1).reshape(2, P, 2 * NFREQ).transpose(1, 0, 2)
    n = np.arange(TOK)[None] + TOK // 2
    ph = np.pi * (np.arange(NFREQ)[:, None] + 0.5) * n / TOK
    back = np.concatenate([np.cos(ph), -np.sin(ph)], 0) / TOK
    back = back.reshape(4, P, TOK).transpose(1, 0, 2)
    bands = (FILTER_EMB - 1) // 2
    w = (2.0 * np.pi * np.arange(TOK) / TOK)[:, None]
    fb = np.linspace(1e-4, bands - 1, bands)[None]
    feats = np.concatenate([np.linspace(0.0, 1.0, TOK)[:, None], np.cos(fb * w), -np.sin(fb * w)], 1).T
    offs = np.abs(np.arange(TOK) - TOK // 2) * (2.0 / TOK)
    deltas = np.abs(np.linspace(MIN_DECAY, MAX_DECAY, D))
    decay = np.exp(-offs[:, None] * deltas[None]).reshape(2, P, 4, 512).transpose(2, 1, 0, 3)
    return {k: np.ascontiguousarray(v, dtype=f32) for k, v in
            (("const", const), ("rope", rope), ("fwd", fwd), ("back", back), ("feats", feats), ("decay", decay))}


def build(nc, a):
    stack = ExitStack()

    def sem(name):
        return stack.enter_context(nc.semaphore(name))

    def sb(name, shape, dt=F32, scope=None):
        return (scope or stack).enter_context(nc.sbuf_tensor(name, shape, dt))

    with stack:
        x = sb("x", [P, KB, TOK])
        vecs = sb("vecs", [P, N_VECS])
        const = sb("const", [P, N_CONST])
        mod = sb("mod", [P, 2 * N_MOD * KB])
        mod_ctx = sb("mod_ctx", [P, 2 * KB])
        silu = sb("silu", [P, 2 * KB])
        silu_e = sb("silu_e", [P, 2 * KB])
        gain = sb("gain", [P, 2 * KB])
        gate_bias = sb("gate_bias", [P, KB])
        ones = sb("ones", [P, 2])
        neg_sink = sb("neg_sink", [P, A_HEADS])
        rs_a, rs_r = sb("rs_a", [P, 32]), sb("rs_r", [P, 32])
        rs_y, rs_t = sb("rs_y", [P, 32]), sb("rs_t", [P, 32])
        rs_lat, rs_ctx = sb("rs_lat", [P, 2]), sb("rs_ctx", [P, 2])
        rs_k, rs_q = sb("rs_k", [P, 8]), sb("rs_q", [P, 16])
        rs_filter = sb("rs_filter", [P, 32])
        raw = sb("raw", [P, RING, UNIT_KB, UNIT_COLS])
        w_hi = sb("w_hi", [P, RING, UNIT_KB, UNIT_COLS], F32R)
        w_lo = sb("w_lo", [P, RING, UNIT_KB, UNIT_COLS], F32R)
        slab = sb("slab", [P, RING, SLAB])
        acc = sb("acc", [P, 2, SLAB])
        lo_sum = sb("lo_sum", [P, 2, 2, TOK])
        sum_sb = sb("sum_sb", [P, 2, 2, TOK])
        with ExitStack() as early:
            s = early
            hid_a, hid_k, hid_1 = (sb(n, [HID, TOK], scope=s) for n in ("hid_a", "hid_k", "hid_1"))
            hid_2 = sb("hid_2", [HID, TOK], scope=s)
            f_w = sb("f_w", [HID, 2 * HID + 4], scope=s)
            feats = sb("feats", [FILTER_EMB, TOK], scope=s)
            w3 = sb("w3", [HID, 2, 2, 512], scope=s)
            decay = sb("decay", [P, 2, 2, 512], scope=s)
            taps = sb("taps", [P, 2, 2, 512], scope=s)
            taps_sq = sb("taps_sq", [P, 2, 512], scope=s)
            spec = sb("spec", [P, 4, 512], scope=s)
            fwd0 = sb("fwd0", [P, 2, 2 * NFREQ], scope=s)
        with ExitStack() as mid:
            s = mid
            probs = sb("probs", [P, 2, 512], scope=s)
            probs_t = sb("probs_t", [P, 2, 4, TOK], scope=s)
            q_rot = sb("q_rot", [P, 2, TOK], scope=s)
            q_sin = sb("q_sin", [P, 2, TOK], scope=s)
            k_sq = sb("k_sq", [P, 4, TOK], scope=s)
            sm = sb("sm", [P, 2, 4], scope=s)
            v = sb("v", [P, KV_HEADS, 4, HEAD], scope=s)
        lat = sb("lat", [P, KB, 2 * TOK], F32R)
        alt = sb("alt", [P, KB, 2 * TOK], F32R)
        with ExitStack() as s:
            sq = sb("sq", [P, 2, 4, TOK], scope=s)
            hm = sb("hm", [P, 2, 4, TOK], scope=s)
            xc = sb("xc", [P, KB, TOK], scope=s)
        with ExitStack() as s:
            q = sb("q", [P, HEADS, TOK], scope=s)
            kt = sb("kt", [P, KV_HEADS, 2 * TOK], scope=s)
            vt = sb("vt", [P, KV_HEADS, 2 * TOK], scope=s)
            rope = sb("rope", [P, N_ROPE], scope=s)
            cos_q, cos_k = sb("cos_q", [P, TOK], scope=s), sb("cos_k", [P, TOK], scope=s)
            swap_q, swap_k = sb("swap_q", [P, P], scope=s), sb("swap_k", [P, P], scope=s)
        with ExitStack() as s:
            u = sb("u", [P, 3, 4, TOK], scope=s)
            z_tok = sb("z_tok", [P, 2, 512], scope=s)
            h_spec = sb("h_spec", [P, 4, 512], scope=s)
            y_spec = sb("y_spec", [P, 4, 512], scope=s)
            fwd = sb("fwd", [P, 2, 2 * NFREQ], scope=s)
            back = sb("back", [P, 4, TOK], scope=s)
        ps = stack.enter_context(nc.psum_tensor("ps", [P, 8, 512], F32))
        spec_dram = nc.dram_tensor("spec_dram", (8, P, 4, 512), F32, kind="Internal").ap()

        ident = const[:, IDENT:IDENT + P]
        swap = const[:, SWAP:SWAP + P]
        cos, sin = rope[:, COS:COS + TOK], rope[:, SIN:SIN + TOK]
        mask = rope[:, MASK:MASK + 2 * P].rearrange("p (b k) -> p b k", b=2)

        def vec(name, i=0, n=1):
            return vecs[:, ds(VECS[name] + i, n)]

        in_const, in_vecs, in_x, in_ctx = sem("in_const"), sem("in_vecs"), sem("in_x"), sem("in_ctx")
        in_fw, in_w1, in_feats, in_fwd0 = sem("in_fw"), sem("in_w1"), sem("in_feats"), sem("in_fwd0")
        in_rope = sem("in_rope")
        in_fwd, in_back = sem("in_fwd"), sem("in_back")
        in_w3 = [sem("in_w3_0"), sem("in_w3_1")]
        in_decay = [sem("in_decay_0"), sem("in_decay_1")]
        unit_landed = [sem(f"unit_landed{j}") for j in range(RING)]
        slab_landed = [sem(f"slab_landed{j}") for j in range(RING)]
        hi_ready, split_ready = sem("hi_ready"), sem("split_ready")
        units_done = sem("units_done")
        lo_copied, psum_free = sem("lo_copied"), sem("psum_free")
        slabs_used, acc_ready = sem("slabs_used"), sem("acc_ready")
        mod_cols, mod_ready = sem("mod_cols"), sem("mod_ready")
        started = sem("started")
        silu_exp, silu_v = sem("silu_exp"), sem("silu_v")
        tables = sem("tables")
        squares, square_sums = sem("squares"), sem("square_sums")
        rs_v, rs_root = sem("rs_v"), sem("rs_root")
        rs_spread = sem("rs_spread")
        gains, normed, norm_hi, norm_ready = sem("gains"), sem("normed"), sem("norm_hi"), sem("norm_ready")
        x_hi_added = sem("x_hi_added")
        squared, hidden_hi, hidden_ready = sem("squared"), sem("hidden_hi"), sem("hidden_ready")
        centred, tapped = sem("centred"), sem("tapped")
        hid_mm, hid_v, hid_sin = sem("hid_mm"), sem("hid_v"), sem("hid_sin")
        taps_mm, taps_ready, taps_squared = sem("taps_mm"), sem("taps_ready"), sem("taps_squared")
        taps_summed = sem("taps_summed")
        spec_mm, spec_copied, spec_stored = sem("spec_mm"), sem("spec_copied"), sem("spec_stored")
        vt_turned, v_ready = sem("vt_turned"), sem("v_ready")
        k_swapped, k_v, k_squared, kq_sums, k_spread = (sem(n) for n in (
            "k_swapped", "k_v", "k_squared", "kq_sums", "k_spread"))
        q_swapped, q_v = sem("q_swapped"), sem("q_v")
        scores, scored_v, row_max, exp_done, prob_v, probs_turned, probs_copied = (sem(n) for n in (
            "scores", "scored_v", "row_max", "exp_done", "prob_v", "probs_turned", "probs_copied"))
        scored_w = sem("scored_w")
        head_out, head_hi, head_ready = sem("head_out"), sem("head_hi"), sem("head_ready")
        h_landed = sem("h_landed")
        turned, tok_ready, z_spec, spec_v, y_back = (sem(n) for n in (
            "turned", "tok_ready", "z_spec", "spec_v", "y_back"))
        conv_v, z_hi, z_ready = sem("conv_v"), sem("z_hi"), sem("z_ready")
        out_v, stored = sem("out_v"), sem("stored")

        T_Q, T_KV, T_OUT, T_MLP0 = 1, 5, 7, 11
        T_HY = T_MLP0 + 32
        T_HOUT = T_HY + 12
        T_MLP1 = T_HOUT + 4
        M_START, M_Q = 0, 16
        M_KV, M_ATT = M_Q + 8, M_Q + 12
        M_OUT = M_ATT + 8
        M_MLP0 = M_OUT + 8
        M_HY = M_MLP0 + 32
        M_HOUT = M_HY + 16
        M_END = M_HOUT + 4
        FIN_Q, FIN_KV, FIN_ATT, FIN_OUT, FIN_MLP0 = 4, 5, 6, 7, 8
        FIN_HY = FIN_MLP0 + 8
        FIN_HOUT = FIN_HY + 4
        half = SLAB // P

        class Slabs:

            def __init__(self, layer, halves, per, m4, first_kb=0):
                self.layer, self.halves, self.per, self.m4, self.kb0 = layer, halves, per, m4, first_kb

            def each(self, i, j0, n):
                nh = len(self.halves)
                for j in range(j0, j0 + n):
                    kb = self.kb0 + i * (self.per // nh) + j // nh
                    first = isinstance(kb, int) and kb == 0
                    yield j % RING, self.m4 + i * (self.per // RING) + j // RING, kb, j % nh, self.halves[j % nh], first

        def sp_slabs(e, sl, i, j0, n):
            for slot, m4, kb, _, h, _ in sl.each(i, j0, n):
                e.wait_ge(slabs_used, 4 * m4 + slot + 1)
                e.dma_start(slab[:, slot, :], a["mod_w"][sl.layer, ds(kb * P, P), ds(h * SLAB, SLAB)]
                            ).then_inc(slab_landed[slot], 16)

        def sp_iter(e, T, w, row, col, i, sl):
            for n in range(8):
                e.wait_ge(split_ready, 8 * T + n - 3)
                src = w[ds(row + (n % 4) * UNIT_KB * P, UNIT_KB * P), ds(col + (n // 4) * UNIT_COLS, UNIT_COLS)]
                e.dma_start(raw[:, n % RING], src.rearrange("(k p) n -> p k n", p=P)
                            ).then_inc(unit_landed[n % RING], 16)
                if sl and n >= 4:
                    r = sl.per // 4
                    sp_slabs(e, sl, i, (n - 4) * r, r)

        def sp_call(e, T, n, w, row, col, sl):
            with e.Fori(0, n) as i:
                sp_iter(e, T + i, w, row, col + i * 512, i, sl)

        def pe_iter(e, T, tile, ready, ctx_tile=None):
            for n in range(8):
                g = n // 4
                e.wait_ge(split_ready, 8 * T + n + 1)
                if ready:
                    e.wait_ge(*ready(n % 4))
                if n % 4 == 0:
                    e.wait_ge(psum_free, 2 * T + g - 1)
                for kk in range(UNIT_KB):
                    kb = (n % 4) * UNIT_KB + kk
                    for fb in range(2):
                        cols = slice(fb * P, (fb + 1) * P)
                        for t, bank in ((tile, 2 * g + fb), (ctx_tile, 4 + 2 * g + fb)):
                            if t is None:
                                continue
                            e.matmul(ps[:, bank, :], w_hi[:, n % RING, kk, cols], t[:, kb, :],
                                     start=(kb == 0), stop=False)
                            mm = e.matmul(ps[:, bank, 0:TOK], w_lo[:, n % RING, kk, cols], t[:, kb, 0:TOK],
                                          start=False, stop=(kb == KB - 1))
                mm.then_inc(units_done, 1)

        def pe_finish(e, sl_count, fin, n_acc):
            e.wait_ge(slabs_used, 4 * sl_count + 4)
            e.wait_ge(mod_ready, fin + 1)
            for h in range(n_acc):
                for b in range(half):
                    mm = e.matmul(ps[:, 7, h * half + b:h * half + b + 1], acc[:, h, b * P:(b + 1) * P], ones[:, 0:1],
                                  start=True, stop=True)
            mm.then_inc(mod_cols, 1)

        def act_split(e, T, n):
            e.wait_ge(unit_landed[n % RING], 16 * (2 * T + n // 4 - 1))
            e.wait_ge(units_done, 8 * T + n - 3)
            e.activation(w_hi[:, n % RING], raw[:, n % RING], ACT.Copy).then_inc(hi_ready, 1)

        def dve_split(e, T, n):
            e.wait_ge(hi_ready, 8 * T + n + 1)
            e.tensor_tensor(w_lo[:, n % RING], raw[:, n % RING], w_hi[:, n % RING].bitcast(F32),
                            ALU.subtract).then_inc(split_ready, 1)

        def dve_slabs(e, sl, i, j0, n):
            for slot, m4, kb, ac, _, first in sl.each(i, j0, n):
                e.wait_ge(slab_landed[slot], 16 * (m4 + 1))
                scale = silu[:, ds(kb, 1)]
                if first:
                    e.tensor_scalar(acc[:, ac], slab[:, slot], scale, None, ALU.mult).then_inc(slabs_used, 1)
                else:
                    e.wait_ge(slabs_used, 4 * m4 + slot + 5 - len(sl.halves))
                    e.scalar_tensor_tensor(acc[:, ac], slab[:, slot], scale, acc[:, ac],
                                           ALU.mult, ALU.add).then_inc(slabs_used, 1)

        def dve_finish(e, fin, dests):
            e.wait_ge(mod_cols, fin + 1)
            for h, at in enumerate(dests):
                ins = e.tensor_tensor(mod[:, ds(at, half)], ps[:, 7, h * half:(h + 1) * half],
                                      vec("mod_b", at, half), ALU.add)
            ins.then_inc(mod_ready, 1)
            e.wait_ge(mod_ready, fin + 2)

        class Readout:

            def bank(self, g, part):
                return ps[:, 2 * g:2 * g + 2, part * TOK:(part + 1) * TOK]

            def act_wait(self, e, T, g):
                e.wait_ge(units_done, 8 * T + 4 * g + 4)
                e.wait_ge(psum_free, 2 * T + g - 1)

            def act_head(self, e, T, g):
                self.act_wait(e, T, g)
                e.activation(lo_sum[:, g], self.bank(g, 1), ACT.Copy).then_inc(lo_copied, 1)

            def act_tail(self, e, T, g):
                pass

            def dve_tail(self, e, T, g):
                pass

        class Queries(Readout):
            def __init__(self, i):
                self.i = i

            def act_head(self, e, T, g):
                self.act_wait(e, T, g)
                e.activation(lo_sum[:, g], self.bank(g, 1), ACT.Copy, scale=QSCALE).then_inc(lo_copied, 1)

            def dve_head(self, e, T, g):
                e.wait_ge(lo_copied, 2 * T + g + 1)
                e.scalar_tensor_tensor(q[:, ds(4 * self.i + 2 * g, 2), :], self.bank(g, 0), QSCALE, lo_sum[:, g],
                                       ALU.mult, ALU.add).then_inc(psum_free, 1)

        class KeysValues(Readout):
            def __init__(self, dst):
                self.dst = dst

            def ctx_bank(self, g, part):
                return ps[:, 4 + 2 * g:6 + 2 * g, part * TOK:(part + 1) * TOK]

            def act_head(self, e, T, g):
                self.act_wait(e, T, g)
                e.activation(lo_sum[:, g], self.bank(g, 1), ACT.Copy)
                e.activation(sum_sb[:, g], self.ctx_bank(g, 1), ACT.Copy).then_inc(lo_copied, 1)

            def dve_head(self, e, T, g):
                e.wait_ge(lo_copied, 2 * T + g + 1)
                d = self.dst[:, 2 * g:2 * g + 2, :]
                e.tensor_tensor(d[:, :, 0:TOK], self.bank(g, 0), lo_sum[:, g], ALU.add)
                e.tensor_tensor(d[:, :, TOK:2 * TOK], self.ctx_bank(g, 0), sum_sb[:, g],
                                ALU.add).then_inc(psum_free, 1)

        class Gated(Readout):

            def __init__(self, gate, i, n_out, bias=None):
                self.gate, self.i, self.n_out, self.bias = gate, i, n_out, bias
                self.ready = {G1: FIN_Q, G2: FIN_MLP0, G3: FIN_HY - 1, G4: FIN_HOUT}[gate] + 2

            def act_head(self, e, T, g):
                self.act_wait(e, T, g)
                e.wait_ge(mod_ready, self.ready)
                for fb in range(2):
                    f = 4 * self.i + 2 * g + fb
                    bias = gate_bias[:, ds(f, 1)] if self.bias else 0.0
                    ins = e.activation(lo_sum[:, g, fb], ps[:, 2 * g + fb, TOK:2 * TOK], ACT.Identity,
                                       bias=bias, scale=mod[:, ds(self.gate + f, 1)])
                ins.then_inc(lo_copied, 1)

            def dve_head(self, e, T, g):
                e.wait_ge(lo_copied, 2 * T + g + 1)
                for fb in range(2):
                    f = 4 * self.i + 2 * g + fb
                    xf = x[:, ds(f, 1), :]
                    ins = e.scalar_tensor_tensor(xf, ps[:, 2 * g + fb:2 * g + fb + 1, 0:TOK],
                                                 mod[:, ds(self.gate + f, 1)], xf, ALU.mult, ALU.add)
                ins.then_inc(x_hi_added, 1)
                e.wait_ge(x_hi_added, self.n_out + 2 * self.i + g + 1)
                xg = x[:, ds(4 * self.i + 2 * g, 2), :]
                e.tensor_tensor(xg, xg, lo_sum[:, g], ALU.add).then_inc(psum_free, 1)

        class Hidden(Readout):

            def __init__(self, i, n_hid):
                self.i, self.n = i, n_hid

            def dve_head(self, e, T, g):
                e.wait_ge(lo_copied, 2 * T + g + 1)
                e.tensor_tensor(sum_sb[:, g], self.bank(g, 0), lo_sum[:, g], ALU.add).then_inc(psum_free, 1)
                e.wait_ge(psum_free, 2 * T + g + 1)
                e.scalar_tensor_tensor(sum_sb[:, g], sum_sb[:, g], 0.0, sum_sb[:, g],
                                       ALU.max, ALU.mult).then_inc(squared, 1)

            def act_tail(self, e, T, g):
                e.wait_ge(squared, self.n + 2 * self.i + g + 1)
                e.activation(alt[:, ds(4 * self.i + 2 * g, 2), 0:TOK], sum_sb[:, g], ACT.Copy).then_inc(hidden_hi, 1)

            def dve_tail(self, e, T, g):
                e.wait_ge(hidden_hi, self.n + 2 * self.i + g + 1)
                f = ds(4 * self.i + 2 * g, 2)
                e.tensor_tensor(alt[:, f, TOK:2 * TOK], sum_sb[:, g], alt[:, f, 0:TOK].bitcast(F32),
                                ALU.subtract).then_inc(hidden_ready, 1)

        class ShortConv(Readout):

            def __init__(self, part, col, n):
                self.part, self.col, self.n = part, col, n

            def act_head(self, e, T, g):
                self.act_wait(e, T, g)
                for fb in range(2):
                    ins = e.activation(lo_sum[:, g, fb], ps[:, 2 * g + fb, TOK:2 * TOK], ACT.Identity,
                                       bias=vec("b_in", self.col + 2 * g + fb))
                ins.then_inc(lo_copied, 1)

            def dve_head(self, e, T, g):
                e.wait_ge(lo_copied, 2 * T + g + 1)
                e.tensor_tensor(sum_sb[:, g], self.bank(g, 0), lo_sum[:, g], ALU.add).then_inc(psum_free, 1)

            def act_tail(self, e, T, g):
                e.wait_ge(psum_free, 2 * T + g + 1)
                for fb in range(2):
                    f = self.col + 2 * g + fb
                    ins = e.activation(u[:, self.part, 2 * g + fb], sum_sb[:, g, fb], ACT.Identity,
                                       bias=vec("conv_b", f), scale=vec("conv_w", 3 * KB + f))
                ins.then_inc(centred, 1)

            def dve_tail(self, e, T, g):
                e.wait_ge(centred, self.n + g + 1)
                for side in range(2):
                    for fb in range(2):
                        o = u[:, self.part, 2 * g + fb]
                        to = o[:, 1:TOK] if side == 0 else o[:, 0:TOK - 1]
                        fr = sum_sb[:, g, fb, 0:TOK - 1] if side == 0 else sum_sb[:, g, fb, 1:TOK]
                        ins = e.scalar_tensor_tensor(to, fr, vec("conv_w", 6 * KB * side + self.col + 2 * g + fb), to,
                                                     ALU.mult, ALU.add)
                    ins.then_inc(tapped, 1)
                    e.wait_ge(tapped, 2 * (self.n + g) + side + 1)

        def act_iter(e, T, prev, cur):
            for n in range(8):
                act_split(e, T, n)
                if n == 0 and prev:
                    prev.act_tail(e, T - 1, 0)
                if n == 3 and prev:
                    prev.act_head(e, T - 1, 1)
                if n == 4 and prev:
                    prev.act_tail(e, T - 1, 1)
                if n == 7:
                    cur.act_head(e, T, 0)

        def act_flush(e, T, r):
            r.act_tail(e, T, 0)
            r.act_head(e, T, 1)
            r.act_tail(e, T, 1)

        def dve_iter(e, T, prev, cur, i, sl, finish=None):
            for n in range(8):
                dve_split(e, T, n)
                if n == 0 and prev:
                    prev.dve_tail(e, T - 1, 0)
                if n == 3:
                    if finish:
                        dve_finish(e, *finish)
                    if prev:
                        prev.dve_head(e, T - 1, 1)
                if n == 4 and prev:
                    prev.dve_tail(e, T - 1, 1)
                if n >= 4 and sl:
                    r = sl.per // 4
                    dve_slabs(e, sl, i, (n - 4) * r, r)
                if n == 7:
                    cur.dve_head(e, T, 0)

        def dve_flush(e, T, r):
            r.dve_tail(e, T, 0)
            r.dve_head(e, T, 1)
            r.dve_tail(e, T, 1)

        def act_call(e, T, n, prev, kind):
            act_iter(e, T, prev, kind(0))
            with e.Fori(1, n) as i:
                act_iter(e, T + i, kind(i - 1), kind(i))
            return kind(n - 1)

        def dve_call(e, T, n, prev, kind, sl, finish=None):
            dve_iter(e, T, prev, kind(0), 0, sl, finish)
            with e.Fori(1, n) as i:
                dve_iter(e, T + i, kind(i - 1), kind(i), i, sl)
            return kind(n - 1)

        def act_stats(e, k, src, *waits):
            for w in waits:
                e.wait_ge(*w)
            for c in range(4):
                if 4 * k + c >= 2:
                    e.wait_ge(square_sums, 4 * k + c - 1)
                e.activation(sq[:, c % 2], src[:, 4 * c:4 * c + 4, :], ACT.Square).then_inc(squares, 1)

        def pe_stats(e, k):
            for c in range(4):
                e.wait_ge(squares, 4 * k + c + 1)
                for kk in range(4):
                    for tb in range(2):
                        mm = e.matmul(ps[:, 6, tb:tb + 1], sq[:, c % 2, kk, tb * P:(tb + 1) * P], ones[:, 0:1],
                                      start=(c == 0 and kk == 0 and tb == 0), stop=(c == 3 and kk == 3 and tb == 1),
                                      skip_group_check=True)
                mm.then_inc(square_sums, 1)

        def dve_rsqrt(e, r, sums, n, scale, eps, out, *waits):
            for w in waits:
                e.wait_ge(*w)
            A, R, Y, Tm = rs_a[:, 0:n], rs_r[:, 0:n], rs_y[:, 0:n], rs_t[:, 0:n]
            e.tensor_scalar(A, sums, scale, eps, ALU.mult, ALU.add).then_inc(rs_v, 1)
            e.wait_ge(rs_v, 6 * r + 1)
            e.reciprocal(R, A).then_inc(rs_v, 1)
            e.wait_ge(rs_root, r + 1)
            e.tensor_tensor(Tm, Y, Y, ALU.mult).then_inc(rs_v, 1)
            e.wait_ge(rs_v, 6 * r + 3)
            e.tensor_tensor(Tm, Tm, A, ALU.mult).then_inc(rs_v, 1)
            e.wait_ge(rs_v, 6 * r + 4)
            e.tensor_scalar(Tm, Tm, -0.5, 1.5, ALU.mult, ALU.add).then_inc(rs_v, 1)
            e.wait_ge(rs_v, 6 * r + 5)
            e.tensor_tensor(out, Y, Tm, ALU.mult).then_inc(rs_v, 1)

        def act_root(e, r, n):
            e.wait_ge(rs_v, 6 * r + 2)
            e.activation(rs_y[:, 0:n], rs_r[:, 0:n], ACT.Sqrt).then_inc(rs_root, 1)

        def pe_spread(e, k, r, rs):
            e.wait_ge(rs_v, 6 * r + 6)
            if k:
                e.wait_ge(normed, 8 * k)
            for tb in range(2):
                mm = e.matmul(ps[:, 5, tb * P:(tb + 1) * P], rs[:, tb:tb + 1].to_broadcast([P, P]), ident,
                              start=True, stop=True)
            mm.then_inc(rs_spread, 1)

        def dve_normalise(e, k, src, gains_ap, shift_ap, c):
            if c == 0:
                e.wait_ge(rs_spread, k + 1)
            h = hm[:, c % 2]
            e.tensor_tensor(h, src[:, 4 * c:4 * c + 4, :], ps[:, 5:6, 0:TOK].to_broadcast([P, 4, TOK]),
                            ALU.mult).then_inc(normed, 1)
            e.wait_ge(normed, 8 * k + 2 * c + 1)
            for kk in range(4):
                kb = 4 * c + kk
                if shift_ap is None:
                    ins = e.tensor_scalar(h[:, kk], h[:, kk], gains_ap[:, kb:kb + 1], None, ALU.mult)
                else:
                    ins = e.tensor_scalar(h[:, kk], h[:, kk], gains_ap[:, kb:kb + 1], shift_ap[:, kb:kb + 1],
                                          ALU.mult, ALU.add)
            ins.then_inc(normed, 1)

        def dve_norm_lo(e, k, dst, c):
            e.wait_ge(norm_hi, 4 * k + c + 1)
            e.tensor_tensor(dst[:, 4 * c:4 * c + 4, TOK:2 * TOK], hm[:, c % 2],
                            dst[:, 4 * c:4 * c + 4, 0:TOK].bitcast(F32), ALU.subtract).then_inc(norm_ready, 1)

        def dve_norm(e, k, src, gains_ap, shift_ap, dst):
            for c in range(4):
                if c >= 2:
                    e.wait_ge(norm_ready, 4 * k + c - 1)
                dve_normalise(e, k, src, gains_ap, shift_ap, c)
                if c:
                    dve_norm_lo(e, k, dst, c - 1)
            dve_norm_lo(e, k, dst, 3)

        def act_norm(e, k, dst):
            for c in range(4):
                e.wait_ge(normed, 8 * k + 2 * c + 2)
                e.activation(dst[:, 4 * c:4 * c + 4, 0:TOK], hm[:, c % 2], ACT.Copy).then_inc(norm_hi, 1)

        def dve_gain(e, n, dst, scale_cols, g):
            e.scalar_tensor_tensor(dst, scale_cols, 1.0, g, ALU.add, ALU.mult).then_inc(gains, 1)
            e.wait_ge(gains, n)

        def mods(layer, s_):
            return mod[:, (layer * N_MOD + s_) * KB:(layer * N_MOD + s_ + 1) * KB]

        SL_Q = Slabs(0, [4, 5], 8, M_Q)
        SL_KV = Slabs(0, [6], 8, M_KV)
        SL_ATT = [Slabs(0, [8, 9], 4, M_ATT + n, 2 * n) for n in range(8)]
        SL_OUT = Slabs(0, [7, 10], 8, M_OUT)
        SL_UP0 = Slabs(0, [11], 4, M_MLP0)

        def sl_mlp0(q_, down):
            return Slabs(1, [2 * q_ - 1 + down], 4, M_MLP0 + 8 * q_ + 4 * down)

        def sl_hy(c):
            return Slabs(1, [7 + c], 4, M_HY + 4 * c)

        SL_HOUT = Slabs(1, [11], 4, M_HOUT)
        HB = SLAB // P

        def mod_col(layer, half_):
            return layer * N_MOD * KB + half_ * HB

        G1, G2, G3, G4 = (2 * KB, 5 * KB, 8 * KB, 11 * KB)
        OUT_0, OUT_M0, OUT_H, OUT_M1 = 0, 8, 40, 48
        w_ff = D_FF // D

        block = stack.enter_context(nc.Block())

        @block.sync
        def _(e):
            e.dma_start(vecs[:], a["vecs"]).then_inc(in_vecs, 16)
            e.dma_start(x[:], a["x"]).then_inc(in_x, 16)
            e.dma_start(f_w[:, :], a["f_w"]).then_inc(in_fw, 16)
            e.dma_start(feats[:], a["feats"]).then_inc(in_feats, 16)
            e.dma_start(const[:], a["const"]).then_inc(in_const, 16)
            e.dma_start(fwd0[:], a["fwd"]).then_inc(in_fwd0, 16)
            e.dma_start(xc[:], a["ctx"]).then_inc(in_ctx, 16)
            e.wait_ge(started, 1)
            with e.Fori(0, 2) as cc:
                for par in range(2):
                    c = 2 * cc + par
                    e.wait_ge(taps_mm, 2 * c + 2)
                    e.dma_start(w3[:, par], a["w3"][:, :, ds(512 * c, 512)]).then_inc(in_w3[par], 16)
                    e.wait_ge(taps_ready, 2 * c + 2)
                    e.dma_start(decay[:, par], a["decay"][ds(c, 1)].rearrange("a p t n -> (a p) t n")).then_inc(in_decay[par], 16)
                    sp_slabs(e, Slabs(0, [c], 16, M_START + 4 * c), 0, 0, 16)
                    for o in range(2):
                        e.wait_ge(spec_copied, 2 * c + o + 2)
                        e.dma_start(spec_dram[ds(2 * c + o, 1)].rearrange("a p f c -> (a p) f c"), spec[:]
                                    ).then_inc(spec_stored, 16)
            sp_call(e, T_Q, 4, a["attn_w_in"], 0, 0, SL_Q)
            e.wait_ge(norm_ready, 8)
            e.dma_start(rope[:], a["rope"]).then_inc(in_rope, 16)
            sp_call(e, T_KV, 2, a["attn_w_in"], 0, KV_COL, SL_KV)
            for n in range(8):
                sp_slabs(e, SL_ATT[n], 0, 0, 4)
            sp_call(e, T_OUT, 4, a["attn_w_out"], 0, 0, SL_OUT)

            def mlp(layer, T, q_, sl_up, sl_down):
                sp_call(e, T, 4, a[f"mlp_w1_{layer}"], 0, q_ * D, sl_up)
                sp_call(e, T + 4, 4, a[f"mlp_w2_{layer}"], q_ * D, 0, sl_down)

            mlp(0, T_MLP0, 0, SL_UP0, sl_mlp0(0, 1))
            with e.Fori(1, w_ff) as q_:
                mlp(0, T_MLP0 + 8 * q_, q_, sl_mlp0(q_, 0), sl_mlp0(q_, 1))
            e.wait_ge(head_ready, 2 + HEADS)
            e.dma_start(fwd[:], a["fwd"]).then_inc(in_fwd, 16)
            e.dma_start(back[:], a["back"]).then_inc(in_back, 16)
            e.wait_ge(spec_stored, 9 * 16)
            with e.Fori(0, 4) as c:
                for k, part in enumerate((2, 0, 1)):
                    sp_iter(e, T_HY + 3 * c + k, a["hy_w_in"], 0, (c + part * 4) * 512, k, sl_hy(c))
                sp_slabs(e, sl_hy(c), 3, 0, 4)
                for o in range(2):
                    e.wait_ge(spec_v, 6 * (2 * c + o) + 6)
                    e.dma_start(h_spec[:], spec_dram[ds(2 * c + o, 1)].rearrange("a p f c -> (a p) f c")
                                ).then_inc(h_landed, 16)
            sp_call(e, T_HOUT, 4, a["hy_w_out"], 0, 0, SL_HOUT)
            mlp(1, T_MLP1, 0, None, None)
            with e.Fori(1, w_ff) as q_:
                mlp(1, T_MLP1 + 8 * q_, q_, None, None)
            for c in range(4):
                e.wait_ge(normed, 8 * 5 + 2 * c + 2)
                e.dma_start(a["y"][:, 4 * c:4 * c + 4, :], hm[:, c % 2]).then_inc(stored, 16)
                if c == 1:
                    e.wait_ge(stored, 2 * 16)
                    e.sem_inc(out_v, 1)
            e.wait_ge(stored, 4 * 16)

        @block.tensor
        def _(e):
            e.sem_inc(units_done, 8)
            e.sem_inc(taps_mm, 4)
            e.sem_inc(scores, 1)
            e.wait_ge(started, 1)
            e.wait_ge(in_fw, 16)
            e.wait_ge(in_feats, 16)
            e.matmul(ps[0:HID, 0, 0:TOK], f_w[0:FILTER_EMB, 0:HID], feats[:], start=True, stop=True).then_inc(hid_mm, 1)
            pe_stats(e, 0)
            e.wait_ge(hid_sin, 1)
            e.matmul(ps[0:HID, 1, 0:TOK], f_w[:, HID:2 * HID], hid_1[:], start=True, stop=True).then_inc(hid_mm, 1)
            e.wait_ge(rs_v, 1)
            pe_stats(e, 1)
            e.wait_ge(hid_sin, 2)
            e.wait_ge(in_fwd0, 16)
            with e.Fori(0, 2) as cc:
                for par in range(2):
                    c = 2 * cc + par
                    e.wait_ge(in_w3[par], 16 * (cc + 1))
                    for o in range(2):
                        e.wait_ge(taps_ready, 2 * c + o + 4)
                        for tb in range(2):
                            mm = e.matmul(ps[:, tb, :], hid_2[:, tb * P:(tb + 1) * P], w3[:, par, o, :],
                                          start=True, stop=True)
                        mm.then_inc(taps_mm, 1)
                        e.wait_ge(taps_ready, 2 * c + o + 5)
                        e.wait_ge(spec_copied, 2 * c + o + 1)
                        for f in range(4):
                            for kb in range(2):
                                mm = e.matmul(ps[:, 2 + f, :], fwd0[:, kb, f * P:(f + 1) * P], taps[:, o, kb, :],
                                              start=(kb == 0), stop=(kb == 1))
                        mm.then_inc(spec_mm, 1)
                        e.wait_ge(taps_squared, 2 * c + o + 1)
                        for b in range(4):
                            for tb in range(2):
                                mm = e.matmul(ps[:, 6, ds(o * KB + 4 * c + b, 1)], taps_sq[:, tb, b * P:(b + 1) * P],
                                              ones[:, 0:1], start=(tb == 0), stop=(tb == 1))
                        mm.then_inc(taps_summed, 1)
                    e.wait_ge(slabs_used, 16 * c + 16 + 4)
                    e.wait_ge(mod_ready, c + 1)
                    for h in range(2):
                        for b in range(half):
                            mm = e.matmul(ps[:, 7, h * half + b:h * half + b + 1], acc[:, h, b * P:(b + 1) * P],
                                          ones[:, 0:1], start=True, stop=True)
                    mm.then_inc(mod_cols, 1)
            e.wait_ge(in_const, 16)
            e.wait_ge(spec_copied, 9)
            pe_spread(e, 0, 0, rs_lat)
            pe_spread(e, 1, 1, rs_ctx)
            with e.Fori(0, 4) as i:
                pe_iter(e, T_Q + i, lat, lambda j: (norm_ready, 1 + j))
            pe_finish(e, M_KV, FIN_Q, 2)
            with e.Fori(0, 2) as i:
                pe_iter(e, T_KV + i, lat, lambda j: (norm_ready, 5 + j), alt)
            e.wait_ge(psum_free, 2 * (T_KV + 2))
            pe_finish(e, M_ATT, FIN_KV, 1)
            for h in range(KV_HEADS):
                for tb in range(4):
                    mm = e.transpose(ps[:, h, tb * P:(tb + 1) * P], vt[:, h, tb * P:(tb + 1) * P], ident)
                mm.then_inc(vt_turned, 1)
            for pr in range(2):
                e.wait_ge(tables, 5)
                for h in range(2):
                    mm = e.matmul(ps[:, 4 + pr, h * TOK:(h + 1) * TOK], swap_k[:] if pr else swap,
                                  kt[:, 2 * pr + h, 0:TOK], start=True, stop=True)
                mm.then_inc(k_swapped, 1)
            for h in range(2):
                for c in range(4):
                    e.wait_ge(k_squared, h + 1)
                    tb = (h * 4 + c) % 8
                    mm = e.matmul(ps[:, 6, tb:tb + 1], k_sq[:, 2 * h + c // 2, (c % 2) * P:(c % 2 + 1) * P],
                                  ones[:, 0:1], start=True, stop=True)
            mm.then_inc(kq_sums, 1)
            for hp in range(4):
                e.wait_ge(k_squared, 3 + hp)
                if hp == 0:
                    e.wait_ge(rs_v, 6 * 3 + 1)
                for h in range(2):
                    for tb in range(2):
                        col = (2 * hp + h) * 2 + tb
                        mm = e.matmul(ps[:, 6, 16 + col:17 + col], k_sq[:, 2 * (hp % 2) + h, tb * P:(tb + 1) * P],
                                      ones[:, 0:1], start=True, stop=True)
                mm.then_inc(kq_sums, 1)
            e.wait_ge(rs_v, 6 * 3 + 6)
            e.wait_ge(v_ready, 4)
            for h in range(2):
                for c in range(4):
                    mm = e.matmul(ps[:, h, c * P:(c + 1) * P], rs_k[:, 4 * h + c:4 * h + c + 1].to_broadcast([P, P]),
                                  ident, start=True, stop=True)
            mm.then_inc(k_spread, 1)
            e.wait_ge(k_v, 6)

            def pe_heads(kv, n, pair):
                e.wait_ge(q_v, 3 * n + 3)
                e.matmul(ps[:, 0, :], swap if kv < 2 else swap_q[:], q[:, ds(4 * kv + 2 * pair, 2), :],
                         start=True, stop=True).then_inc(q_swapped, 1)
                e.wait_ge(q_v, 3 * n + 6)

                def score(j):
                    e.wait_ge(exp_done, 4 * n + j + 1)
                    e.matmul(ps[:, 1 + j % 2, :], q_rot[:, j // 2, (j % 2) * P:(j % 2 + 1) * P], kt[:, kv, :],
                             start=True, stop=True).then_inc(scores, 1)

                def turn(j):
                    e.wait_ge(prob_v, 4 * n + j + 1)
                    e.wait_ge(probs_copied, 4 * n + j + 1)
                    for kc in range(4):
                        mm = e.transpose(ps[:, 3 + j % 2, kc * P:(kc + 1) * P], probs[:, j % 2, kc * P:(kc + 1) * P], ident)
                    mm.then_inc(probs_turned, 1)

                def values(h):
                    e.wait_ge(probs_copied, 4 * n + 2 * h + 2 + 2)
                    e.wait_ge(head_ready, 2 * n + h + 1)
                    for kc in range(4):
                        mm = e.matmul(ps[:, 5 + h, 0:TOK], v[:, kv, kc, :], probs_t[:, h, kc, :],
                                      start=(kc == 0), stop=(kc == 3))
                    mm.then_inc(head_out, 1)

                score(0)
                score(1)
                turn(0)
                score(2)
                turn(1)
                score(3)
                values(0)
                turn(2)
                turn(3)
                values(1)

            for kv in range(KV_HEADS):
                with e.Fori(0, 2) as pair:
                    pe_heads(kv, 2 * kv + pair, pair)
            pe_finish(e, M_OUT, FIN_ATT, 2)
            with e.Fori(0, 4) as i:
                pe_iter(e, T_OUT + i, alt, lambda j: (head_ready, 2 + HEADS))
            pe_finish(e, M_MLP0, FIN_OUT, 2)

            def mlp_q(layer, q_):
                T = (T_MLP0, T_MLP1)[layer] + 8 * q_
                h0 = 32 * layer + 8 * q_
                with e.Fori(0, 4) as i:
                    pe_iter(e, T + i, lat, lambda j: (norm_ready, (9, 17)[layer] + j))
                if layer == 0:
                    pe_finish(e, M_MLP0 + 8 * q_ + 4, FIN_MLP0 + 2 * q_, 1)
                with e.Fori(0, 4) as i:
                    pe_iter(e, T + 4 + i, alt, lambda j: (hidden_ready, h0 + 2 * j + 2))
                if layer == 0:
                    pe_finish(e, M_MLP0 + 8 * q_ + 8, FIN_MLP0 + 2 * q_ + 1, 1)

            pe_stats(e, 2)
            pe_spread(e, 2, 5, rs_lat)
            with e.Fori(0, w_ff) as q_:
                mlp_q(0, q_)
            pe_stats(e, 3)
            pe_spread(e, 3, 6, rs_lat)
            with e.Fori(0, 4) as c:
                for k in range(3):
                    pe_iter(e, T_HY + 3 * c + k, lat, lambda j: (norm_ready, 13 + j))
                for o in range(2):
                    s_ = 2 * c + o
                    if o == 0:
                        e.wait_ge(tapped, 4 * (3 * c + 3))
                    else:
                        e.wait_ge(conv_v, 6 * c + 3)
                    for tb in range(2):
                        for fb in range(4):
                            mm = e.transpose(ps[:, tb, fb * P:(fb + 1) * P], u[:, 0, fb, tb * P:(tb + 1) * P], ident)
                    mm.then_inc(turned, 1)
                    e.wait_ge(tok_ready, s_ + 1)
                    if o == 0:
                        e.wait_ge(in_fwd, 16)
                    for f in range(4):
                        for kb in range(2):
                            mm = e.matmul(ps[:, 2 + f, :], fwd[:, kb, f * P:(f + 1) * P], z_tok[:, kb, :],
                                          start=(kb == 0), stop=(kb == 1))
                    mm.then_inc(z_spec, 1)
                    e.wait_ge(spec_v, 6 * s_ + 6 + 6)
                    if o == 0:
                        e.wait_ge(in_back, 16)
                    for fb in range(4):
                        for f in range(4):
                            mm = e.matmul(ps[:, fb // 2, (fb % 2) * TOK:(fb % 2 + 1) * TOK],
                                          y_spec[:, f, fb * P:(fb + 1) * P], back[:, f, :],
                                          start=(f == 0), stop=(f == 3))
                    mm.then_inc(y_back, 1)
                pe_finish(e, M_HY + 4 * c + 4, FIN_HY + c, 1)
                e.wait_ge(conv_v, 6 * c + 6)
            with e.Fori(0, 4) as i:
                pe_iter(e, T_HOUT + i, alt, lambda j: (z_ready, 4))
            pe_finish(e, M_END, FIN_HOUT, 1)
            pe_stats(e, 4)
            pe_spread(e, 4, 7, rs_lat)
            with e.Fori(0, w_ff) as q_:
                mlp_q(1, q_)
            pe_stats(e, 5)
            pe_spread(e, 5, 8, rs_lat)

        @block.scalar
        def _(e):
            e.sem_inc(hi_ready, 8)
            e.sem_inc(lo_copied, 2)
            e.sem_inc(spec_copied, 1)
            e.sem_inc(exp_done, 2)
            e.sem_inc(probs_copied, 2)
            e.wait_ge(in_vecs, 16)
            e.activation(silu_e[:], vec("c", 0, 2 * KB), ACT.Exp, scale=-1.0).then_inc(silu_exp, 1)
            e.wait_ge(in_x, 16)
            act_stats(e, 0, x)
            e.wait_ge(hid_v, 7)
            e.activation(hid_1[:], hid_a[:], ACT.Sin).then_inc(hid_sin, 1)
            e.wait_ge(hid_v, 14)
            e.activation(hid_2[:], hid_a[:], ACT.Sin).then_inc(hid_sin, 1)
            act_root(e, 0, 2)
            e.wait_ge(in_ctx, 16)
            act_stats(e, 1, xc)
            act_root(e, 1, 2)
            with e.Fori(0, 4) as c:
                for o in range(2):
                    e.wait_ge(taps_ready, 2 * c + o + 5)
                    e.wait_ge(taps_summed, 2 * c + o + 1)
                    e.activation(taps_sq[:], taps[:, o], ACT.Square).then_inc(taps_squared, 1)
                    e.wait_ge(spec_mm, 2 * c + o + 1)
                    e.wait_ge(spec_stored, 16 * (2 * c + o + 1))
                    e.activation(spec[:, 0:2], ps[:, 2:4, :], ACT.Copy)
                    e.activation(spec[:, 2:4], ps[:, 4:6, :], ACT.Copy).then_inc(spec_copied, 1)
            act_root(e, 2, 32)
            e.wait_ge(spec_stored, 9 * 16)
            act_norm(e, 0, lat)
            act_norm(e, 1, alt)
            r = act_call(e, T_Q, 4, None, Queries)
            act_iter(e, T_KV, r, KeysValues(kt))
            act_iter(e, T_KV + 1, KeysValues(kt), KeysValues(vt))
            act_flush(e, T_KV + 1, KeysValues(vt))
            for h in range(2):
                e.wait_ge(psum_free, 2 * (T_KV + 2))
                e.activation(k_sq[:, 2 * h:2 * h + 2, :].rearrange("p a t -> p (a t)"), kt[:, 2 + h, :],
                             ACT.Square).then_inc(k_squared, 1)
            for hp in range(4):
                e.wait_ge(kq_sums, 1 if hp < 2 else hp)
                e.activation(k_sq[:, 2 * (hp % 2):2 * (hp % 2) + 2, :], q[:, A_HEADS + 2 * hp:A_HEADS + 2 * hp + 2, :],
                             ACT.Square).then_inc(k_squared, 1)
            for h in range(KV_HEADS):
                e.wait_ge(vt_turned, h + 1)
                e.activation(v[:, h].rearrange("p a d -> p (a d)"), ps[:, h, :], ACT.Copy).then_inc(v_ready, 1)
            act_root(e, 3, 8)
            act_root(e, 4, 16)

            def act_heads(kv, n, pair):
                def soft(j):
                    h = 4 * kv + 2 * pair + j // 2
                    e.wait_ge(row_max, 4 * n + j + 1)
                    e.wait_ge(probs_turned, 4 * n + j + 1)
                    m = sm[:, j % 2]
                    scale = 1.0 if kv < 2 else rs_q[:, ds(2 * (h - A_HEADS) + j % 2, 1)]
                    ins = e.activation(probs[:, j % 2, :], ps[:, 1 + j % 2, :], ACT.Exp, bias=m[:, 0:1], scale=scale,
                                       accum_out=m[:, 1:2])
                    if kv < 2:
                        ins = e.activation(m[:, 2:3], vec("sink", h), ACT.Exp, bias=m[:, 0:1])
                    ins.then_inc(exp_done, 1)

                def copy(j):
                    e.wait_ge(probs_turned, 4 * n + j + 1 + 2)
                    if j % 2 == 0:
                        e.wait_ge(head_out, 2 * n + j // 2 + 1)
                    e.activation(probs_t[:, j // 2, :, (j % 2) * P:(j % 2 + 1) * P],
                                 ps[:, 3 + j % 2, :].rearrange("p (k t) -> p k t", k=4), ACT.Copy).then_inc(probs_copied, 1)

                def head(h):
                    e.wait_ge(head_out, 2 * n + h + 1 + 2)
                    e.activation(alt[:, ds(4 * kv + 2 * pair + h, 1), 0:TOK], ps[:, 5 + h:6 + h, 0:TOK],
                                 ACT.Copy).then_inc(head_hi, 1)

                soft(0)
                soft(1)
                copy(0)
                soft(2)
                copy(1)
                soft(3)
                head(0)
                copy(2)
                copy(3)
                head(1)

            for kv in range(KV_HEADS):
                with e.Fori(0, 2) as pair:
                    act_heads(kv, 2 * kv + pair, pair)

            def mlp(layer, q_, prev):
                T = (T_MLP0, T_MLP1)[layer] + 8 * q_
                h0, n_out = 32 * layer + 8 * q_, (OUT_M0, OUT_M1)[layer] + 8 * q_
                r = act_call(e, T, 4, prev, lambda i: Hidden(i, h0))
                return act_call(e, T + 4, 4, r, lambda i: Gated((G2, G4)[layer], i, n_out))

            def mlps(layer):
                r = mlp(layer, 0, None)
                with e.Fori(1, w_ff) as q_:
                    mlp(layer, q_, Gated((G2, G4)[layer], 3, (OUT_M0, OUT_M1)[layer] + 8 * (q_ - 1)))
                T = (T_MLP0, T_MLP1)[layer]
                act_flush(e, T + 31, Gated((G2, G4)[layer], 3, (OUT_M0, OUT_M1)[layer] + 24))

            r = act_call(e, T_OUT, 4, None, lambda i: Gated(G1, i, OUT_0))
            act_flush(e, T_OUT + 3, r)
            act_stats(e, 2, x, (psum_free, 2 * T_MLP0))
            act_root(e, 5, 2)
            act_norm(e, 2, lat)
            mlps(0)
            act_stats(e, 3, x, (psum_free, 2 * T_HY))
            act_root(e, 6, 2)
            act_norm(e, 3, lat)
            with e.Fori(0, 4) as c:
                prev = None
                for k, part in enumerate((2, 0, 1)):
                    cur = ShortConv(k, part * KB + 4 * c, 6 * c + 2 * k)
                    act_iter(e, T_HY + 3 * c + k, prev, cur)
                    prev = cur
                act_flush(e, T_HY + 3 * c + 2, prev)
                for o in range(2):
                    s_ = 2 * c + o
                    e.wait_ge(turned, s_ + 1)
                    e.activation(z_tok[:], ps[:, 0:2, :], ACT.Copy).then_inc(tok_ready, 1)
                e.wait_ge(conv_v, 6 * c + 6)
                e.activation(alt[:, ds(4 * c, 4), 0:TOK], u[:, 0], ACT.Copy).then_inc(z_hi, 1)
            e.wait_ge(gains, 4)
            r = act_call(e, T_HOUT, 4, None, lambda i: Gated(G3, i, OUT_H, bias=True))
            act_flush(e, T_HOUT + 3, r)
            act_stats(e, 4, x, (psum_free, 2 * T_MLP1))
            act_root(e, 7, 2)
            act_norm(e, 4, lat)
            mlps(1)
            act_stats(e, 5, x, (psum_free, 2 * (T_MLP1 + 32)))
            act_root(e, 8, 2)

        @block.vector
        def _(e):
            e.sem_inc(split_ready, 8)
            e.sem_inc(psum_free, 2)
            e.sem_inc(slabs_used, 4)
            e.sem_inc(mod_ready, 1)
            e.sem_inc(taps_ready, 4)
            e.sem_inc(taps_summed, 1)
            e.sem_inc(spec_stored, 16)
            e.sem_inc(q_v, 3)
            e.sem_inc(probs_turned, 2)
            e.sem_inc(head_ready, 2)
            e.sem_inc(head_out, 2)
            e.sem_inc(spec_v, 6)
            e.memset(ones[:], 1.0).then_inc(started, 1)
            e.wait_ge(silu_exp, 1)
            e.tensor_scalar(silu_e[:], silu_e[:], 1.0, None, ALU.add).then_inc(silu_v, 1)
            e.wait_ge(silu_v, 1)
            e.reciprocal(silu[:], silu_e[:]).then_inc(silu_v, 1)
            e.wait_ge(silu_v, 2)
            e.tensor_tensor(silu[:], silu[:], vec("c", 0, 2 * KB), ALU.mult).then_inc(silu_v, 1)

            def hidden_arg(n, b, fr):
                e.wait_ge(hid_mm, n + 1)
                e.tensor_scalar(hid_a[:], ps[0:HID, n, 0:TOK], b, fr, ALU.add, ALU.mult).then_inc(hid_v, 1)
                e.wait_ge(hid_v, 7 * n + 1)
                e.tensor_scalar(hid_k[:], hid_a[:], 1.0 / (2.0 * math.pi), MAGIC, ALU.mult, ALU.add).then_inc(hid_v, 1)
                e.wait_ge(hid_v, 7 * n + 2)
                e.tensor_scalar(hid_k[:], hid_k[:], MAGIC, None, ALU.subtract).then_inc(hid_v, 1)
                parts = [6.28125, 0.0019340515136718750]
                parts.append(2.0 * math.pi - sum(parts))
                for m, part in enumerate(parts):
                    e.wait_ge(hid_v, 7 * n + 3 + m)
                    e.scalar_tensor_tensor(hid_a[:], hid_k[:], -part, hid_a[:], ALU.mult, ALU.add).then_inc(hid_v, 1)
                e.wait_ge(hid_v, 7 * n + 6)
                e.tensor_scalar(hid_a[:], hid_a[:], 3.1415925, -3.1415925, ALU.min, ALU.max).then_inc(hid_v, 1)

            e.wait_ge(in_fw, 16)
            b1, fr1, b2, fr2 = (f_w[:, 2 * HID + n:2 * HID + n + 1] for n in range(4))
            hidden_arg(0, b1, fr1)
            hidden_arg(1, b2, fr2)
            dve_rsqrt(e, 0, ps[:, 6, 0:2], 2, 1.0 / D, EPS, rs_lat[:], (square_sums, 4))
            dve_rsqrt(e, 1, ps[:, 6, 0:2], 2, 1.0 / D, EPS, rs_ctx[:], (square_sums, 8))
            with e.Fori(0, 2) as cc:
                for par in range(2):
                    c = 2 * cc + par
                    sl = Slabs(0, [c], 16, M_START + 4 * c)
                    for j in range(16):
                        if j in (1, 6):
                            o = j // 6
                            e.wait_ge(taps_mm, 2 * c + o + 5)
                            e.wait_ge(in_decay[par], 16 * (cc + 1))
                            e.tensor_tensor(taps[:, o], ps[:, 0:2, :], decay[:, par], ALU.mult).then_inc(taps_ready, 1)
                        e.wait_ge(slab_landed[j % RING], 16 * (4 * c + j // RING + 1))
                        s_ = slab[:, j % RING]
                        if j == 0:
                            e.tensor_scalar(acc[:, 0], s_, silu[:, 0:1], None, ALU.mult).then_inc(acc_ready, 1)
                            e.tensor_scalar(acc[:, 1], s_, silu[:, KB:KB + 1], None, ALU.mult).then_inc(slabs_used, 1)
                        else:
                            e.wait_ge(acc_ready, 16 * c + j)
                            e.scalar_tensor_tensor(acc[:, 0], s_, silu[:, j:j + 1], acc[:, 0],
                                                   ALU.mult, ALU.add).then_inc(acc_ready, 1)
                            e.wait_ge(slabs_used, 16 * c + j + 4)
                            e.scalar_tensor_tensor(acc[:, 1], s_, silu[:, KB + j:KB + j + 1], acc[:, 1],
                                                   ALU.mult, ALU.add).then_inc(slabs_used, 1)
                    e.wait_ge(mod_cols, c + 1)
                    e.tensor_tensor(mod_ctx[:, ds(half * c, half)], ps[:, 7, half:2 * half],
                                    vec("mod_b", half * c, half), ALU.add)
                    e.tensor_tensor(mod[:, ds(half * c, half)], ps[:, 7, 0:half],
                                    vec("mod_b", half * c, half), ALU.add).then_inc(mod_ready, 1)
            dve_rsqrt(e, 2, ps[:, 6, 0:32], 32, 1.0, EPS, rs_filter[:], (taps_summed, 9))
            e.wait_ge(mod_ready, 5)
            dve_gain(e, 1, gain[:, 0:KB], mods(0, 1), vec("mix_g", 0, KB))
            dve_norm(e, 0, x, gain[:, 0:KB], mods(0, 0), lat)
            dve_gain(e, 2, gain[:, KB:2 * KB], mod_ctx[:, KB:2 * KB], vec("mix_g", 0, KB))
            dve_norm(e, 1, xc, gain[:, KB:2 * KB], mod_ctx[:, 0:KB], alt)
            r = dve_call(e, T_Q, 4, None, Queries, SL_Q)
            dve_iter(e, T_KV, r, KeysValues(kt), 0, SL_KV, (FIN_Q, [mod_col(0, 4), mod_col(0, 5)]))
            dve_iter(e, T_KV + 1, KeysValues(kt), KeysValues(vt), 1, SL_KV)
            dve_flush(e, T_KV + 1, KeysValues(vt))
            e.wait_ge(in_rope, 16)
            e.wait_ge(in_const, 16)
            qn, kn = vec("q_norm"), vec("k_norm")
            e.tensor_scalar(cos_q[:], cos, qn, None, ALU.mult).then_inc(tables, 1)
            e.tensor_scalar(cos_k[:], cos, kn, None, ALU.mult).then_inc(tables, 1)
            e.tensor_scalar(swap_q[:], swap, qn, None, ALU.mult).then_inc(tables, 1)
            e.tensor_scalar(swap_k[:], swap, kn, None, ALU.mult).then_inc(tables, 1)
            e.tensor_scalar(neg_sink[:], vec("sink", 0, A_HEADS), -1.0, None, ALU.mult).then_inc(tables, 1)
            sin_b = sin.rearrange("p (a t) -> p a t", a=1).to_broadcast([P, 2, TOK])

            def rotate(dst, src, bank, table, done, n):
                tb_ = table.rearrange("p (a t) -> p a t", a=1).to_broadcast([P, 2, TOK])
                e.tensor_tensor(q_sin[:], ps[:, bank, :].rearrange("p (a t) -> p a t", a=2), sin_b, ALU.mult)
                e.tensor_tensor(dst, src, tb_, ALU.mult).then_inc(done, 1)
                e.wait_ge(done, n + 1)
                e.tensor_tensor(dst, dst, q_sin[:], ALU.add).then_inc(done, 1)
                e.wait_ge(done, n + 2)

            dve_finish(e, FIN_KV, [mod_col(0, 6)])
            e.wait_ge(k_swapped, 1)
            rotate(kt[:, 0:2, 0:TOK], kt[:, 0:2, 0:TOK], 4, cos, k_v, 0)
            dve_rsqrt(e, 3, ps[:, 6, 0:8], 8, 1.0 / HEAD, EPS, rs_k[:], (kq_sums, 1))
            e.wait_ge(k_swapped, 2)
            rotate(kt[:, 2:4, 0:TOK], kt[:, 2:4, 0:TOK], 5, cos_k[:], k_v, 2)
            dve_rsqrt(e, 4, ps[:, 6, 16:32], 16, 1.0 / HEAD, EPS * QSCALE * QSCALE, rs_q[:], (kq_sums, 5))
            e.wait_ge(rs_v, 6 * 4 + 6)
            e.tensor_scalar(rs_q[:], rs_q[:], QSCALE, None, ALU.mult).then_inc(k_v, 1)
            e.wait_ge(k_spread, 1)
            for h in range(2):
                kl, kc = kt[:, 2 + h, 0:TOK], kt[:, 2 + h, TOK:2 * TOK]
                e.tensor_tensor(kl, kl, ps[:, h, 0:TOK], ALU.mult)
                ins = e.scalar_tensor_tensor(kc, kc, kn, ps[:, h, TOK:2 * TOK], ALU.mult, ALU.mult)
            ins.then_inc(k_v, 1)
            e.wait_ge(k_v, 6)
            e.memset(acc[:], 0.0).then_inc(acc_ready, 1)
            e.wait_ge(acc_ready, 65)

            def dve_heads(kv, n, pair):
                e.wait_ge(q_swapped, n + 1)
                e.wait_ge(scores, 4 * n + 1)
                hq = q[:, ds(4 * kv + 2 * pair, 2), :]
                tb_ = (cos if kv < 2 else cos_q[:]).rearrange("p (a t) -> p a t", a=1).to_broadcast([P, 2, TOK])
                e.tensor_tensor(q_sin[:], ps[:, 0, :].rearrange("p (a t) -> p a t", a=2), sin_b, ALU.mult).then_inc(q_v, 1)
                e.tensor_tensor(q_rot[:], hq, tb_, ALU.mult).then_inc(q_v, 1)
                e.wait_ge(q_v, 3 * n + 5)
                e.tensor_tensor(q_rot[:], q_rot[:], q_sin[:], ALU.add).then_inc(q_v, 1)

                def peak(j):
                    h = 4 * kv + 2 * pair + j // 2
                    e.wait_ge(scores, 4 * n + j + 2)
                    m, s_ = sm[:, j % 2], ps[:, 1 + j % 2, :]
                    if kv < 2:
                        part = s_[:, (1 - j % 2) * P:(2 - j % 2) * P]
                        e.tensor_tensor(part, part, mask[:, j % 2, :], ALU.add).then_inc(scored_v, 1)
                        e.wait_ge(scored_v, 2 * (4 * n + j) + 1)
                    else:
                        e.sem_inc(scored_v, 1)
                    e.tensor_reduce(m[:, 3:4], s_, AX.X, ALU.max, negate=True).then_inc(scored_v, 1)
                    e.wait_ge(scored_v, 2 * (4 * n + j) + 2)
                    if kv < 2:
                        e.tensor_tensor(m[:, 0:1], m[:, 3:4], neg_sink[:, ds(h, 1)], ALU.min).then_inc(row_max, 1)
                    else:
                        e.tensor_tensor(m[:, 0:1], m[:, 3:4], rs_q[:, ds(2 * (h - A_HEADS) + j % 2, 1)],
                                        ALU.mult).then_inc(row_max, 1)

                def weigh(j):
                    m = sm[:, j % 2]
                    e.wait_ge(exp_done, 4 * n + j + 1 + 2)
                    if kv < 2:
                        e.tensor_tensor(m[:, 1:2], m[:, 1:2], m[:, 2:3], ALU.add).then_inc(scored_w, 1)
                        e.wait_ge(scored_w, 2 * (4 * n + j) + 1)
                    else:
                        e.sem_inc(scored_w, 1)
                    e.reciprocal(m[:, 3:4], m[:, 1:2]).then_inc(scored_w, 1)
                    e.wait_ge(scored_w, 2 * (4 * n + j) + 2)
                    e.tensor_scalar(probs[:, j % 2, :], probs[:, j % 2, :], m[:, 3:4], None, ALU.mult).then_inc(prob_v, 1)

                def head(h):
                    e.wait_ge(head_hi, 2 * n + h + 1)
                    at = ds(4 * kv + 2 * pair + h, 1)
                    e.tensor_tensor(alt[:, at, TOK:2 * TOK], ps[:, 5 + h:6 + h, 0:TOK], alt[:, at, 0:TOK].bitcast(F32),
                                    ALU.subtract).then_inc(head_ready, 1)

                def fold(j):
                    for slot, m4, kb, ac, _, _ in Slabs(0, [8, 9], 4, M_ATT + n, 2 * n).each(0, j, 1):
                        e.wait_ge(slab_landed[slot], 16 * (m4 + 1))
                        e.wait_ge(slabs_used, 4 * m4 + slot + 3)
                        e.scalar_tensor_tensor(acc[:, ac], slab[:, slot], silu[:, ds(kb, 1)], acc[:, ac],
                                               ALU.mult, ALU.add).then_inc(slabs_used, 1)

                peak(0)
                peak(1)
                weigh(0)
                fold(0)
                peak(2)
                weigh(1)
                fold(1)
                peak(3)
                weigh(2)
                fold(2)
                head(0)
                weigh(3)
                fold(3)
                head(1)

            for kv in range(KV_HEADS):
                with e.Fori(0, 2) as pair:
                    dve_heads(kv, 2 * kv + pair, pair)
            r = dve_call(e, T_OUT, 4, None, lambda i: Gated(G1, i, OUT_0), SL_OUT,
                         (FIN_ATT, [mod_col(0, 8), mod_col(0, 9)]))
            dve_flush(e, T_OUT + 3, r)
            dve_finish(e, FIN_OUT, [mod_col(0, 7), mod_col(0, 10)])
            dve_rsqrt(e, 5, ps[:, 6, 0:2], 2, 1.0 / D, EPS, rs_lat[:], (square_sums, 12))
            e.wait_ge(mod_ready, FIN_OUT + 2)
            dve_gain(e, 3, gain[:, 0:KB], mods(0, 4), vec("mlp_g", 0, KB))
            dve_norm(e, 2, x, gain[:, 0:KB], mods(0, 3), lat)

            def mlp(layer, q_, prev, sl_up, sl_down, fin_before, fin_mid):
                T = (T_MLP0, T_MLP1)[layer] + 8 * q_
                h0, n_out = 32 * layer + 8 * q_, (OUT_M0, OUT_M1)[layer] + 8 * q_
                r = dve_call(e, T, 4, prev, lambda i: Hidden(i, h0), sl_up, fin_before)
                return dve_call(e, T + 4, 4, r, lambda i: Gated((G2, G4)[layer], i, n_out), sl_down, fin_mid)

            mlp(0, 0, None, SL_UP0, sl_mlp0(0, 1), None, (FIN_MLP0, [mod_col(0, 11)]))
            with e.Fori(1, w_ff) as q_:
                mlp(0, q_, Gated(G2, 3, OUT_M0 + 8 * (q_ - 1)), sl_mlp0(q_, 0), sl_mlp0(q_, 1),
                    (FIN_MLP0 + 2 * q_ - 1, [mod_col(1, 2 * q_ - 2)]), (FIN_MLP0 + 2 * q_, [mod_col(1, 2 * q_ - 1)]))
            dve_flush(e, T_MLP0 + 31, Gated(G2, 3, OUT_M0 + 24))
            dve_finish(e, FIN_MLP0 + 7, [mod_col(1, 6)])
            dve_rsqrt(e, 6, ps[:, 6, 0:2], 2, 1.0 / D, EPS, rs_lat[:], (square_sums, 16))
            e.wait_ge(mod_ready, FIN_HY + 1)
            e.tensor_tensor(gate_bias[:], mods(1, 2), vec("b_out", 0, KB), ALU.mult)
            dve_gain(e, 4, gain[:, 0:KB], mods(1, 1), vec("mix_g", KB, KB))
            dve_norm(e, 3, x, gain[:, 0:KB], mods(1, 0), lat)
            with e.Fori(0, 4) as c:
                prev = None
                for k, part in enumerate((2, 0, 1)):
                    cur = ShortConv(k, part * KB + 4 * c, 6 * c + 2 * k)
                    dve_iter(e, T_HY + 3 * c + k, prev, cur, k, sl_hy(c))
                    prev = cur
                dve_flush(e, T_HY + 3 * c + 2, prev)
                dve_slabs(e, sl_hy(c), 3, 0, 4)
                z = u[:, 0]
                for o in range(2):
                    s_ = 2 * c + o
                    e.wait_ge(z_spec, s_ + 1)
                    e.wait_ge(h_landed, 16 * (s_ + 1))
                    zr, zi, hr, hi = ps[:, 2:4, :], ps[:, 4:6, :], h_spec[:, 0:2], h_spec[:, 2:4]
                    yr, yi, tmp = y_spec[:, 0:2], y_spec[:, 2:4], z_tok[:]
                    n0 = 6 * s_ + 6
                    e.tensor_tensor(yr, zr, hr, ALU.mult).then_inc(spec_v, 1)
                    e.tensor_tensor(tmp, zi, hi, ALU.mult).then_inc(spec_v, 1)
                    e.wait_ge(spec_v, n0 + 2)
                    e.tensor_tensor(yr, yr, tmp, ALU.subtract).then_inc(spec_v, 1)
                    e.tensor_tensor(yi, zr, hi, ALU.mult).then_inc(spec_v, 1)
                    e.wait_ge(spec_v, n0 + 4)
                    e.tensor_tensor(tmp, zi, hr, ALU.mult).then_inc(spec_v, 1)
                    e.wait_ge(spec_v, n0 + 5)
                    e.tensor_tensor(yi, yi, tmp, ALU.add).then_inc(spec_v, 1)
                    for fb in range(4):
                        ins = e.tensor_scalar(z[:, fb], z[:, fb], vec("skip", o * KB + 4 * c + fb), None, ALU.mult)
                    ins.then_inc(conv_v, 1)
                    e.wait_ge(conv_v, 6 * c + 3 * o + 1)
                    e.wait_ge(y_back, s_ + 1)
                    for fb in range(4):
                        ins = e.scalar_tensor_tensor(z[:, fb], ps[:, fb // 2, (fb % 2) * TOK:(fb % 2 + 1) * TOK],
                                                     rs_filter[:, ds(o * KB + 4 * c + fb, 1)], z[:, fb],
                                                     ALU.mult, ALU.add)
                    ins.then_inc(conv_v, 1)
                    e.wait_ge(conv_v, 6 * c + 3 * o + 2)
                    e.tensor_tensor(z, z, u[:, 1 + o], ALU.mult).then_inc(conv_v, 1)
                e.wait_ge(z_hi, c + 1)
                e.tensor_tensor(alt[:, ds(4 * c, 4), TOK:2 * TOK], z, alt[:, ds(4 * c, 4), 0:TOK].bitcast(F32),
                                ALU.subtract).then_inc(z_ready, 1)
                dve_finish(e, FIN_HY + c, [mod_col(1, 7 + c)])
            r = dve_call(e, T_HOUT, 4, None, lambda i: Gated(G3, i, OUT_H), SL_HOUT)
            dve_flush(e, T_HOUT + 3, r)
            dve_finish(e, FIN_HOUT, [mod_col(1, 11)])
            dve_rsqrt(e, 7, ps[:, 6, 0:2], 2, 1.0 / D, EPS, rs_lat[:], (square_sums, 20))
            e.wait_ge(mod_ready, FIN_HOUT + 2)
            dve_gain(e, 5, gain[:, 0:KB], mods(1, 4), vec("mlp_g", KB, KB))
            dve_norm(e, 4, x, gain[:, 0:KB], mods(1, 3), lat)
            mlp(1, 0, None, None, None, None, None)
            with e.Fori(1, w_ff) as q_:
                mlp(1, q_, Gated(G4, 3, OUT_M1 + 8 * (q_ - 1)), None, None, None, None)
            dve_flush(e, T_MLP1 + 31, Gated(G4, 3, OUT_M1 + 24))
            dve_rsqrt(e, 8, ps[:, 6, 0:2], 2, 1.0 / D, EPS, rs_lat[:], (square_sums, 24))
            for c in range(4):
                if c == 2:
                    e.wait_ge(out_v, 1)
                dve_normalise(e, 5, x, vec("final_g", 0, KB), None, c)


def columns(v):
    return v.reshape(-1, P).T


def kernel(**inputs):
    import concourse.bacc as bacc
    from concourse.bass_utils import run_bass_kernel_spmd

    i = {k: np.asarray(v_) for k, v_ in inputs.items()}
    arrays = constants()
    feature_major = lambda t: np.ascontiguousarray(t.T.reshape(KB, P, TOK).transpose(1, 0, 2))
    arrays["x"] = feature_major(i["x"][0])
    arrays["ctx"] = feature_major(i["ctx"][0])
    arrays["vecs"] = np.ascontiguousarray(np.concatenate([
        columns(i["c"]), columns(i["c_ctx"]), columns(i["mod_b"]), columns(i["norm_mix_g"]), columns(i["norm_mlp_g"]),
        columns(i["final_g"]), columns(i["hy_b_in"]), columns(i["hy_conv_w"]), columns(i["hy_conv_b"]),
        columns(i["hy_skip"]), columns(i["hy_b_out"]), columns(i["attn_q_norm"]), columns(i["attn_k_norm"]),
        np.broadcast_to(i["attn_sink"], (P, A_HEADS))], 1))
    f_w1 = np.zeros((HID, HID), np.float32)
    f_w1[:FILTER_EMB] = i["hy_f_w1"][0]
    arrays["f_w"] = np.ascontiguousarray(np.concatenate([
        f_w1, i["hy_f_w2"][0], i["hy_f_b1"].T, i["hy_f_freq1"].T, i["hy_f_b2"].T, i["hy_f_freq2"].T], 1))
    arrays["w3"] = i["hy_f_w3"][0].reshape(HID, 2, D)
    arrays["mod_w"] = i["mod_w"]
    for name in ("attn_w_in", "attn_w_out", "hy_w_in", "hy_w_out"):
        arrays[name] = i[name][0]
    for layer in range(2):
        arrays[f"mlp_w1_{layer}"] = i["mlp_w1"][layer]
        arrays[f"mlp_w2_{layer}"] = i["mlp_w2"][layer]
    nc = bacc.Bacc("TRN2", target_bir_lowering=False, num_devices=1)
    a = {k: nc.dram_tensor(f"in_{k}", v_.shape, F32, kind="ExternalInput").ap() for k, v_ in arrays.items()}
    a["y"] = nc.dram_tensor("out_y", (P, KB, TOK), F32, kind="ExternalOutput").ap()
    build(nc, a)
    r = run_bass_kernel_spmd(nc, [{f"in_{k}": v_ for k, v_ in arrays.items()}], core_ids=[0])
    y = r.results[0]["out_y"]
    return np.ascontiguousarray(y.transpose(1, 0, 2).reshape(D, TOK).T)[None]
```

```python
import math
from contextlib import ExitStack

import numpy as np

import concourse.bass as bass
from concourse import mybir

P = 128
D = 2048
TOK = 256
KB = D // P
D_FF = 4 * D
GRID_W = 64
HEAD = 128
THETA = 10000.0
WINDOW = 128
EPS = 1e-6
QSCALE = HEAD ** -0.5
HEADS = 16
A_HEADS = 8
KV_HEADS = 4
KV_COL = HEADS * HEAD
FILTER_EMB = 33
HID = 64
TARGET = 1e-2
MAX_DECAY = math.log(TARGET) / 0.3
MIN_DECAY = math.log(TARGET) / 1.5
NFREQ = 256
N_MOD = 6

UNIT_KB = 4
UNIT_COLS = 256
SLAB = 1024
RING = 4
PE_SLABS = (1, 4, 7, 10, 12, 14)
START_RING = 8
MAGIC = 1.5 * 2.0 ** 23

F32 = mybir.dt.float32
F32R = mybir.dt.float32r
ACT = mybir.ActivationFunctionType
ALU = mybir.AluOpType
AX = mybir.AxisListType
ds = bass.ds

VECS = {}
_at = 0
for _name, _n in (("c", KB), ("c_ctx", KB), ("mod_b", 2 * N_MOD * KB), ("mix_g", 2 * KB), ("mlp_g", 2 * KB),
                  ("final_g", KB), ("b_in", 3 * KB), ("conv_w", 9 * KB), ("conv_b", 3 * KB), ("skip", 2 * KB),
                  ("b_out", KB), ("q_norm", 1), ("k_norm", 1), ("sink", A_HEADS)):
    VECS[_name] = _at
    _at += _n
N_VECS = _at
IDENT, SWAP, N_CONST = 0, P, 2 * P
COS, SIN, MASK, N_ROPE = 0, TOK, 2 * TOK, 3 * TOK


def constants():
    f32 = np.float32
    ident = np.eye(P, dtype=f32)
    swap = np.zeros((P, P), f32)
    for m in range(P):
        swap[m ^ 32, m] = 1.0
    tok = np.arange(TOK)
    inv = THETA ** (-np.arange(0, HEAD // 2, 2, dtype=f32) / f32(HEAD // 2))
    ang = np.empty((P, TOK), f32)
    for m in range(P):
        pos = (tok // GRID_W if m < HEAD // 2 else tok % GRID_W).astype(f32)
        ang[m] = pos * f32(inv[m % 32])
    sign = np.where((np.arange(P) // 32) % 2 == 0, -1.0, 1.0)[:, None]
    q = np.arange(P)[:, None]
    k = np.arange(P)[None]
    mask = np.stack([np.where(k + P - q <= WINDOW, 0.0, -1e30), np.where(q + P - k <= WINDOW, 0.0, -1e30)], 1)
    const = np.concatenate([ident, swap], 1)
    rope = np.concatenate([np.cos(ang), np.sin(ang) * sign, mask.reshape(P, 2 * P)], 1)
    t = np.arange(TOK)[:, None]
    f = np.arange(NFREQ)[None] + 0.5
    th = np.pi * f * t / TOK
    fwd = np.concatenate([np.cos(th), -np.sin(th)], 1).reshape(2, P, 2 * NFREQ).transpose(1, 0, 2)
    n = np.arange(TOK)[None] + TOK // 2
    ph = np.pi * (np.arange(NFREQ)[:, None] + 0.5) * n / TOK
    back = np.concatenate([np.cos(ph), -np.sin(ph)], 0) / TOK
    back = back.reshape(4, P, TOK).transpose(1, 0, 2)
    bands = (FILTER_EMB - 1) // 2
    w = (2.0 * np.pi * np.arange(TOK) / TOK)[:, None]
    fb = np.linspace(1e-4, bands - 1, bands)[None]
    feats = np.concatenate([np.linspace(0.0, 1.0, TOK)[:, None], np.cos(fb * w), -np.sin(fb * w)], 1).T
    offs = np.abs(np.arange(TOK) - TOK // 2) * (2.0 / TOK)
    deltas = np.abs(np.linspace(MIN_DECAY, MAX_DECAY, D))
    decay = np.exp(-offs[:, None] * deltas[None]).reshape(2, P, 4, 512).transpose(2, 1, 0, 3)
    return {k: np.ascontiguousarray(v, dtype=f32) for k, v in
            (("const", const), ("rope", rope), ("fwd", fwd), ("back", back), ("feats", feats), ("decay", decay))}


def build(nc, a):
    stack = ExitStack()

    def sem(name):
        return stack.enter_context(nc.semaphore(name))

    def sb(name, shape, dt=F32, scope=None):
        return (scope or stack).enter_context(nc.sbuf_tensor(name, shape, dt))

    with stack:
        x = sb("x", [P, KB, TOK])
        vecs = sb("vecs", [P, N_VECS])
        const = sb("const", [P, N_CONST])
        mod = sb("mod", [P, 2 * N_MOD * KB])
        mod_ctx = sb("mod_ctx", [P, 2 * KB])
        silu = sb("silu", [P, 2 * KB])
        silu_e = sb("silu_e", [P, 2 * KB])
        gain = sb("gain", [P, 2 * KB])
        gate_bias = sb("gate_bias", [P, KB])
        ones = sb("ones", [P, P])
        mod_part = sb("mod_part", [P, 2, SLAB // P])
        neg_sink = sb("neg_sink", [P, A_HEADS])
        rs_a, rs_r = sb("rs_a", [P, 32]), sb("rs_r", [P, 32])
        rs_y, rs_t = sb("rs_y", [P, 32]), sb("rs_t", [P, 32])
        tap_sums = sb("tap_sums", [P, 2 * KB])
        rs_k, rs_q = sb("rs_k", [P, 8]), sb("rs_q", [P, 16])
        rs_filter = sb("rs_filter", [P, 32])
        raw = sb("raw", [P, RING, UNIT_KB, UNIT_COLS])
        w_hi = sb("w_hi", [P, RING, UNIT_KB, UNIT_COLS], F32R)
        w_lo = sb("w_lo", [P, RING, UNIT_KB, UNIT_COLS], F32R)
        slab = sb("slab", [P, RING, SLAB])
        acc = sb("acc", [P, 2, SLAB])
        lo_sum = sb("lo_sum", [P, 2, 2, TOK])
        sum_sb = sb("sum_sb", [P, 2, 2, TOK])
        with ExitStack() as early:
            s = early
            hid_a, hid_k, hid_1 = (sb(n, [HID, TOK], scope=s) for n in ("hid_a", "hid_k", "hid_1"))
            hid_2 = sb("hid_2", [HID, TOK], scope=s)
            f_w = sb("f_w", [HID, 2 * HID + 4], scope=s)
            feats = sb("feats", [FILTER_EMB, TOK], scope=s)
            w3 = sb("w3", [HID, 2, 2, 512], scope=s)
            decay = sb("decay", [P, 2, 2, 512], scope=s)
            taps = sb("taps", [P, 2, 2, 512], scope=s)
            start_part = sb("start_part", [P, 2, 4 * SLAB // P], scope=s)
            spec = sb("spec", [P, 4, 512], scope=s)
            acc_odd = sb("acc_odd", [P, 2, SLAB], scope=s)
            rows = sb("rows", [2, SLAB], scope=s)
            sum_sq = sb("sum_sq", [P, 4, 2 * TOK], scope=s)
            fwd0 = sb("fwd0", [P, 2, 2 * NFREQ], scope=s)
        with ExitStack() as mid:
            s = mid
            probs = sb("probs", [P, 2, 512], scope=s)
            probs_t = sb("probs_t", [P, 2, 4, TOK], scope=s)
            q_rot = sb("q_rot", [P, 2, TOK], scope=s)
            q_sin = sb("q_sin", [P, 2, TOK], scope=s)
            k_sq = sb("k_sq", [P, 4, TOK], scope=s)
            sm = sb("sm", [P, 2, 4], scope=s)
            v = sb("v", [P, KV_HEADS, 4, HEAD], scope=s)
        lat = sb("lat", [P, KB, 2 * TOK], F32R)
        alt = sb("alt", [P, KB, 2 * TOK], F32R)
        with ExitStack() as s:
            hm = sb("hm", [P, 2, 4, TOK], scope=s)
            sq = sb("sq", [P, 2, 4, TOK], scope=s)
            rn = [sb(n, [P, 2 * TOK], scope=s) for n in ("rn_a", "rn_r", "rn_y")]
            rn.append(rn[1])
            xc = sb("xc", [P, KB, TOK], scope=s)
            rs_tok = sb("rs_tok", [P, 2 * TOK], scope=s)
        with ExitStack() as s:
            rope = sb("rope", [P, N_ROPE], scope=s)
            swap_q, swap_k = sb("swap_q", [P, P], scope=s), sb("swap_k", [P, P], scope=s)
            q = sb("q", [P, HEADS, TOK], scope=s)
            kt = sb("kt", [P, KV_HEADS, 2 * TOK], scope=s)
            vt = sb("vt", [P, KV_HEADS, 2 * TOK], scope=s)
            cos_q, cos_k = sb("cos_q", [P, TOK], scope=s), sb("cos_k", [P, TOK], scope=s)
        with ExitStack() as s:
            u = sb("u", [P, 3, 4, TOK], scope=s)
            z_tok = sb("z_tok", [P, 2, 2, 256], scope=s)
            h_spec = sb("h_spec", [P, 4, 512], scope=s)
            y_spec = sb("y_spec", [P, 2, 4, 256], scope=s)
            fwd = sb("fwd", [P, 2, 2 * NFREQ], scope=s)
            back = sb("back", [P, 4, TOK], scope=s)
        ps = stack.enter_context(nc.psum_tensor("ps", [P, 8, 512], F32))
        spec_dram = nc.dram_tensor("spec_dram", (8, P, 4, 512), F32, kind="Internal").ap()

        ident = const[:, IDENT:IDENT + P]
        swap = const[:, SWAP:SWAP + P]
        cos, sin = rope[:, COS:COS + TOK], rope[:, SIN:SIN + TOK]
        mask = rope[:, MASK:MASK + 2 * P].rearrange("p (b k) -> p b k", b=2)

        def vec(name, i=0, n=1):
            return vecs[:, ds(VECS[name] + i, n)]

        in_const, in_vecs, in_x, in_ctx = sem("in_const"), sem("in_vecs"), sem("in_x"), sem("in_ctx")
        in_fw, in_w1, in_feats, in_fwd0 = sem("in_fw"), sem("in_w1"), sem("in_feats"), sem("in_fwd0")
        in_rope = sem("in_rope")
        in_fwd, in_back = sem("in_fwd"), sem("in_back")
        in_w3 = [sem("in_w3_0"), sem("in_w3_1")]
        in_decay = [sem("in_decay_0"), sem("in_decay_1")]
        unit_landed = [sem(f"unit_landed{j}") for j in range(RING)]
        slab_landed = [sem(f"slab_landed{j}") for j in range(RING)]
        hi_ready, split_ready = sem("hi_ready"), sem("split_ready")
        units_done = sem("units_done")
        lo_copied, psum_free = sem("lo_copied"), sem("psum_free")
        slabs_used, acc_ready = sem("slabs_used"), sem("acc_ready")
        start_landed = [sem(f"start_landed{j}") for j in range(START_RING)]
        start_free = [sem(f"start_free{j}") for j in range(START_RING)]
        rows_copied, start_turned, start_summed = sem("rows_copied"), sem("start_turned"), sem("start_summed")
        sq_summed = sem("sq_summed")
        mod_cols, mod_ready, mod_summed = sem("mod_cols"), sem("mod_ready"), sem("mod_summed")
        started = sem("started")
        silu_exp, silu_v = sem("silu_exp"), sem("silu_v")
        tables = sem("tables")
        squares, square_sums = sem("squares"), sem("square_sums")
        rs_v, rs_root = sem("rs_v"), sem("rs_root")
        gains, normed, norm_hi, norm_ready = sem("gains"), sem("normed"), sem("norm_hi"), sem("norm_ready")
        x_hi_added = sem("x_hi_added")
        squared, hidden_hi, hidden_ready = sem("squared"), sem("hidden_hi"), sem("hidden_ready")
        centred, tapped = sem("centred"), sem("tapped")
        hid_mm, hid_v, hid_sin = sem("hid_mm"), sem("hid_v"), sem("hid_sin")
        taps_mm, taps_ready = sem("taps_mm"), sem("taps_ready")
        spec_mm, spec_copied, spec_stored = sem("spec_mm"), sem("spec_copied"), sem("spec_stored")
        vt_turned, v_ready = sem("vt_turned"), sem("v_ready")
        k_swapped, k_v, k_squared, kq_sums, k_spread = (sem(n) for n in (
            "k_swapped", "k_v", "k_squared", "kq_sums", "k_spread"))
        q_swapped, q_v = sem("q_swapped"), sem("q_v")
        scores, scored_v, row_max, exp_done, prob_v, probs_turned, probs_copied = (sem(n) for n in (
            "scores", "scored_v", "row_max", "exp_done", "prob_v", "probs_turned", "probs_copied"))
        scored_w = sem("scored_w")
        head_out, head_hi, head_ready = sem("head_out"), sem("head_hi"), sem("head_ready")
        h_landed = sem("h_landed")
        turned, tok_ready, z_spec, spec_v, y_back = (sem(n) for n in (
            "turned", "tok_ready", "z_spec", "spec_v", "y_back"))
        conv_v = [sem("conv_v0"), sem("conv_v1")]
        z_hi, z_ready = sem("z_hi"), sem("z_ready")
        stored = [sem(f"stored{c}") for c in range(4)]

        T_Q, T_KV, T_OUT, T_MLP0 = 1, 5, 7, 11
        T_HY = T_MLP0 + 32
        T_HOUT = T_HY + 12
        T_MLP1 = T_HOUT + 4
        M_Q = 0
        M_KV, M_ATT = M_Q + 8, M_Q + 12
        M_OUT = M_ATT + 8
        M_MLP0 = M_OUT + 8
        M_HY = M_MLP0 + 32
        M_HOUT = M_HY + 16
        M_END = M_HOUT + 4
        FIN_Q, FIN_KV, FIN_ATT, FIN_OUT, FIN_MLP0 = 1, 2, 3, 4, 5
        FIN_HY = FIN_MLP0 + 8
        FIN_HOUT = FIN_HY + 4
        half = SLAB // P

        class Slabs:

            def __init__(self, layer, halves, per, m4, first_kb=0):
                self.layer, self.halves, self.per, self.m4, self.kb0 = layer, halves, per, m4, first_kb

            def each(self, i, j0, n):
                nh = len(self.halves)
                for j in range(j0, j0 + n):
                    kb = self.kb0 + i * (self.per // nh) + j // nh
                    first = isinstance(kb, int) and kb == 0
                    yield j % RING, self.m4 + i * (self.per // RING) + j // RING, kb, j % nh, self.halves[j % nh], first

        def sp_slabs(e, sl, i, j0, n):
            for slot, m4, kb, _, h, _ in sl.each(i, j0, n):
                e.wait_ge(slabs_used, 4 * m4 + slot + 1)
                e.dma_start(slab[:, slot, :], a["mod_w"][sl.layer, ds(kb * P, P), ds(h * SLAB, SLAB)]
                            ).then_inc(slab_landed[slot], 16)

        def sp_iter(e, T, w, row, col, i, sl):
            for n in range(8):
                e.wait_ge(split_ready, 8 * T + n - 3)
                src = w[ds(row + (n % 4) * UNIT_KB * P, UNIT_KB * P), ds(col + (n // 4) * UNIT_COLS, UNIT_COLS)]
                e.dma_start(raw[:, n % RING], src.rearrange("(k p) n -> p k n", p=P)
                            ).then_inc(unit_landed[n % RING], 16)
                if sl and n >= 4:
                    r = sl.per // 4
                    sp_slabs(e, sl, i, (n - 4) * r, r)

        def start_slot(j):
            j %= START_RING
            return slab[:, j] if j < RING else raw[:, j - RING].rearrange("p k n -> p (k n)")

        def sp_call(e, T, n, w, row, col, sl):
            with e.Fori(0, n) as i:
                sp_iter(e, T + i, w, row, col + i * 512, i, sl)

        def pe_iter(e, T, tile, ready, ctx_tile=None):
            for n in range(8):
                g = n // 4
                e.wait_ge(split_ready, 8 * T + n + 1)
                if ready:
                    e.wait_ge(*ready(n % 4))
                if n % 4 == 0:
                    e.wait_ge(psum_free, 2 * T + g - 1)
                for kk in range(UNIT_KB):
                    kb = (n % 4) * UNIT_KB + kk
                    for fb in range(2):
                        cols = slice(fb * P, (fb + 1) * P)
                        for t, bank in ((tile, 2 * g + fb), (ctx_tile, 4 + 2 * g + fb)):
                            if t is None:
                                continue
                            e.matmul(ps[:, bank, :], w_hi[:, n % RING, kk, cols], t[:, kb, :],
                                     start=(kb == 0), stop=False)
                            mm = e.matmul(ps[:, bank, 0:TOK], w_lo[:, n % RING, kk, cols], t[:, kb, 0:TOK],
                                          start=False, stop=(kb == KB - 1))
                mm.then_inc(units_done, 1)

        def pe_finish(e, sl_count, fin, n_acc):
            e.wait_ge(slabs_used, 4 * sl_count + 4)
            e.wait_ge(mod_ready, fin + 1)
            for h in range(n_acc):
                for b in range(half):
                    mm = e.transpose(ps[:, 4 + 2 * h + b // 4, (b % 4) * P:(b % 4 + 1) * P],
                                     acc[:, h, b * P:(b + 1) * P], ident)
            mm.then_inc(mod_cols, 1)

        def act_split(e, T, n):
            e.wait_ge(unit_landed[n % RING], 16 * (2 * T + n // 4 - 1))
            e.wait_ge(units_done, 8 * T + n - 3)
            e.activation(w_hi[:, n % RING], raw[:, n % RING], ACT.Copy).then_inc(hi_ready, 1)

        def dve_split(e, T, n):
            e.wait_ge(hi_ready, 8 * T + n + 1)
            e.tensor_tensor(w_lo[:, n % RING], raw[:, n % RING], w_hi[:, n % RING].bitcast(F32),
                            ALU.subtract).then_inc(split_ready, 1)

        def dve_slabs(e, sl, i, j0, n):
            for slot, m4, kb, ac, _, first in sl.each(i, j0, n):
                e.wait_ge(slab_landed[slot], 16 * (m4 + 1))
                scale = silu[:, ds(kb, 1)]
                if first:
                    e.tensor_scalar(acc[:, ac], slab[:, slot], scale, None, ALU.mult).then_inc(slabs_used, 1)
                else:
                    e.wait_ge(slabs_used, 4 * m4 + slot + 5 - len(sl.halves))
                    e.scalar_tensor_tensor(acc[:, ac], slab[:, slot], scale, acc[:, ac],
                                           ALU.mult, ALU.add).then_inc(slabs_used, 1)

        def dve_finish(e, fin, dests):
            e.wait_ge(mod_cols, fin + 1)
            for h in range(len(dests)):
                ins = e.tensor_reduce(mod_part[:, h], ps[:, 4 + 2 * h:6 + 2 * h, :].rearrange("p a (b k) -> p (a b) k", k=P),
                                      AX.X, ALU.add)
            ins.then_inc(mod_summed, 1)
            e.wait_ge(mod_summed, fin + 1)
            for h, at in enumerate(dests):
                ins = e.tensor_tensor(mod[:, ds(at, half)], mod_part[:, h], vec("mod_b", at, half), ALU.add)
            ins.then_inc(mod_ready, 1)
            e.wait_ge(mod_ready, fin + 2)

        class Readout:

            def bank(self, g, part):
                return ps[:, 2 * g:2 * g + 2, part * TOK:(part + 1) * TOK]

            def act_wait(self, e, T, g):
                e.wait_ge(units_done, 8 * T + 4 * g + 4)
                e.wait_ge(psum_free, 2 * T + g - 1)

            def act_head(self, e, T, g):
                self.act_wait(e, T, g)
                e.activation(lo_sum[:, g], self.bank(g, 1), ACT.Copy).then_inc(lo_copied, 1)

            def act_tail(self, e, T, g):
                pass

            def dve_tail(self, e, T, g):
                pass

        class Queries(Readout):
            def __init__(self, i):
                self.i = i

            def act_head(self, e, T, g):
                self.act_wait(e, T, g)
                e.activation(lo_sum[:, g], self.bank(g, 1), ACT.Copy, scale=QSCALE).then_inc(lo_copied, 1)

            def dve_head(self, e, T, g):
                e.wait_ge(lo_copied, 2 * T + g + 1)
                e.scalar_tensor_tensor(q[:, ds(4 * self.i + 2 * g, 2), :], self.bank(g, 0), QSCALE, lo_sum[:, g],
                                       ALU.mult, ALU.add).then_inc(psum_free, 1)

        class KeysValues(Readout):
            def __init__(self, dst):
                self.dst = dst

            def ctx_bank(self, g, part):
                return ps[:, 4 + 2 * g:6 + 2 * g, part * TOK:(part + 1) * TOK]

            def act_head(self, e, T, g):
                self.act_wait(e, T, g)
                e.activation(lo_sum[:, g], self.bank(g, 1), ACT.Copy)
                e.activation(sum_sb[:, g], self.ctx_bank(g, 1), ACT.Copy).then_inc(lo_copied, 1)

            def dve_head(self, e, T, g):
                e.wait_ge(lo_copied, 2 * T + g + 1)
                d = self.dst[:, 2 * g:2 * g + 2, :]
                e.tensor_tensor(d[:, :, 0:TOK], self.bank(g, 0), lo_sum[:, g], ALU.add)
                e.tensor_tensor(d[:, :, TOK:2 * TOK], self.ctx_bank(g, 0), sum_sb[:, g],
                                ALU.add).then_inc(psum_free, 1)

        class Gated(Readout):

            def __init__(self, gate, i, n_out, bias=None):
                self.gate, self.i, self.n_out, self.bias = gate, i, n_out, bias
                self.ready = {G1: FIN_Q, G2: FIN_MLP0, G3: FIN_HY - 1, G4: FIN_HOUT}[gate] + 2

            def act_head(self, e, T, g):
                self.act_wait(e, T, g)
                e.wait_ge(mod_ready, self.ready)
                for fb in range(2):
                    f = 4 * self.i + 2 * g + fb
                    bias = gate_bias[:, ds(f, 1)] if self.bias else 0.0
                    ins = e.activation(lo_sum[:, g, fb], ps[:, 2 * g + fb, TOK:2 * TOK], ACT.Identity,
                                       bias=bias, scale=mod[:, ds(self.gate + f, 1)])
                ins.then_inc(lo_copied, 1)

            def dve_head(self, e, T, g):
                e.wait_ge(lo_copied, 2 * T + g + 1)
                for fb in range(2):
                    f = 4 * self.i + 2 * g + fb
                    xf = x[:, ds(f, 1), :]
                    ins = e.scalar_tensor_tensor(xf, ps[:, 2 * g + fb:2 * g + fb + 1, 0:TOK],
                                                 mod[:, ds(self.gate + f, 1)], xf, ALU.mult, ALU.add)
                ins.then_inc(x_hi_added, 1)
                e.wait_ge(x_hi_added, self.n_out + 2 * self.i + g + 1)
                xg = x[:, ds(4 * self.i + 2 * g, 2), :]
                e.tensor_tensor(xg, xg, lo_sum[:, g], ALU.add).then_inc(psum_free, 1)

        class Hidden(Readout):

            def __init__(self, i, n_hid):
                self.i, self.n = i, n_hid

            def dve_head(self, e, T, g):
                e.wait_ge(lo_copied, 2 * T + g + 1)
                e.tensor_tensor(sum_sb[:, g], self.bank(g, 0), lo_sum[:, g], ALU.add).then_inc(psum_free, 1)
                e.wait_ge(psum_free, 2 * T + g + 1)
                e.scalar_tensor_tensor(sum_sb[:, g], sum_sb[:, g], 0.0, sum_sb[:, g],
                                       ALU.max, ALU.mult).then_inc(squared, 1)

            def act_tail(self, e, T, g):
                e.wait_ge(squared, self.n + 2 * self.i + g + 1)
                e.activation(alt[:, ds(4 * self.i + 2 * g, 2), 0:TOK], sum_sb[:, g], ACT.Copy).then_inc(hidden_hi, 1)

            def dve_tail(self, e, T, g):
                e.wait_ge(hidden_hi, self.n + 2 * self.i + g + 1)
                f = ds(4 * self.i + 2 * g, 2)
                e.tensor_tensor(alt[:, f, TOK:2 * TOK], sum_sb[:, g], alt[:, f, 0:TOK].bitcast(F32),
                                ALU.subtract).then_inc(hidden_ready, 1)

        class ShortConv(Readout):

            def __init__(self, part, col, n):
                self.part, self.col, self.n = part, col, n

            def act_head(self, e, T, g):
                self.act_wait(e, T, g)
                for fb in range(2):
                    ins = e.activation(lo_sum[:, g, fb], ps[:, 2 * g + fb, TOK:2 * TOK], ACT.Identity,
                                       bias=vec("b_in", self.col + 2 * g + fb))
                ins.then_inc(lo_copied, 1)

            def dve_head(self, e, T, g):
                e.wait_ge(lo_copied, 2 * T + g + 1)
                e.tensor_tensor(sum_sb[:, g], self.bank(g, 0), lo_sum[:, g], ALU.add).then_inc(psum_free, 1)

            def act_tail(self, e, T, g):
                e.wait_ge(psum_free, 2 * T + g + 1)
                for fb in range(2):
                    f = self.col + 2 * g + fb
                    ins = e.activation(u[:, self.part, 2 * g + fb], sum_sb[:, g, fb], ACT.Identity,
                                       bias=vec("conv_b", f), scale=vec("conv_w", 3 * KB + f))
                ins.then_inc(centred, 1)

            def dve_tail(self, e, T, g):
                e.wait_ge(centred, self.n + g + 1)
                for side in range(2):
                    for fb in range(2):
                        o = u[:, self.part, 2 * g + fb]
                        to = o[:, 1:TOK] if side == 0 else o[:, 0:TOK - 1]
                        fr = sum_sb[:, g, fb, 0:TOK - 1] if side == 0 else sum_sb[:, g, fb, 1:TOK]
                        ins = e.scalar_tensor_tensor(to, fr, vec("conv_w", 6 * KB * side + self.col + 2 * g + fb), to,
                                                     ALU.mult, ALU.add)
                    ins.then_inc(tapped, 1)
                    e.wait_ge(tapped, 2 * (self.n + g) + side + 1)

        def act_iter(e, T, prev, cur, norm=None, ctx_chunk=None):
            for n in range(8):
                act_split(e, T, n)
                if norm and n < 4:
                    act_norm_hi(e, norm[0], norm[4], n)
                if ctx_chunk is not None and n == 5:
                    act_norm_hi(e, 1, alt, ctx_chunk)
                if n == 0 and prev:
                    prev.act_tail(e, T - 1, 0)
                if n == 3 and prev:
                    prev.act_head(e, T - 1, 1)
                if n == 4 and prev:
                    prev.act_tail(e, T - 1, 1)
                if n == 7:
                    cur.act_head(e, T, 0)

        def act_flush(e, T, r):
            r.act_tail(e, T, 0)
            r.act_head(e, T, 1)
            r.act_tail(e, T, 1)

        def dve_iter(e, T, prev, cur, i, sl, finish=None, norm=None, ctx_chunk=None):
            for n in range(8):
                if norm and n < 4:
                    dve_normalise(e, *norm[:4], n)
                if ctx_chunk is not None and n == 5:
                    dve_normalise(e, *NORM_CTX[:4], ctx_chunk)
                dve_split(e, T, n)
                if norm and n < 4:
                    dve_norm_lo(e, norm[0], norm[4], n)
                if ctx_chunk is not None and n == 5:
                    dve_norm_lo(e, 1, alt, ctx_chunk)
                if n == 0 and prev:
                    prev.dve_tail(e, T - 1, 0)
                if n == 3:
                    if finish:
                        dve_finish(e, *finish)
                    if prev:
                        prev.dve_head(e, T - 1, 1)
                if n == 4 and prev:
                    prev.dve_tail(e, T - 1, 1)
                if n >= 4 and sl:
                    r = sl.per // 4
                    dve_slabs(e, sl, i, (n - 4) * r, r)
                if n == 7:
                    cur.dve_head(e, T, 0)

        def dve_flush(e, T, r):
            r.dve_tail(e, T, 0)
            r.dve_head(e, T, 1)
            r.dve_tail(e, T, 1)

        def act_call(e, T, n, prev, kind, norm=None):
            with_ctx = norm is not None and norm[0] == 0
            act_iter(e, T, prev, kind(0), norm, 0 if with_ctx else None)
            with e.Fori(1, n) as i:
                act_iter(e, T + i, kind(i - 1), kind(i), None, i if with_ctx else None)
            return kind(n - 1)

        def dve_call(e, T, n, prev, kind, sl, finish=None, norm=None):
            with_ctx = norm is not None and norm[0] == 0
            dve_iter(e, T, prev, kind(0), 0, sl, finish, norm, 0 if with_ctx else None)
            with e.Fori(1, n) as i:
                dve_iter(e, T + i, kind(i - 1), kind(i), i, sl, None, None, i if with_ctx else None)
            return kind(n - 1)

        def act_stats(e, k, src, *waits):
            for w in waits:
                e.wait_ge(*w)
            for c in range(4):
                if 4 * k + c >= 2:
                    e.wait_ge(square_sums, 4 * k + c - 1)
                e.activation(sq[:, c % 2], src[:, 4 * c:4 * c + 4, :], ACT.Square).then_inc(squares, 1)

        def pe_stats(e, k):
            for c in range(4):
                e.wait_ge(squares, 4 * k + c + 1)
                for kk in range(4):
                    mm = e.matmul(ps[:, 6, 0:TOK], ones[:], sq[:, c % 2, kk, :],
                                  start=(c == 0 and kk == 0), stop=(c == 3 and kk == 3))
                mm.then_inc(square_sums, 1)

        def dve_rsqrt(e, r, sums, n, scale, eps, out, *waits, temps=(rs_a, rs_r, rs_y, rs_t)):
            for w in waits:
                e.wait_ge(*w)
            A, R, Y, Tm = (t[:, 0:n] for t in temps)
            e.tensor_scalar(A, sums, scale, eps, ALU.mult, ALU.add).then_inc(rs_v, 1)
            e.wait_ge(rs_v, 6 * r + 1)
            e.reciprocal(R, A).then_inc(rs_v, 1)
            e.wait_ge(rs_root, r + 1)
            e.tensor_tensor(Tm, Y, Y, ALU.mult).then_inc(rs_v, 1)
            e.wait_ge(rs_v, 6 * r + 3)
            e.tensor_tensor(Tm, Tm, A, ALU.mult).then_inc(rs_v, 1)
            e.wait_ge(rs_v, 6 * r + 4)
            e.tensor_scalar(Tm, Tm, -0.5, 1.5, ALU.mult, ALU.add).then_inc(rs_v, 1)
            e.wait_ge(rs_v, 6 * r + 5)
            e.tensor_tensor(out, Y, Tm, ALU.mult).then_inc(rs_v, 1)
            e.wait_ge(rs_v, 6 * r + 6)

        def act_root(e, r, n, temps=(rs_a, rs_r, rs_y, rs_t)):
            e.wait_ge(rs_v, 6 * r + 2)
            e.activation(temps[2][:, 0:n], temps[1][:, 0:n], ACT.Sqrt).then_inc(rs_root, 1)

        def factors(k):
            at = TOK * (k == 1)
            return rs_tok[:, at:at + TOK].rearrange("p (a t) -> p a t", a=1).to_broadcast([P, 4, TOK])

        def norm_part(k, c):
            return hm[:, 0 if k == 1 else c % 2]

        def dve_normalise(e, k, src, gains_ap, shift_ap, c):
            h = norm_part(k, c)
            if k == 1:
                e.wait_ge(norm_ready, 4 + c)
            elif c >= 2 and shift_ap is not None:
                e.wait_ge(norm_ready, 4 * k + c - 1)
            e.tensor_tensor(h, src[:, ds(4 * c, 4), :], factors(k),
                            ALU.mult).then_inc(normed, 1)
            e.wait_ge(normed, 8 * k + 2 * c + 1)
            for kk in range(4):
                kb = ds(4 * c + kk, 1)
                if shift_ap is None:
                    ins = e.tensor_scalar(h[:, kk], h[:, kk], gains_ap[:, kb], None, ALU.mult)
                else:
                    ins = e.tensor_scalar(h[:, kk], h[:, kk], gains_ap[:, kb], shift_ap[:, kb],
                                          ALU.mult, ALU.add)
            ins.then_inc(normed, 1)

        def dve_norm_lo(e, k, dst, c):
            e.wait_ge(norm_hi, 4 * k + c + 1)
            e.tensor_tensor(dst[:, ds(4 * c, 4), TOK:2 * TOK], norm_part(k, c),
                            dst[:, ds(4 * c, 4), 0:TOK].bitcast(F32), ALU.subtract).then_inc(norm_ready, 1)

        def act_norm_hi(e, k, dst, c):
            e.wait_ge(normed, 8 * k + 2 * c + 2)
            e.activation(dst[:, ds(4 * c, 4), 0:TOK], norm_part(k, c), ACT.Copy).then_inc(norm_hi, 1)

        def dve_gain(e, n, dst, scale_cols, g):
            e.scalar_tensor_tensor(dst, scale_cols, 1.0, g, ALU.add, ALU.mult).then_inc(gains, 1)
            e.wait_ge(gains, n)

        def mods(layer, s_):
            return mod[:, (layer * N_MOD + s_) * KB:(layer * N_MOD + s_ + 1) * KB]

        NORM_X = (0, x, gain[:, 0:KB], mods(0, 0), lat)
        NORM_CTX = (1, xc, gain[:, KB:2 * KB], mod_ctx[:, 0:KB], alt)
        NORM_MLP = ((2, x, gain[:, 0:KB], mods(0, 3), lat), (4, x, gain[:, 0:KB], mods(1, 3), lat))
        NORM_HY = (3, x, gain[:, 0:KB], mods(1, 0), lat)

        SL_Q = Slabs(0, [4, 5], 8, M_Q)
        SL_KV = Slabs(0, [6], 8, M_KV)
        SL_ATT = [Slabs(0, [8, 9], 4, M_ATT + n, 2 * n) for n in range(8)]
        SL_OUT = Slabs(0, [7, 10], 8, M_OUT)
        SL_UP0 = Slabs(0, [11], 4, M_MLP0)

        def sl_mlp0(q_, down):
            return Slabs(1, [2 * q_ - 1 + down], 4, M_MLP0 + 8 * q_ + 4 * down)

        def sl_hy(c):
            return Slabs(1, [7 + c], 4, M_HY + 4 * c)

        SL_HOUT = Slabs(1, [11], 4, M_HOUT)
        HB = SLAB // P

        def mod_col(layer, half_):
            return layer * N_MOD * KB + half_ * HB

        G1, G2, G3, G4 = (2 * KB, 5 * KB, 8 * KB, 11 * KB)
        OUT_0, OUT_M0, OUT_H, OUT_M1 = 0, 8, 40, 48
        w_ff = D_FF // D

        block = stack.enter_context(nc.Block())

        @block.sync
        def _(e):
            e.dma_start(vecs[:], a["vecs"]).then_inc(in_vecs, 16)
            e.dma_start(f_w[:, :], a["f_w"]).then_inc(in_fw, 16)
            e.dma_start(feats[:], a["feats"]).then_inc(in_feats, 16)
            e.dma_start(const[:], a["const"]).then_inc(in_const, 16)
            e.dma_start(fwd0[:], a["fwd"]).then_inc(in_fwd0, 16)
            e.wait_ge(started, 1)
            with e.Fori(0, 2) as cc:
                for par in range(2):
                    c = 2 * cc + par
                    for j in range(16):
                        e.wait_ge(start_free[j % START_RING], 2 * c + j // START_RING + 1)
                        e.dma_start(start_slot(j), a["mod_w"][0, j * P:(j + 1) * P, ds(c * SLAB, SLAB)]
                                    ).then_inc(start_landed[j % START_RING], 16)
                        if j == 1:
                            e.wait_ge(taps_mm, 2 * c + 2)
                            e.dma_start(w3[:, par], a["w3"][:, :, ds(512 * c, 512)]).then_inc(in_w3[par], 16)
                            e.wait_ge(taps_ready, 2 * c + 2)
                            e.dma_start(decay[:, par], a["decay"][ds(c, 1)].rearrange("a p t n -> (a p) t n")
                                        ).then_inc(in_decay[par], 16)
                        if j in (4, 7):
                            name, dst, signal = (("x", x, in_x), ("ctx", xc, in_ctx))[j // 7]
                            e.dma_start(dst[:, ds(4 * c, 4), :], a[name][:, ds(4 * c, 4), :]).then_inc(signal, 16)
            for j in range(START_RING):
                e.wait_ge(start_free[j], 4 * 2 + 1)
            sp_call(e, T_Q, 4, a["attn_w_in"], 0, 0, SL_Q)
            e.wait_ge(norm_ready, 8)
            e.dma_start(rope[:], a["rope"]).then_inc(in_rope, 16)
            sp_call(e, T_KV, 2, a["attn_w_in"], 0, KV_COL, SL_KV)
            for n in range(8):
                sp_slabs(e, SL_ATT[n], 0, 0, 4)
            sp_call(e, T_OUT, 4, a["attn_w_out"], 0, 0, SL_OUT)

            def mlp(layer, T, q_, sl_up, sl_down):
                sp_call(e, T, 4, a[f"mlp_w1_{layer}"], 0, q_ * D, sl_up)
                sp_call(e, T + 4, 4, a[f"mlp_w2_{layer}"], q_ * D, 0, sl_down)

            mlp(0, T_MLP0, 0, SL_UP0, sl_mlp0(0, 1))
            with e.Fori(1, w_ff) as q_:
                mlp(0, T_MLP0 + 8 * q_, q_, sl_mlp0(q_, 0), sl_mlp0(q_, 1))
            e.wait_ge(spec_stored, 9 * 16)
            with e.Fori(0, 4) as c:
                for k, part in enumerate((2, 0, 1)):
                    sp_iter(e, T_HY + 3 * c + k, a["hy_w_in"], 0, (c + part * 4) * 512, k, sl_hy(c))
                sp_slabs(e, sl_hy(c), 3, 0, 4)
                for o in range(2):
                    e.wait_ge(spec_v, 12 * (2 * c + o) + 6)
                    e.dma_start(h_spec[:], spec_dram[ds(2 * c + o, 1)].rearrange("a p f c -> (a p) f c")
                                ).then_inc(h_landed, 16)
            sp_call(e, T_HOUT, 4, a["hy_w_out"], 0, 0, SL_HOUT)
            mlp(1, T_MLP1, 0, None, None)
            with e.Fori(1, w_ff) as q_:
                mlp(1, T_MLP1 + 8 * q_, q_, None, None)
            for c in range(4):
                e.wait_ge(normed, 8 * 5 + 2 * c + 2)
                e.dma_start(a["y"][:, 4 * c:4 * c + 4, :], hm[:, c % 2]).then_inc(stored[c], 16)
            for c in range(4):
                e.wait_ge(stored[c], 16)

        @block.tensor
        def _(e):
            e.sem_inc(units_done, 8)
            e.sem_inc(taps_mm, 4)
            e.sem_inc(scores, 1)
            e.sem_inc(mod_cols, 1)
            e.wait_ge(started, 1)
            e.wait_ge(in_fw, 16)
            e.wait_ge(in_feats, 16)
            e.matmul(ps[0:HID, 0, 0:TOK], f_w[0:FILTER_EMB, 0:HID], feats[:], start=True, stop=True).then_inc(hid_mm, 1)
            e.wait_ge(hid_sin, 1)
            e.matmul(ps[0:HID, 1, 0:TOK], f_w[:, HID:2 * HID], hid_1[:], start=True, stop=True).then_inc(hid_mm, 1)
            e.wait_ge(hid_sin, 2)
            e.wait_ge(silu_v, 3)
            e.wait_ge(in_fwd0, 16)
            e.wait_ge(in_const, 16)

            def pe_slab(c, r):
                j = PE_SLABS[r]
                e.wait_ge(start_landed[j % START_RING], 16 * (2 * c + j // START_RING + 1))
                pair = silu[:].rearrange("p (w k) -> p w k", w=2)[:, :, j]
                for b in range(2):
                    mm = e.matmul(ps[0:2, 4 + b, :], pair, start_slot(j)[:, b * 512:(b + 1) * 512],
                                  start=(r == 0), stop=(r == len(PE_SLABS) - 1))
                mm.then_inc(start_free[j % START_RING], 1)

            with e.Fori(0, 2) as cc:
                for par in range(2):
                    c = 2 * cc + par
                    for o in range(2):
                        if o == 0:
                            e.wait_ge(start_summed, c + 1)
                        pe_slab(c, 3 * o)
                        if o == 0:
                            e.wait_ge(in_w3[par], 16 * (cc + 1))
                        e.wait_ge(taps_ready, 2 * c + o + 4)
                        for tb in range(2):
                            mm = e.matmul(ps[:, tb, :], hid_2[:, tb * P:(tb + 1) * P], w3[:, par, o, :],
                                          start=True, stop=True)
                        mm.then_inc(taps_mm, 1)
                        pe_slab(c, 3 * o + 1)
                        if o == 1:
                            pe_slab(c, 5)
                        e.wait_ge(taps_ready, 2 * c + o + 5)
                        e.wait_ge(spec_copied, 4 * (2 * c + o) + 2)
                        for b in range(4):
                            for tb in range(2):
                                e.transpose(ps[:, 6 + b // 2, (b % 2) * TOK + tb * P:(b % 2) * TOK + (tb + 1) * P],
                                            taps[:, o, tb, b * P:(b + 1) * P], ident)
                        for f in range(4):
                            e.wait_ge(spec_copied, 4 * (2 * c + o) + f + 1)
                            for kb in range(2):
                                mm = e.matmul(ps[:, 2 + f % 2, :], fwd0[:, kb, f * P:(f + 1) * P], taps[:, o, kb, :],
                                              start=(kb == 0), stop=(kb == 1))
                            mm.then_inc(spec_mm, 1)
                        if o == 0:
                            pe_slab(c, 2)
                    e.wait_ge(rows_copied, c + 1)
                    e.wait_ge(start_free[15 % START_RING], 2 * c + 3)
                    for w in range(2):
                        for b in range(half):
                            e.transpose(ps[:, 4 + 2 * w + b // 4, (b % 4) * P:(b % 4 + 1) * P],
                                        (acc, acc_odd)[par][:, w, b * P:(b + 1) * P], ident)
                    for b in range(half):
                        mm = e.transpose(ps[:, 0, 2 * b:2 * b + 2], rows[:, b * P:(b + 1) * P], ident[0:2, 0:2])
                    mm.then_inc(start_turned, 1)
            e.wait_ge(sq_summed, 10)
            for c in range(4):
                mm = e.matmul(ps[:, 1, :], ones[:], sum_sq[:, c, :], start=(c == 0), stop=(c == 3))
            mm.then_inc(square_sums, 8)
            e.wait_ge(start_summed, 5)
            with e.Fori(0, 4) as i:
                pe_iter(e, T_Q + i, lat, lambda j: (norm_ready, 1 + j))
            pe_finish(e, M_KV, FIN_Q, 2)
            e.wait_ge(mod_ready, FIN_Q + 2)
            with e.Fori(0, 2) as i:
                pe_iter(e, T_KV + i, lat, lambda j: (norm_ready, 5 + j), alt)
            e.wait_ge(psum_free, 2 * (T_KV + 2))
            pe_finish(e, M_ATT, FIN_KV, 1)
            e.wait_ge(mod_ready, FIN_KV + 2)
            for h in range(KV_HEADS):
                for tb in range(4):
                    mm = e.transpose(ps[:, h, tb * P:(tb + 1) * P], vt[:, h, tb * P:(tb + 1) * P], ident)
                mm.then_inc(vt_turned, 1)
            for pr in range(2):
                e.wait_ge(tables, 5)
                for h in range(2):
                    mm = e.matmul(ps[:, 4 + pr, h * TOK:(h + 1) * TOK], swap_k[:] if pr else swap,
                                  kt[:, 2 * pr + h, 0:TOK], start=True, stop=True)
                mm.then_inc(k_swapped, 1)
            for h in range(2):
                for c in range(4):
                    e.wait_ge(k_squared, h + 1)
                    tb = (h * 4 + c) % 8
                    mm = e.matmul(ps[:, 6, tb:tb + 1], k_sq[:, 2 * h + c // 2, (c % 2) * P:(c % 2 + 1) * P],
                                  ones[:, 0:1], start=True, stop=True)
            mm.then_inc(kq_sums, 1)
            for hp in range(4):
                e.wait_ge(k_squared, 3 + hp)
                if hp == 0:
                    e.wait_ge(rs_v, 6 * 2 + 1)
                for h in range(2):
                    for tb in range(2):
                        col = (2 * hp + h) * 2 + tb
                        mm = e.matmul(ps[:, 6, 16 + col:17 + col], k_sq[:, 2 * (hp % 2) + h, tb * P:(tb + 1) * P],
                                      ones[:, 0:1], start=True, stop=True)
                mm.then_inc(kq_sums, 1)
            e.wait_ge(rs_v, 6 * 2 + 6)
            e.wait_ge(v_ready, 4)
            for h in range(2):
                for c in range(4):
                    mm = e.matmul(ps[:, h, c * P:(c + 1) * P], rs_k[:, 4 * h + c:4 * h + c + 1].to_broadcast([P, P]),
                                  ident, start=True, stop=True)
            mm.then_inc(k_spread, 1)
            e.wait_ge(k_v, 6)

            def pe_heads(kv, n, pair):
                e.wait_ge(q_v, 3 * n + 3)
                e.matmul(ps[:, 0, :], swap if kv < 2 else swap_q[:], q[:, ds(4 * kv + 2 * pair, 2), :],
                         start=True, stop=True).then_inc(q_swapped, 1)
                e.wait_ge(q_v, 3 * n + 6)

                def score(j):
                    e.wait_ge(exp_done, 4 * n + j + 1)
                    e.matmul(ps[:, 1 + j % 2, :], q_rot[:, j // 2, (j % 2) * P:(j % 2 + 1) * P], kt[:, kv, :],
                             start=True, stop=True).then_inc(scores, 1)

                def turn(j):
                    e.wait_ge(prob_v, 4 * n + j + 1)
                    e.wait_ge(probs_copied, 4 * n + j + 1)
                    for kc in range(4):
                        mm = e.transpose(ps[:, 3 + j % 2, kc * P:(kc + 1) * P], probs[:, j % 2, kc * P:(kc + 1) * P], ident)
                    mm.then_inc(probs_turned, 1)

                def values(h):
                    e.wait_ge(probs_copied, 4 * n + 2 * h + 2 + 2)
                    e.wait_ge(head_ready, 2 * n + h + 1)
                    for kc in range(4):
                        mm = e.matmul(ps[:, 5 + h, 0:TOK], v[:, kv, kc, :], probs_t[:, h, kc, :],
                                      start=(kc == 0), stop=(kc == 3))
                    mm.then_inc(head_out, 1)

                score(0)
                score(1)
                turn(0)
                score(2)
                turn(1)
                score(3)
                values(0)
                turn(2)
                turn(3)
                values(1)

            for kv in range(KV_HEADS):
                with e.Fori(0, 2) as pair:
                    pe_heads(kv, 2 * kv + pair, pair)
            e.wait_ge(head_ready, 2 + HEADS)
            pe_finish(e, M_OUT, FIN_ATT, 2)
            with e.Fori(0, 4) as i:
                pe_iter(e, T_OUT + i, alt, lambda j: (head_ready, 2 + HEADS))
            pe_finish(e, M_MLP0, FIN_OUT, 2)

            def mlp_q(layer, q_):
                T = (T_MLP0, T_MLP1)[layer] + 8 * q_
                h0 = 32 * layer + 8 * q_
                with e.Fori(0, 4) as i:
                    pe_iter(e, T + i, lat, lambda j: (norm_ready, (9, 17)[layer] + j))
                if layer == 0:
                    pe_finish(e, M_MLP0 + 8 * q_ + 4, FIN_MLP0 + 2 * q_, 1)
                with e.Fori(0, 4) as i:
                    pe_iter(e, T + 4 + i, alt, lambda j: (hidden_ready, h0 + 2 * j + 2))
                if layer == 0:
                    pe_finish(e, M_MLP0 + 8 * q_ + 8, FIN_MLP0 + 2 * q_ + 1, 1)

            e.wait_ge(mod_ready, FIN_OUT + 2)
            pe_stats(e, 2)
            with e.Fori(0, w_ff) as q_:
                mlp_q(0, q_)
            pe_stats(e, 3)
            with e.Fori(0, 4) as c:
                for k in range(3):
                    pe_iter(e, T_HY + 3 * c + k, lat, lambda j: (norm_ready, 13 + j))

                def turn(o, hf):
                    if o == 0:
                        e.wait_ge(tapped, 4 * (3 * c + 3))
                    else:
                        e.wait_ge(conv_v[hf], 6 * c + 3)
                    for tb in range(2):
                        for fb in range(2):
                            mm = e.transpose(ps[:, hf, tb * 256 + fb * P:tb * 256 + (fb + 1) * P],
                                             u[:, 0, 2 * hf + fb, tb * P:(tb + 1) * P], ident)
                    mm.then_inc(turned, 1)

                def spectrum(o, hf):
                    e.wait_ge(tok_ready, 2 * (2 * c + o) + hf + 1)
                    for f in range(4):
                        for kb in range(2):
                            mm = e.matmul(ps[:, 2 + 2 * hf + f // 2, (f % 2) * 256:(f % 2 + 1) * 256],
                                          fwd[:, kb, f * P:(f + 1) * P], z_tok[:, hf, kb, :],
                                          start=(kb == 0), stop=(kb == 1))
                    mm.then_inc(z_spec, 1)

                def invert(o, hf):
                    e.wait_ge(spec_v, 6 * (2 * (2 * c + o) + hf) + 6 + 6)
                    for fb in range(2):
                        for f in range(4):
                            mm = e.matmul(ps[:, 6 + hf, fb * TOK:(fb + 1) * TOK],
                                          y_spec[:, hf, f, fb * P:(fb + 1) * P], back[:, f, :],
                                          start=(f == 0), stop=(f == 3))
                    mm.then_inc(y_back, 1)

                turn(0, 0)
                turn(0, 1)
                e.wait_ge(in_fwd, 16)
                e.wait_ge(mod_ready, FIN_HY + c + 1)
                for o in range(2):
                    spectrum(o, 0)
                    if o == 1:
                        turn(1, 1)
                    spectrum(o, 1)
                    e.wait_ge(in_back, 16)
                    invert(o, 0)
                    invert(o, 1)
                    if o == 0:
                        turn(1, 0)
                pe_finish(e, M_HY + 4 * c + 4, FIN_HY + c, 1)
            with e.Fori(0, 4) as i:
                pe_iter(e, T_HOUT + i, alt, lambda j: (z_ready, 8))
            pe_finish(e, M_END, FIN_HOUT, 1)
            pe_stats(e, 4)
            with e.Fori(0, w_ff) as q_:
                mlp_q(1, q_)
            pe_stats(e, 5)

        @block.scalar
        def _(e):
            e.sem_inc(hi_ready, 8)
            e.sem_inc(lo_copied, 2)
            e.sem_inc(spec_copied, 2)
            e.sem_inc(exp_done, 2)
            e.sem_inc(probs_copied, 2)
            e.wait_ge(in_vecs, 16)
            e.activation(silu_e[:], vec("c", 0, 2 * KB), ACT.Exp, scale=-1.0).then_inc(silu_exp, 1)
            e.wait_ge(hid_v, 7)
            e.activation(hid_1[:], hid_a[:], ACT.Sin).then_inc(hid_sin, 1)
            e.wait_ge(hid_v, 14)
            e.activation(hid_2[:], hid_a[:], ACT.Sin).then_inc(hid_sin, 1)
            with e.Fori(0, 4) as c:
                for o in range(2):
                    e.wait_ge(spec_stored, 16 * (2 * c + o + 1))
                    for f in range(4):
                        e.wait_ge(spec_mm, 4 * (2 * c + o) + f + 1)
                        e.activation(spec[:, f], ps[:, 2 + f % 2, :], ACT.Copy).then_inc(spec_copied, 1)
                        if f == 0:
                            for b in range(4):
                                turned_taps = ps[:, 6 + b // 2, (b % 2) * TOK:(b % 2 + 1) * TOK]
                                e.activation(turned_taps, turned_taps, ACT.Square,
                                             accum_out=tap_sums[:, ds(o * KB + 4 * c + b, 1)])
                    e.wait_ge(spec_copied, 4 * (2 * c + o) + 4 + 2)
                    e.dma_start(spec_dram[ds(2 * c + o, 1)].rearrange("a p f c -> (a p) f c"), spec[:]
                                ).then_inc(spec_stored, 16)
                    if o == 0:
                        e.wait_ge(sq_summed, 2 * c + 2)
                        for k, (src, landed) in enumerate(((x, in_x), (xc, in_ctx))):
                            e.wait_ge(landed, 16 * (c + 1))
                            e.activation(sq[:, k], src[:, ds(4 * c, 4), :], ACT.Square).then_inc(squares, 1)
                e.activation(rows[:].rearrange("w (b n) -> w b n", b=2), ps[0:2, 4:6, :], ACT.Copy).then_inc(rows_copied, 1)
            act_root(e, 0, 2 * TOK, rn)
            act_root(e, 1, 32)
            e.wait_ge(spec_stored, 9 * 16)
            r = act_call(e, T_Q, 4, None, Queries, NORM_X)
            act_iter(e, T_KV, r, KeysValues(kt))
            act_iter(e, T_KV + 1, KeysValues(kt), KeysValues(vt))
            act_flush(e, T_KV + 1, KeysValues(vt))
            for h in range(2):
                e.wait_ge(psum_free, 2 * (T_KV + 2))
                e.activation(k_sq[:, 2 * h:2 * h + 2, :].rearrange("p a t -> p (a t)"), kt[:, 2 + h, :],
                             ACT.Square).then_inc(k_squared, 1)
            for hp in range(4):
                e.wait_ge(kq_sums, 1 if hp < 2 else hp)
                e.activation(k_sq[:, 2 * (hp % 2):2 * (hp % 2) + 2, :], q[:, A_HEADS + 2 * hp:A_HEADS + 2 * hp + 2, :],
                             ACT.Square).then_inc(k_squared, 1)
            for h in range(KV_HEADS):
                e.wait_ge(vt_turned, h + 1)
                e.activation(v[:, h].rearrange("p a d -> p (a d)"), ps[:, h, :], ACT.Copy).then_inc(v_ready, 1)
            act_root(e, 2, 8)
            act_root(e, 3, 16)

            def act_heads(kv, n, pair):
                def soft(j):
                    h = 4 * kv + 2 * pair + j // 2
                    e.wait_ge(row_max, 4 * n + j + 1)
                    e.wait_ge(probs_turned, 4 * n + j + 1)
                    m = sm[:, j % 2]
                    scale = 1.0 if kv < 2 else rs_q[:, ds(2 * (h - A_HEADS) + j % 2, 1)]
                    ins = e.activation(probs[:, j % 2, :], ps[:, 1 + j % 2, :], ACT.Exp, bias=m[:, 0:1], scale=scale,
                                       accum_out=m[:, 1:2])
                    if kv < 2:
                        ins = e.activation(m[:, 2:3], vec("sink", h), ACT.Exp, bias=m[:, 0:1])
                    ins.then_inc(exp_done, 1)

                def copy(j):
                    e.wait_ge(probs_turned, 4 * n + j + 1 + 2)
                    if j % 2 == 0:
                        e.wait_ge(head_out, 2 * n + j // 2 + 1)
                    e.activation(probs_t[:, j // 2, :, (j % 2) * P:(j % 2 + 1) * P],
                                 ps[:, 3 + j % 2, :].rearrange("p (k t) -> p k t", k=4), ACT.Copy).then_inc(probs_copied, 1)

                def head(h):
                    e.wait_ge(head_out, 2 * n + h + 1 + 2)
                    e.activation(alt[:, ds(4 * kv + 2 * pair + h, 1), 0:TOK], ps[:, 5 + h:6 + h, 0:TOK],
                                 ACT.Copy).then_inc(head_hi, 1)

                soft(0)
                soft(1)
                copy(0)
                soft(2)
                copy(1)
                soft(3)
                head(0)
                copy(2)
                copy(3)
                head(1)

            for kv in range(KV_HEADS):
                with e.Fori(0, 2) as pair:
                    act_heads(kv, 2 * kv + pair, pair)

            def mlp(layer, q_, prev):
                T = (T_MLP0, T_MLP1)[layer] + 8 * q_
                h0, n_out = 32 * layer + 8 * q_, (OUT_M0, OUT_M1)[layer] + 8 * q_
                norm = NORM_MLP[layer] if prev is None else None
                r = act_call(e, T, 4, prev, lambda i: Hidden(i, h0), norm)
                return act_call(e, T + 4, 4, r, lambda i: Gated((G2, G4)[layer], i, n_out))

            def mlps(layer):
                r = mlp(layer, 0, None)
                with e.Fori(1, w_ff) as q_:
                    mlp(layer, q_, Gated((G2, G4)[layer], 3, (OUT_M0, OUT_M1)[layer] + 8 * (q_ - 1)))
                T = (T_MLP0, T_MLP1)[layer]
                act_flush(e, T + 31, Gated((G2, G4)[layer], 3, (OUT_M0, OUT_M1)[layer] + 24))

            r = act_call(e, T_OUT, 4, None, lambda i: Gated(G1, i, OUT_0))
            act_flush(e, T_OUT + 3, r)
            act_stats(e, 2, x, (psum_free, 2 * T_MLP0))
            act_root(e, 4, TOK, rn)
            mlps(0)
            act_stats(e, 3, x, (psum_free, 2 * T_HY))
            act_root(e, 5, TOK, rn)
            for c in range(4):
                act_norm_hi(e, 3, lat, c)
            e.wait_ge(norm_ready, 16)
            e.dma_start(fwd[:], a["fwd"]).then_inc(in_fwd, 16)
            e.dma_start(back[:], a["back"]).then_inc(in_back, 16)
            with e.Fori(0, 4) as c:
                prev = None
                for k, part in enumerate((2, 0, 1)):
                    cur = ShortConv(k, part * KB + 4 * c, 6 * c + 2 * k)
                    act_iter(e, T_HY + 3 * c + k, prev, cur)
                    prev = cur
                act_flush(e, T_HY + 3 * c + 2, prev)
                for o in range(2):
                    for hf in range(2):
                        e.wait_ge(turned, 2 * (2 * c + o) + hf + 1)
                        e.activation(z_tok[:, hf].rearrange("p a n -> p (a n)"), ps[:, hf, :], ACT.Copy).then_inc(tok_ready, 1)
                for hf in range(2):
                    e.wait_ge(conv_v[hf], 6 * c + 6)
                    e.activation(alt[:, ds(4 * c + 2 * hf, 2), 0:TOK], u[:, 0, 2 * hf:2 * hf + 2], ACT.Copy).then_inc(z_hi, 1)
            e.wait_ge(gains, 4)
            r = act_call(e, T_HOUT, 4, None, lambda i: Gated(G3, i, OUT_H, bias=True))
            act_flush(e, T_HOUT + 3, r)
            act_stats(e, 4, x, (psum_free, 2 * T_MLP1))
            act_root(e, 6, TOK, rn)
            mlps(1)
            act_stats(e, 5, x, (psum_free, 2 * (T_MLP1 + 32)))
            act_root(e, 7, TOK, rn)

        @block.vector
        def _(e):
            e.sem_inc(split_ready, 8)
            e.sem_inc(psum_free, 2)
            e.sem_inc(slabs_used, 4)
            for j in range(START_RING):
                e.sem_inc(start_free[j], 1)
            e.sem_inc(mod_ready, 1)
            e.sem_inc(taps_ready, 4)
            e.sem_inc(sq_summed, 2)
            e.sem_inc(start_summed, 1)
            e.sem_inc(spec_stored, 16)
            e.sem_inc(q_v, 3)
            e.sem_inc(probs_turned, 2)
            e.sem_inc(head_ready, 2)
            e.sem_inc(head_out, 2)
            e.sem_inc(spec_v, 6)
            e.memset(ones[:], 1.0).then_inc(started, 1)
            e.wait_ge(silu_exp, 1)
            e.tensor_scalar(silu_e[:], silu_e[:], 1.0, None, ALU.add).then_inc(silu_v, 1)
            e.wait_ge(silu_v, 1)
            e.reciprocal(silu[:], silu_e[:]).then_inc(silu_v, 1)
            e.wait_ge(silu_v, 2)
            e.tensor_tensor(silu[:], silu[:], vec("c", 0, 2 * KB), ALU.mult).then_inc(silu_v, 1)

            def hidden_arg(n, b, fr):
                e.wait_ge(hid_mm, n + 1)
                e.tensor_scalar(hid_a[:], ps[0:HID, n, 0:TOK], b, fr, ALU.add, ALU.mult).then_inc(hid_v, 1)
                e.wait_ge(hid_v, 7 * n + 1)
                e.tensor_scalar(hid_k[:], hid_a[:], 1.0 / (2.0 * math.pi), MAGIC, ALU.mult, ALU.add).then_inc(hid_v, 1)
                e.wait_ge(hid_v, 7 * n + 2)
                e.tensor_scalar(hid_k[:], hid_k[:], MAGIC, None, ALU.subtract).then_inc(hid_v, 1)
                parts = [6.28125, 0.0019340515136718750]
                parts.append(2.0 * math.pi - sum(parts))
                for m, part in enumerate(parts):
                    e.wait_ge(hid_v, 7 * n + 3 + m)
                    e.scalar_tensor_tensor(hid_a[:], hid_k[:], -part, hid_a[:], ALU.mult, ALU.add).then_inc(hid_v, 1)
                e.wait_ge(hid_v, 7 * n + 6)
                e.tensor_scalar(hid_a[:], hid_a[:], 3.1415925, -3.1415925, ALU.min, ALU.max).then_inc(hid_v, 1)

            e.wait_ge(in_fw, 16)
            b1, fr1, b2, fr2 = (f_w[:, 2 * HID + n:2 * HID + n + 1] for n in range(4))
            hidden_arg(0, b1, fr1)
            hidden_arg(1, b2, fr2)
            with e.Fori(0, 2) as cc:
                for par in range(2):
                    c = 2 * cc + par
                    sums = (acc, acc_odd)[par]
                    mine = [j for j in range(16) if j not in PE_SLABS]
                    for r, j in enumerate(mine):
                        if r in (1, 6):
                            o = r // 6
                            e.wait_ge(taps_mm, 2 * c + o + 5)
                            e.wait_ge(in_decay[par], 16 * (cc + 1))
                            e.tensor_tensor(taps[:, o], ps[:, 0:2, :], decay[:, par], ALU.mult).then_inc(taps_ready, 1)
                        e.wait_ge(start_landed[j % START_RING], 16 * (2 * c + j // START_RING + 1))
                        s_ = start_slot(j)
                        if r == 0:
                            e.tensor_scalar(sums[:, 0], s_, silu[:, 0:1], None, ALU.mult).then_inc(acc_ready, 1)
                            e.tensor_scalar(sums[:, 1], s_, silu[:, KB:KB + 1], None,
                                            ALU.mult).then_inc(start_free[j % START_RING], 1)
                        else:
                            before = mine[r - 1]
                            e.wait_ge(acc_ready, len(mine) * c + r)
                            e.scalar_tensor_tensor(sums[:, 0], s_, silu[:, j:j + 1], sums[:, 0],
                                                   ALU.mult, ALU.add).then_inc(acc_ready, 1)
                            e.wait_ge(start_free[before % START_RING], 2 * c + before // START_RING + 2)
                            e.scalar_tensor_tensor(sums[:, 1], s_, silu[:, KB + j:KB + j + 1], sums[:, 1],
                                                   ALU.mult, ALU.add).then_inc(start_free[j % START_RING], 1)
                    for k in range(2):
                        e.wait_ge(squares, 2 * c + k + 1)
                        e.tensor_reduce(sum_sq[:, ds(c, 1), k * TOK:(k + 1) * TOK].rearrange("p a t -> p (a t)"),
                                        sq[:, k].rearrange("p k t -> p t k"), AX.X, ALU.add).then_inc(sq_summed, 1)
                    e.wait_ge(start_turned, c + 1)
                    for w in range(2):
                        ins = e.tensor_reduce(mod_part[:, w], ps[:, 4 + 2 * w:6 + 2 * w, :].rearrange(
                            "p a (b k) -> p (a b) k", k=P), AX.X, ALU.add)
                    ins.then_inc(silu_v, 1)
                    e.wait_ge(silu_v, 4 + c)
                    e.tensor_tensor(start_part[:, :, ds(half * c, half)], mod_part[:],
                                    ps[:, 0, 0:2 * half].rearrange("p (b w) -> p w b", w=2), ALU.add).then_inc(start_summed, 1)
            e.wait_ge(start_summed, 5)
            for w, dst in enumerate((mod, mod_ctx)):
                ins = e.tensor_tensor(dst[:, 0:2 * KB], start_part[:, w], vec("mod_b", 0, 2 * KB), ALU.add)
            ins.then_inc(mod_ready, 1)
            e.sem_inc(mod_summed, 1)
            dve_rsqrt(e, 0, ps[:, 1, :], 2 * TOK, 1.0 / D, EPS, rs_tok[:], (square_sums, 8), temps=rn)
            dve_rsqrt(e, 1, tap_sums[:], 32, 1.0, EPS, rs_filter[:], (rows_copied, 4))
            e.wait_ge(mod_ready, 2)
            dve_gain(e, 1, gain[:, 0:KB], mods(0, 1), vec("mix_g", 0, KB))
            dve_gain(e, 2, gain[:, KB:2 * KB], mod_ctx[:, KB:2 * KB], vec("mix_g", 0, KB))
            r = dve_call(e, T_Q, 4, None, Queries, SL_Q, None, NORM_X)
            dve_finish(e, FIN_Q, [mod_col(0, 4), mod_col(0, 5)])
            dve_iter(e, T_KV, r, KeysValues(kt), 0, SL_KV)
            dve_iter(e, T_KV + 1, KeysValues(kt), KeysValues(vt), 1, SL_KV)
            dve_flush(e, T_KV + 1, KeysValues(vt))
            e.wait_ge(in_rope, 16)
            e.wait_ge(in_const, 16)
            qn, kn = vec("q_norm"), vec("k_norm")
            e.tensor_scalar(cos_q[:], cos, qn, None, ALU.mult).then_inc(tables, 1)
            e.tensor_scalar(cos_k[:], cos, kn, None, ALU.mult).then_inc(tables, 1)
            e.tensor_scalar(swap_q[:], swap, qn, None, ALU.mult).then_inc(tables, 1)
            e.tensor_scalar(swap_k[:], swap, kn, None, ALU.mult).then_inc(tables, 1)
            e.tensor_scalar(neg_sink[:], vec("sink", 0, A_HEADS), -1.0, None, ALU.mult).then_inc(tables, 1)
            sin_b = sin.rearrange("p (a t) -> p a t", a=1).to_broadcast([P, 2, TOK])

            def rotate(dst, src, bank, table, done, n):
                tb_ = table.rearrange("p (a t) -> p a t", a=1).to_broadcast([P, 2, TOK])
                e.tensor_tensor(q_sin[:], ps[:, bank, :].rearrange("p (a t) -> p a t", a=2), sin_b, ALU.mult)
                e.tensor_tensor(dst, src, tb_, ALU.mult).then_inc(done, 1)
                e.wait_ge(done, n + 1)
                e.tensor_tensor(dst, dst, q_sin[:], ALU.add).then_inc(done, 1)
                e.wait_ge(done, n + 2)

            dve_finish(e, FIN_KV, [mod_col(0, 6)])
            e.wait_ge(k_swapped, 1)
            rotate(kt[:, 0:2, 0:TOK], kt[:, 0:2, 0:TOK], 4, cos, k_v, 0)
            dve_rsqrt(e, 2, ps[:, 6, 0:8], 8, 1.0 / HEAD, EPS, rs_k[:], (kq_sums, 1))
            e.wait_ge(k_swapped, 2)
            rotate(kt[:, 2:4, 0:TOK], kt[:, 2:4, 0:TOK], 5, cos_k[:], k_v, 2)
            dve_rsqrt(e, 3, ps[:, 6, 16:32], 16, 1.0 / HEAD, EPS * QSCALE * QSCALE, rs_q[:], (kq_sums, 5))
            e.wait_ge(rs_v, 6 * 3 + 6)
            e.tensor_scalar(rs_q[:], rs_q[:], QSCALE, None, ALU.mult).then_inc(k_v, 1)
            e.wait_ge(k_spread, 1)
            for h in range(2):
                kl, kc = kt[:, 2 + h, 0:TOK], kt[:, 2 + h, TOK:2 * TOK]
                e.tensor_tensor(kl, kl, ps[:, h, 0:TOK], ALU.mult)
                ins = e.scalar_tensor_tensor(kc, kc, kn, ps[:, h, TOK:2 * TOK], ALU.mult, ALU.mult)
            ins.then_inc(k_v, 1)
            e.wait_ge(k_v, 6)
            e.memset(acc[:], 0.0).then_inc(acc_ready, 1)
            e.wait_ge(acc_ready, 4 * (16 - len(PE_SLABS)) + 1)

            def dve_heads(kv, n, pair):
                e.wait_ge(q_swapped, n + 1)
                e.wait_ge(scores, 4 * n + 1)
                hq = q[:, ds(4 * kv + 2 * pair, 2), :]
                tb_ = (cos if kv < 2 else cos_q[:]).rearrange("p (a t) -> p a t", a=1).to_broadcast([P, 2, TOK])
                e.tensor_tensor(q_sin[:], ps[:, 0, :].rearrange("p (a t) -> p a t", a=2), sin_b, ALU.mult).then_inc(q_v, 1)
                e.tensor_tensor(q_rot[:], hq, tb_, ALU.mult).then_inc(q_v, 1)
                e.wait_ge(q_v, 3 * n + 5)
                e.tensor_tensor(q_rot[:], q_rot[:], q_sin[:], ALU.add).then_inc(q_v, 1)

                def peak(j):
                    h = 4 * kv + 2 * pair + j // 2
                    e.wait_ge(scores, 4 * n + j + 2)
                    m, s_ = sm[:, j % 2], ps[:, 1 + j % 2, :]
                    if kv < 2:
                        part = s_[:, (1 - j % 2) * P:(2 - j % 2) * P]
                        e.tensor_tensor(part, part, mask[:, j % 2, :], ALU.add).then_inc(scored_v, 1)
                        e.wait_ge(scored_v, 2 * (4 * n + j) + 1)
                    else:
                        e.sem_inc(scored_v, 1)
                    e.tensor_reduce(m[:, 3:4], s_, AX.X, ALU.max, negate=True).then_inc(scored_v, 1)
                    e.wait_ge(scored_v, 2 * (4 * n + j) + 2)
                    if kv < 2:
                        e.tensor_tensor(m[:, 0:1], m[:, 3:4], neg_sink[:, ds(h, 1)], ALU.min).then_inc(row_max, 1)
                    else:
                        e.tensor_tensor(m[:, 0:1], m[:, 3:4], rs_q[:, ds(2 * (h - A_HEADS) + j % 2, 1)],
                                        ALU.mult).then_inc(row_max, 1)

                def weigh(j):
                    m = sm[:, j % 2]
                    e.wait_ge(exp_done, 4 * n + j + 1 + 2)
                    if kv < 2:
                        e.tensor_tensor(m[:, 1:2], m[:, 1:2], m[:, 2:3], ALU.add).then_inc(scored_w, 1)
                        e.wait_ge(scored_w, 2 * (4 * n + j) + 1)
                    else:
                        e.sem_inc(scored_w, 1)
                    e.reciprocal(m[:, 3:4], m[:, 1:2]).then_inc(scored_w, 1)
                    e.wait_ge(scored_w, 2 * (4 * n + j) + 2)
                    e.tensor_scalar(probs[:, j % 2, :], probs[:, j % 2, :], m[:, 3:4], None, ALU.mult).then_inc(prob_v, 1)

                def head(h):
                    e.wait_ge(head_hi, 2 * n + h + 1)
                    at = ds(4 * kv + 2 * pair + h, 1)
                    e.tensor_tensor(alt[:, at, TOK:2 * TOK], ps[:, 5 + h:6 + h, 0:TOK], alt[:, at, 0:TOK].bitcast(F32),
                                    ALU.subtract).then_inc(head_ready, 1)

                def fold(j):
                    for slot, m4, kb, ac, _, _ in Slabs(0, [8, 9], 4, M_ATT + n, 2 * n).each(0, j, 1):
                        e.wait_ge(slab_landed[slot], 16 * (m4 + 1))
                        e.wait_ge(slabs_used, 4 * m4 + slot + 3)
                        e.scalar_tensor_tensor(acc[:, ac], slab[:, slot], silu[:, ds(kb, 1)], acc[:, ac],
                                               ALU.mult, ALU.add).then_inc(slabs_used, 1)

                peak(0)
                peak(1)
                weigh(0)
                fold(0)
                peak(2)
                weigh(1)
                fold(1)
                peak(3)
                weigh(2)
                fold(2)
                head(0)
                weigh(3)
                fold(3)
                head(1)

            for kv in range(KV_HEADS):
                with e.Fori(0, 2) as pair:
                    dve_heads(kv, 2 * kv + pair, pair)
            r = dve_call(e, T_OUT, 4, None, lambda i: Gated(G1, i, OUT_0), SL_OUT,
                         (FIN_ATT, [mod_col(0, 8), mod_col(0, 9)]))
            dve_flush(e, T_OUT + 3, r)
            dve_finish(e, FIN_OUT, [mod_col(0, 7), mod_col(0, 10)])
            dve_rsqrt(e, 4, ps[:, 6, 0:TOK], TOK, 1.0 / D, EPS, rs_tok[:, 0:TOK], (square_sums, 12), temps=rn)
            e.wait_ge(mod_ready, FIN_OUT + 2)
            dve_gain(e, 3, gain[:, 0:KB], mods(0, 4), vec("mlp_g", 0, KB))

            def mlp(layer, q_, prev, sl_up, sl_down, fin_before, fin_mid):
                T = (T_MLP0, T_MLP1)[layer] + 8 * q_
                h0, n_out = 32 * layer + 8 * q_, (OUT_M0, OUT_M1)[layer] + 8 * q_
                norm = NORM_MLP[layer] if prev is None else None
                r = dve_call(e, T, 4, prev, lambda i: Hidden(i, h0), sl_up, fin_before, norm)
                return dve_call(e, T + 4, 4, r, lambda i: Gated((G2, G4)[layer], i, n_out), sl_down, fin_mid)

            mlp(0, 0, None, SL_UP0, sl_mlp0(0, 1), None, (FIN_MLP0, [mod_col(0, 11)]))
            with e.Fori(1, w_ff) as q_:
                mlp(0, q_, Gated(G2, 3, OUT_M0 + 8 * (q_ - 1)), sl_mlp0(q_, 0), sl_mlp0(q_, 1),
                    (FIN_MLP0 + 2 * q_ - 1, [mod_col(1, 2 * q_ - 2)]), (FIN_MLP0 + 2 * q_, [mod_col(1, 2 * q_ - 1)]))
            dve_flush(e, T_MLP0 + 31, Gated(G2, 3, OUT_M0 + 24))
            dve_finish(e, FIN_MLP0 + 7, [mod_col(1, 6)])
            dve_rsqrt(e, 5, ps[:, 6, 0:TOK], TOK, 1.0 / D, EPS, rs_tok[:, 0:TOK], (square_sums, 16), temps=rn)
            e.wait_ge(mod_ready, FIN_HY + 1)
            e.tensor_tensor(gate_bias[:], mods(1, 2), vec("b_out", 0, KB), ALU.mult)
            dve_gain(e, 4, gain[:, 0:KB], mods(1, 1), vec("mix_g", KB, KB))
            for c in range(4):
                dve_normalise(e, *NORM_HY[:4], c)
                if c:
                    dve_norm_lo(e, 3, lat, c - 1)
            dve_norm_lo(e, 3, lat, 3)
            with e.Fori(0, 4) as c:
                prev = None
                for k, part in enumerate((2, 0, 1)):
                    cur = ShortConv(k, part * KB + 4 * c, 6 * c + 2 * k)
                    dve_iter(e, T_HY + 3 * c + k, prev, cur, k, sl_hy(c))
                    prev = cur
                dve_flush(e, T_HY + 3 * c + 2, prev)

                def multiply(o, hf):
                    m = 2 * (2 * c + o) + hf
                    e.wait_ge(z_spec, m + 1)
                    e.wait_ge(h_landed, 16 * (2 * c + o + 1))
                    zr, zi = (ps[:, 2 + 2 * hf + n, :].rearrange("p (f n) -> p f n", f=2) for n in range(2))
                    hr, hi = (h_spec[:, 2 * n:2 * n + 2, hf * 256:(hf + 1) * 256] for n in range(2))
                    yr, yi, tmp = y_spec[:, hf, 0:2], y_spec[:, hf, 2:4], z_tok[:, hf]
                    n0 = 6 * m + 6
                    e.tensor_tensor(yr, zr, hr, ALU.mult).then_inc(spec_v, 1)
                    e.tensor_tensor(tmp, zi, hi, ALU.mult).then_inc(spec_v, 1)
                    e.wait_ge(spec_v, n0 + 2)
                    e.tensor_tensor(yr, yr, tmp, ALU.subtract).then_inc(spec_v, 1)
                    e.tensor_tensor(yi, zr, hi, ALU.mult).then_inc(spec_v, 1)
                    e.wait_ge(spec_v, n0 + 4)
                    e.tensor_tensor(tmp, zi, hr, ALU.mult).then_inc(spec_v, 1)
                    e.wait_ge(spec_v, n0 + 5)
                    e.tensor_tensor(yi, yi, tmp, ALU.add).then_inc(spec_v, 1)

                def skip(o, hf):
                    for fb in range(2 * hf, 2 * hf + 2):
                        ins = e.tensor_scalar(u[:, 0, fb], u[:, 0, fb], vec("skip", o * KB + 4 * c + fb), None, ALU.mult)
                    ins.then_inc(conv_v[hf], 1)

                def combine(o, hf):
                    e.wait_ge(conv_v[hf], 6 * c + 3 * o + 1)
                    e.wait_ge(y_back, 2 * (2 * c + o) + hf + 1)
                    for fb in range(2):
                        z = u[:, 0, 2 * hf + fb]
                        ins = e.scalar_tensor_tensor(z, ps[:, 6 + hf, fb * TOK:(fb + 1) * TOK],
                                                     rs_filter[:, ds(o * KB + 4 * c + 2 * hf + fb, 1)], z,
                                                     ALU.mult, ALU.add)
                    ins.then_inc(conv_v[hf], 1)
                    e.wait_ge(conv_v[hf], 6 * c + 3 * o + 2)
                    z = u[:, 0, 2 * hf:2 * hf + 2]
                    e.tensor_tensor(z, z, u[:, 1 + o, 2 * hf:2 * hf + 2], ALU.mult).then_inc(conv_v[hf], 1)

                dve_slabs(e, sl_hy(c), 3, 0, 1)
                for o in range(2):
                    multiply(o, 0)
                    skip(o, 0)
                    multiply(o, 1)
                    skip(o, 1)
                    if o == 0:
                        dve_slabs(e, sl_hy(c), 3, 1, 1)
                    combine(o, 0)
                    if o == 0:
                        dve_slabs(e, sl_hy(c), 3, 2, 1)
                    combine(o, 1)
                    if o == 0:
                        dve_slabs(e, sl_hy(c), 3, 3, 1)
                for hf in range(2):
                    e.wait_ge(z_hi, 2 * c + hf + 1)
                    e.tensor_tensor(alt[:, ds(4 * c + 2 * hf, 2), TOK:2 * TOK], u[:, 0, 2 * hf:2 * hf + 2],
                                    alt[:, ds(4 * c + 2 * hf, 2), 0:TOK].bitcast(F32),
                                    ALU.subtract).then_inc(z_ready, 1)
                dve_finish(e, FIN_HY + c, [mod_col(1, 7 + c)])
            r = dve_call(e, T_HOUT, 4, None, lambda i: Gated(G3, i, OUT_H), SL_HOUT)
            dve_flush(e, T_HOUT + 3, r)
            dve_finish(e, FIN_HOUT, [mod_col(1, 11)])
            dve_rsqrt(e, 6, ps[:, 6, 0:TOK], TOK, 1.0 / D, EPS, rs_tok[:, 0:TOK], (square_sums, 20), temps=rn)
            e.wait_ge(mod_ready, FIN_HOUT + 2)
            dve_gain(e, 5, gain[:, 0:KB], mods(1, 4), vec("mlp_g", KB, KB))
            mlp(1, 0, None, None, None, None, None)
            with e.Fori(1, w_ff) as q_:
                mlp(1, q_, Gated(G4, 3, OUT_M1 + 8 * (q_ - 1)), None, None, None, None)
            dve_flush(e, T_MLP1 + 31, Gated(G4, 3, OUT_M1 + 24))
            dve_rsqrt(e, 7, ps[:, 6, 0:TOK], TOK, 1.0 / D, EPS, rs_tok[:, 0:TOK], (square_sums, 24), temps=rn)
            for c in range(4):
                if c >= 2:
                    e.wait_ge(stored[c - 2], 16)
                dve_normalise(e, 5, x, vec("final_g", 0, KB), None, c)


def columns(v):
    return v.reshape(-1, P).T


def kernel(**inputs):
    import concourse.bacc as bacc
    from concourse.bass_utils import run_bass_kernel_spmd

    i = {k: np.asarray(v_) for k, v_ in inputs.items()}
    arrays = constants()
    feature_major = lambda t: np.ascontiguousarray(t.T.reshape(KB, P, TOK).transpose(1, 0, 2))
    arrays["x"] = feature_major(i["x"][0])
    arrays["ctx"] = feature_major(i["ctx"][0])
    arrays["vecs"] = np.ascontiguousarray(np.concatenate([
        columns(i["c"]), columns(i["c_ctx"]), columns(i["mod_b"]), columns(i["norm_mix_g"]), columns(i["norm_mlp_g"]),
        columns(i["final_g"]), columns(i["hy_b_in"]), columns(i["hy_conv_w"]), columns(i["hy_conv_b"]),
        columns(i["hy_skip"]), columns(i["hy_b_out"]), columns(i["attn_q_norm"]), columns(i["attn_k_norm"]),
        np.broadcast_to(i["attn_sink"], (P, A_HEADS))], 1))
    f_w1 = np.zeros((HID, HID), np.float32)
    f_w1[:FILTER_EMB] = i["hy_f_w1"][0]
    arrays["f_w"] = np.ascontiguousarray(np.concatenate([
        f_w1, i["hy_f_w2"][0], i["hy_f_b1"].T, i["hy_f_freq1"].T, i["hy_f_b2"].T, i["hy_f_freq2"].T], 1))
    arrays["w3"] = i["hy_f_w3"][0].reshape(HID, 2, D)
    arrays["mod_w"] = i["mod_w"]
    for name in ("attn_w_in", "attn_w_out", "hy_w_in", "hy_w_out"):
        arrays[name] = i[name][0]
    for layer in range(2):
        arrays[f"mlp_w1_{layer}"] = i["mlp_w1"][layer]
        arrays[f"mlp_w2_{layer}"] = i["mlp_w2"][layer]
    nc = bacc.Bacc("TRN2", target_bir_lowering=False, num_devices=1)
    a = {k: nc.dram_tensor(f"in_{k}", v_.shape, F32, kind="ExternalInput").ap() for k, v_ in arrays.items()}
    a["y"] = nc.dram_tensor("out_y", (P, KB, TOK), F32, kind="ExternalOutput").ap()
    build(nc, a)
    r = run_bass_kernel_spmd(nc, [{f"in_{k}": v_ for k, v_ in arrays.items()}], core_ids=[0])
    y = r.results[0]["out_y"]
    return np.ascontiguousarray(y.transpose(1, 0, 2).reshape(D, TOK).T)[None]
```

```python
import math
from contextlib import ExitStack

import numpy as np

import concourse.bass as bass
from concourse import mybir

P = 128
D = 2048
TOK = 256
KB = D // P
D_FF = 4 * D
GRID_W = 64
HEAD = 128
THETA = 10000.0
WINDOW = 128
EPS = 1e-6
QSCALE = HEAD ** -0.5
HEADS = 16
A_HEADS = 8
KV_HEADS = 4
KV_COL = HEADS * HEAD
FILTER_EMB = 33
HID = 64
TARGET = 1e-2
MAX_DECAY = math.log(TARGET) / 0.3
MIN_DECAY = math.log(TARGET) / 1.5
NFREQ = 256
N_MOD = 6

UNIT_KB = 4
UNIT_COLS = 256
SLAB = 1024
RING = 4
PE_SLABS = (1, 4, 7, 10, 12, 14)
START_RING = 8
MAGIC = 1.5 * 2.0 ** 23

F32 = mybir.dt.float32
F32R = mybir.dt.float32r
ACT = mybir.ActivationFunctionType
ALU = mybir.AluOpType
AX = mybir.AxisListType
ds = bass.ds

VECS = {}
_at = 0
for _name, _n in (("c", KB), ("c_ctx", KB), ("mod_b", 2 * N_MOD * KB), ("mix_g", 2 * KB), ("mlp_g", 2 * KB),
                  ("final_g", KB), ("b_in", 3 * KB), ("conv_w", 9 * KB), ("conv_b", 3 * KB), ("skip", 2 * KB),
                  ("b_out", KB), ("q_norm", 1), ("k_norm", 1), ("sink", HEADS)):
    VECS[_name] = _at
    _at += _n
N_VECS = _at
IDENT, SWAP, N_CONST = 0, P, 2 * P
COS, SIN, MASK, N_ROPE = 0, TOK, 2 * TOK, 2 * TOK + KV_HEADS * 2 * P
NO_SINK = -1e30


def constants():
    f32 = np.float32
    ident = np.eye(P, dtype=f32)
    swap = np.zeros((P, P), f32)
    for m in range(P):
        swap[m ^ 32, m] = 1.0
    tok = np.arange(TOK)
    inv = THETA ** (-np.arange(0, HEAD // 2, 2, dtype=f32) / f32(HEAD // 2))
    ang = np.empty((P, TOK), f32)
    for m in range(P):
        pos = (tok // GRID_W if m < HEAD // 2 else tok % GRID_W).astype(f32)
        ang[m] = pos * f32(inv[m % 32])
    sign = np.where((np.arange(P) // 32) % 2 == 0, -1.0, 1.0)[:, None]
    q = np.arange(P)[:, None]
    k = np.arange(P)[None]
    mask = np.stack([np.where(k + P - q <= WINDOW, 0.0, -1e30), np.where(q + P - k <= WINDOW, 0.0, -1e30)], 1)
    mask = np.concatenate([mask, mask, 0.0 * mask, 0.0 * mask], 1)
    const = np.concatenate([ident, swap], 1)
    rope = np.concatenate([np.cos(ang), np.sin(ang) * sign, mask.reshape(P, KV_HEADS * 2 * P)], 1)
    t = np.arange(TOK)[:, None]
    f = np.arange(NFREQ)[None] + 0.5
    th = np.pi * f * t / TOK
    fwd = np.concatenate([np.cos(th), -np.sin(th)], 1).reshape(2, P, 2 * NFREQ).transpose(1, 0, 2)
    n = np.arange(TOK)[None] + TOK // 2
    ph = np.pi * (np.arange(NFREQ)[:, None] + 0.5) * n / TOK
    back = np.concatenate([np.cos(ph), -np.sin(ph)], 0) / TOK
    back = back.reshape(4, P, TOK).transpose(1, 0, 2)
    bands = (FILTER_EMB - 1) // 2
    w = (2.0 * np.pi * np.arange(TOK) / TOK)[:, None]
    fb = np.linspace(1e-4, bands - 1, bands)[None]
    feats = np.concatenate([np.linspace(0.0, 1.0, TOK)[:, None], np.cos(fb * w), -np.sin(fb * w)], 1).T
    offs = np.abs(np.arange(TOK) - TOK // 2) * (2.0 / TOK)
    deltas = np.abs(np.linspace(MIN_DECAY, MAX_DECAY, D))
    decay = np.exp(-offs[:, None] * deltas[None]).reshape(2, P, 4, 512).transpose(2, 1, 0, 3)
    return {k: np.ascontiguousarray(v, dtype=f32) for k, v in
            (("const", const), ("rope", rope), ("fwd", fwd), ("back", back), ("feats", feats), ("decay", decay))}


def build(nc, a):
    stack = ExitStack()

    def sem(name):
        return stack.enter_context(nc.semaphore(name))

    def sb(name, shape, dt=F32, scope=None):
        return (scope or stack).enter_context(nc.sbuf_tensor(name, shape, dt))

    with stack:
        x = sb("x", [P, KB, TOK])
        vecs = sb("vecs", [P, N_VECS])
        const = sb("const", [P, N_CONST])
        mod = sb("mod", [P, 2 * N_MOD * KB])
        mod_ctx = sb("mod_ctx", [P, 2 * KB])
        silu = sb("silu", [P, 2 * KB])
        silu_e = sb("silu_e", [P, 2 * KB])
        gain = sb("gain", [P, 2 * KB])
        gate_bias = sb("gate_bias", [P, KB])
        ones = sb("ones", [P, P])
        mod_part = sb("mod_part", [P, 2, SLAB // P])
        neg_sink = sb("neg_sink", [P, HEADS])
        sm = sb("sm", [P, 2, 4])
        rs_a, rs_r = sb("rs_a", [P, 32]), sb("rs_r", [P, 32])
        rs_y, rs_t = sb("rs_y", [P, 32]), sb("rs_t", [P, 32])
        tap_sums = sb("tap_sums", [P, 2 * KB])
        rs_k, rs_q = sb("rs_k", [P, 8]), sb("rs_q", [P, 2 * HEADS])
        rs_filter = sb("rs_filter", [P, 32])
        raw = sb("raw", [P, RING, UNIT_KB, UNIT_COLS])
        w_hi = sb("w_hi", [P, RING, UNIT_KB, UNIT_COLS], F32R)
        w_lo = sb("w_lo", [P, RING, UNIT_KB, UNIT_COLS], F32R)
        slab = sb("slab", [P, RING, SLAB])
        acc = sb("acc", [P, 2, SLAB])
        lo_sum = sb("lo_sum", [P, 2, 2, TOK])
        sum_sb = sb("sum_sb", [P, 2, 2, TOK])
        with ExitStack() as early:
            s = early
            hid_a, hid_k, hid_1 = (sb(n, [HID, TOK], scope=s) for n in ("hid_a", "hid_k", "hid_1"))
            hid_2 = sb("hid_2", [HID, TOK], scope=s)
            f_w = sb("f_w", [HID, 2 * HID + 4], scope=s)
            feats = sb("feats", [FILTER_EMB, TOK], scope=s)
            w3 = sb("w3", [HID, 2, 2, 512], scope=s)
            decay = sb("decay", [P, 2, 2, 512], scope=s)
            taps = sb("taps", [P, 2, 2, 512], scope=s)
            start_part = sb("start_part", [P, 2, 4 * SLAB // P], scope=s)
            spec = sb("spec", [P, 4, 512], scope=s)
            acc_odd = sb("acc_odd", [P, 2, SLAB], scope=s)
            rows = sb("rows", [2, SLAB], scope=s)
            sum_sq = sb("sum_sq", [P, 4, 2 * TOK], scope=s)
            fwd0 = sb("fwd0", [P, 2, 2 * NFREQ], scope=s)
        with ExitStack() as mid:
            s = mid
            probs = sb("probs", [P, 4, 512], scope=s)
            probs_t = sb("probs_t", [P, 2, 4, TOK], scope=s)
            k_sq = probs_t[:, 0]
            q_rot = sb("q_rot", [P, 2, 2, TOK], scope=s)
            q_sin = sb("q_sin", [P, 2, TOK], scope=s)
            v = sb("v", [P, KV_HEADS, 4, HEAD], scope=s)
            v_now = sb("v_now", [P, 4, HEAD], scope=s)
        lat = sb("lat", [P, KB, 2 * TOK], F32R)
        alt = sb("alt", [P, KB, 2 * TOK], F32R)
        with ExitStack() as s:
            hm = sb("hm", [P, 2, 4, TOK], scope=s)
            sq = sb("sq", [P, 2, 4, TOK], scope=s)
            rn = [sb(n, [P, 2 * TOK], scope=s) for n in ("rn_a", "rn_r", "rn_y")]
            rn.append(rn[1])
            xc = sb("xc", [P, KB, TOK], scope=s)
            rs_tok = sb("rs_tok", [P, 2 * TOK], scope=s)
        with ExitStack() as s:
            rope = sb("rope", [P, N_ROPE], scope=s)
            q = sb("q", [P, HEADS, TOK], scope=s)
            kt = sb("kt", [P, KV_HEADS, 2 * TOK], scope=s)
            vt = sb("vt", [P, KV_HEADS, 2 * TOK], scope=s)
        with ExitStack() as s:
            u = sb("u", [P, 3, 4, TOK], scope=s)
            z_tok = sb("z_tok", [P, 2, 2, 256], scope=s)
            h_spec = sb("h_spec", [P, 4, 512], scope=s)
            y_spec = sb("y_spec", [P, 2, 4, 256], scope=s)
            fwd = sb("fwd", [P, 2, 2 * NFREQ], scope=s)
            back = sb("back", [P, 4, TOK], scope=s)
        ps = stack.enter_context(nc.psum_tensor("ps", [P, 8, 512], F32))
        acc_pool = vt[:, 0:2, :].rearrange("p h t -> p (h t)")
        ps_all = ps[:].rearrange("p b n -> p (b n)")
        spec_dram = nc.dram_tensor("spec_dram", (8, P, 4, 512), F32, kind="Internal").ap()

        ident = const[:, IDENT:IDENT + P]
        swap = const[:, SWAP:SWAP + P]
        cos, sin = rope[:, COS:COS + TOK], rope[:, SIN:SIN + TOK]
        mask = rope[:, MASK:N_ROPE].rearrange("p (h b k) -> p h b k", h=KV_HEADS, b=2)

        def vec(name, i=0, n=1):
            return vecs[:, ds(VECS[name] + i, n)]

        in_const, in_vecs, in_x, in_ctx = sem("in_const"), sem("in_vecs"), sem("in_x"), sem("in_ctx")
        in_fw, in_feats, in_fwd0 = sem("in_fw"), sem("in_feats"), sem("in_fwd0")
        in_rope = sem("in_rope")
        in_fwd, in_back = sem("in_fwd"), sem("in_back")
        in_w3 = [sem("in_w3_0"), sem("in_w3_1")]
        in_decay = [sem("in_decay_0"), sem("in_decay_1")]
        unit_landed = [sem(f"unit_landed{j}") for j in range(RING)]
        slab_landed = [sem(f"slab_landed{j}") for j in range(RING)]
        hi_ready, split_ready = sem("hi_ready"), sem("split_ready")
        units_done = sem("units_done")
        lo_copied, psum_free = sem("lo_copied"), sem("psum_free")
        slabs_used, acc_ready = sem("slabs_used"), sem("acc_ready")
        pool_landed = [sem(f"pool_landed{j}") for j in range(RING)]
        pool_used, pool_scaled = sem("pool_used"), sem("pool_scaled")
        start_landed = [sem(f"start_landed{j}") for j in range(START_RING)]
        start_free = [sem(f"start_free{j}") for j in range(START_RING)]
        rows_copied, start_turned, start_summed = sem("rows_copied"), sem("start_turned"), sem("start_summed")
        sq_summed, stat_summed = sem("sq_summed"), sem("stat_summed")
        mod_cols, mod_ready, mod_summed = sem("mod_cols"), sem("mod_ready"), sem("mod_summed")
        started = sem("started")
        silu_exp, silu_v = sem("silu_exp"), sem("silu_v")
        squares, square_sums = sem("squares"), sem("square_sums")
        rs_v, rs_root = sem("rs_v"), sem("rs_root")
        gains, normed, norm_hi, norm_ready = sem("gains"), sem("normed"), sem("norm_hi"), sem("norm_ready")
        x_hi_added = sem("x_hi_added")
        squared, hidden_hi, hidden_ready = sem("squared"), sem("hidden_hi"), sem("hidden_ready")
        centred, tapped = sem("centred"), sem("tapped")
        hid_mm, hid_v, hid_sin = sem("hid_mm"), sem("hid_v"), sem("hid_sin")
        taps_mm, taps_ready = sem("taps_mm"), sem("taps_ready")
        spec_mm, spec_copied, spec_stored = sem("spec_mm"), sem("spec_copied"), sem("spec_stored")
        vt_turned, v_ready = sem("vt_turned"), sem("v_ready")
        k_swapped, k_v, k_squared, kq_sums, k_spread = (sem(n) for n in (
            "k_swapped", "k_v", "k_squared", "kq_sums", "k_spread"))
        q_swapped, q_v = sem("q_swapped"), sem("q_v")
        scores, scored_v, row_max, exp_done, prob_v, probs_turned, probs_copied = (sem(n) for n in (
            "scores", "scored_v", "row_max", "exp_done", "prob_v", "probs_turned", "probs_copied"))
        scored_w, recip_v, v_copied = sem("scored_w"), sem("recip_v"), sem("v_copied")
        b_scaled = sem("b_scaled")
        head_out, head_hi, head_ready = sem("head_out"), sem("head_hi"), sem("head_ready")
        h_landed = sem("h_landed")
        turned, tok_ready, z_spec, spec_v, y_back = (sem(n) for n in (
            "turned", "tok_ready", "z_spec", "spec_v", "y_back"))
        conv_v = [sem("conv_v0"), sem("conv_v1")]
        z_hi, z_ready = sem("z_hi"), sem("z_ready")
        stored = [sem(f"stored{c}") for c in range(4)]

        T_Q, T_KV, T_OUT, T_MLP0 = 1, 5, 7, 11
        T_HY = T_MLP0 + 32
        T_HOUT = T_HY + 12
        T_MLP1 = T_HOUT + 4
        M_Q = 0
        M_KV, M_ATT = M_Q + 4, M_Q + 12
        M_OUT = M_ATT + 8
        M_MLP0 = M_OUT + 4
        M_HY = M_MLP0 + 32
        M_HOUT = M_HY + 16
        M_END = M_HOUT + 4
        FIN_Q, FIN_KV, FIN_ATT, FIN_OUT, FIN_MLP0 = 1, 2, 3, 4, 5
        FIN_HY = FIN_MLP0 + 8
        FIN_HOUT = FIN_HY + 4
        half = SLAB // P

        class Slabs:

            def __init__(self, layer, halves, per, m4, first_kb=0):
                self.layer, self.halves, self.per, self.m4, self.kb0 = layer, halves, per, m4, first_kb

            def each(self, i, j0, n):
                nh = len(self.halves)
                for j in range(j0, j0 + n):
                    kb = self.kb0 + i * (self.per // nh) + j // nh
                    first = isinstance(kb, int) and kb == 0
                    yield j % RING, self.m4 + i * (self.per // RING) + j // RING, kb, j % nh, self.halves[j % nh], first

        def sp_slabs(e, sl, i, j0, n):
            for slot, m4, kb, _, h, _ in sl.each(i, j0, n):
                e.wait_ge(slabs_used, 4 * m4 + slot + 1)
                e.dma_start(slab[:, slot, :], a["mod_w"][sl.layer, ds(kb * P, P), ds(h * SLAB, SLAB)]
                            ).then_inc(slab_landed[slot], 16)

        def sp_iter(e, T, w, row, col, i, sl):
            for n in range(8):
                e.wait_ge(split_ready, 8 * T + n - 3)
                src = w[ds(row + (n % 4) * UNIT_KB * P, UNIT_KB * P), ds(col + (n // 4) * UNIT_COLS, UNIT_COLS)]
                e.dma_start(raw[:, n % RING], src.rearrange("(k p) n -> p k n", p=P)
                            ).then_inc(unit_landed[n % RING], 16)
                if sl and n >= 4:
                    r = sl.per // 4
                    sp_slabs(e, sl, i, (n - 4) * r, r)

        def pool_slot(j):
            return raw[:, j % RING].rearrange("p k n -> p (k n)")

        def start_slot(j):
            j %= START_RING
            return slab[:, j] if j < RING else raw[:, j - RING].rearrange("p k n -> p (k n)")

        def sp_call(e, T, n, w, row, col, sl):
            with e.Fori(0, n) as i:
                sp_iter(e, T + i, w, row, col + i * 512, i, sl)

        def pe_iter(e, T, tile, ready, ctx_tile=None, stats=None, before=None):
            for n in range(8):
                if before:
                    before(n)
                if stats is not None and n == 7:
                    pe_stats(e, *stats)
                g = n // 4
                e.wait_ge(split_ready, 8 * T + n + 1)
                if ready:
                    e.wait_ge(*ready(n % 4))
                if n % 4 == 0:
                    e.wait_ge(psum_free, 2 * T + g - 1)
                for kk in range(UNIT_KB):
                    kb = (n % 4) * UNIT_KB + kk
                    for fb in range(2):
                        cols = slice(fb * P, (fb + 1) * P)
                        for t, bank in ((tile, 2 * g + fb), (ctx_tile, 4 + 2 * g + fb)):
                            if t is None:
                                continue
                            e.matmul(ps[:, bank, :], w_hi[:, n % RING, kk, cols], t[:, kb, :],
                                     start=(kb == 0), stop=False)
                            mm = e.matmul(ps[:, bank, 0:TOK], w_lo[:, n % RING, kk, cols], t[:, kb, 0:TOK],
                                          start=False, stop=(kb == KB - 1))
                mm.then_inc(units_done, 1)

        def pe_call(e, T, n, tile, ready, k=None):
            pe_iter(e, T, tile, ready(0))
            with e.Fori(1, n) as i:
                pe_iter(e, T + i, tile, ready(i), None, None if k is None else (k, i - 1))

        def pe_finish(e, sl_count, fin, n_acc, second=None):
            e.wait_ge(slabs_used, 4 * sl_count + 4)
            e.wait_ge(mod_ready, fin + 1)
            for h in range(n_acc):
                for b in range(half):
                    mm = e.transpose(ps[:, 4 * (1 - h) + b // 4, (b % 4) * P:(b % 4 + 1) * P],
                                     (acc[:, h] if h == 0 or second is None else second)[:, b * P:(b + 1) * P], ident)
            mm.then_inc(mod_cols, 1)

        def act_split(e, T, n):
            e.wait_ge(unit_landed[n % RING], 16 * (2 * T + n // 4 - 1))
            e.wait_ge(units_done, 8 * T + n - 3)
            e.activation(w_hi[:, n % RING], raw[:, n % RING], ACT.Copy).then_inc(hi_ready, 1)

        def dve_split(e, T, n):
            e.wait_ge(hi_ready, 8 * T + n + 1)
            e.tensor_tensor(w_lo[:, n % RING], raw[:, n % RING], w_hi[:, n % RING].bitcast(F32),
                            ALU.subtract).then_inc(split_ready, 1)

        def dve_slabs(e, sl, i, j0, n):
            for slot, m4, kb, ac, _, first in sl.each(i, j0, n):
                e.wait_ge(slab_landed[slot], 16 * (m4 + 1))
                scale = silu[:, ds(kb, 1)]
                if first:
                    e.tensor_scalar(acc[:, ac], slab[:, slot], scale, None, ALU.mult).then_inc(slabs_used, 1)
                else:
                    e.wait_ge(slabs_used, 4 * m4 + slot + 5 - len(sl.halves))
                    e.scalar_tensor_tensor(acc[:, ac], slab[:, slot], scale, acc[:, ac],
                                           ALU.mult, ALU.add).then_inc(slabs_used, 1)

        def dve_finish(e, fin, dests):
            e.wait_ge(mod_cols, fin + 1)
            for h in range(len(dests)):
                ins = e.tensor_reduce(mod_part[:, h], ps[:, 4 * (1 - h):4 * (1 - h) + 2, :].rearrange("p a (b k) -> p (a b) k", k=P),
                                      AX.X, ALU.add)
            ins.then_inc(mod_summed, 1)
            e.wait_ge(mod_summed, fin + 1)
            for h, at in enumerate(dests):
                ins = e.tensor_tensor(mod[:, ds(at, half)], mod_part[:, h], vec("mod_b", at, half), ALU.add)
            ins.then_inc(mod_ready, 1)
            e.wait_ge(mod_ready, fin + 2)

        class Readout:

            def bank(self, g, part):
                return ps[:, 2 * g:2 * g + 2, part * TOK:(part + 1) * TOK]

            def act_wait(self, e, T, g):
                e.wait_ge(units_done, 8 * T + 4 * g + 4)
                e.wait_ge(psum_free, 2 * T + g - 1)

            def act_head(self, e, T, g):
                self.act_wait(e, T, g)
                e.activation(lo_sum[:, g], self.bank(g, 1), ACT.Copy).then_inc(lo_copied, 1)

            def act_tail(self, e, T, g):
                pass

            def dve_tail(self, e, T, g):
                pass

        class Queries(Readout):
            def __init__(self, i):
                self.i = i

            def act_head(self, e, T, g):
                self.act_wait(e, T, g)
                e.activation(lo_sum[:, g], self.bank(g, 1), ACT.Copy, scale=QSCALE).then_inc(lo_copied, 1)

            def dve_head(self, e, T, g):
                e.wait_ge(lo_copied, 2 * T + g + 1)
                e.scalar_tensor_tensor(q[:, ds(4 * self.i + 2 * g, 2), :], self.bank(g, 0), QSCALE, lo_sum[:, g],
                                       ALU.mult, ALU.add).then_inc(psum_free, 1)

        class KeysValues(Readout):
            def __init__(self, dst):
                self.dst = dst

            def ctx_bank(self, g, part):
                return ps[:, 4 + 2 * g:6 + 2 * g, part * TOK:(part + 1) * TOK]

            def act_head(self, e, T, g):
                self.act_wait(e, T, g)
                e.activation(lo_sum[:, g], self.bank(g, 1), ACT.Copy)
                e.activation(sum_sb[:, g], self.ctx_bank(g, 1), ACT.Copy).then_inc(lo_copied, 1)

            def dve_head(self, e, T, g):
                e.wait_ge(lo_copied, 2 * T + g + 1)
                d = self.dst[:, 2 * g:2 * g + 2, :]
                e.tensor_tensor(d[:, :, 0:TOK], self.bank(g, 0), lo_sum[:, g], ALU.add)
                e.tensor_tensor(d[:, :, TOK:2 * TOK], self.ctx_bank(g, 0), sum_sb[:, g],
                                ALU.add).then_inc(psum_free, 1)

        class Gated(Readout):

            def __init__(self, gate, i, n_out, bias=None):
                self.gate, self.i, self.n_out, self.bias = gate, i, n_out, bias
                self.ready = {G1: FIN_KV, G2: FIN_MLP0, G3: FIN_HY - 1, G4: FIN_HOUT}[gate] + 2

            def act_head(self, e, T, g):
                self.act_wait(e, T, g)
                e.wait_ge(mod_ready, self.ready)
                for fb in range(2):
                    f = 4 * self.i + 2 * g + fb
                    bias = gate_bias[:, ds(f, 1)] if self.bias else 0.0
                    ins = e.activation(lo_sum[:, g, fb], ps[:, 2 * g + fb, TOK:2 * TOK], ACT.Identity,
                                       bias=bias, scale=mod[:, ds(self.gate + f, 1)])
                ins.then_inc(lo_copied, 1)

            def dve_head(self, e, T, g):
                e.wait_ge(lo_copied, 2 * T + g + 1)
                for fb in range(2):
                    f = 4 * self.i + 2 * g + fb
                    xf = x[:, ds(f, 1), :]
                    ins = e.scalar_tensor_tensor(xf, ps[:, 2 * g + fb:2 * g + fb + 1, 0:TOK],
                                                 mod[:, ds(self.gate + f, 1)], xf, ALU.mult, ALU.add)
                ins.then_inc(x_hi_added, 1)
                e.wait_ge(x_hi_added, self.n_out + 2 * self.i + g + 1)
                xg = x[:, ds(4 * self.i + 2 * g, 2), :]
                e.tensor_tensor(xg, xg, lo_sum[:, g], ALU.add).then_inc(psum_free, 1)

        class Hidden(Readout):

            def __init__(self, i, n_hid):
                self.i, self.n = i, n_hid

            def dve_head(self, e, T, g):
                e.wait_ge(lo_copied, 2 * T + g + 1)
                e.tensor_tensor(sum_sb[:, g], self.bank(g, 0), lo_sum[:, g], ALU.add).then_inc(psum_free, 1)
                e.wait_ge(psum_free, 2 * T + g + 1)
                e.scalar_tensor_tensor(sum_sb[:, g], sum_sb[:, g], 0.0, sum_sb[:, g],
                                       ALU.max, ALU.mult).then_inc(squared, 1)

            def act_tail(self, e, T, g):
                e.wait_ge(squared, self.n + 2 * self.i + g + 1)
                e.activation(alt[:, ds(4 * self.i + 2 * g, 2), 0:TOK], sum_sb[:, g], ACT.Copy).then_inc(hidden_hi, 1)

            def dve_tail(self, e, T, g):
                e.wait_ge(hidden_hi, self.n + 2 * self.i + g + 1)
                f = ds(4 * self.i + 2 * g, 2)
                e.tensor_tensor(alt[:, f, TOK:2 * TOK], sum_sb[:, g], alt[:, f, 0:TOK].bitcast(F32),
                                ALU.subtract).then_inc(hidden_ready, 1)

        class ShortConv(Readout):

            def __init__(self, part, col, n):
                self.part, self.col, self.n = part, col, n

            def act_head(self, e, T, g):
                self.act_wait(e, T, g)
                for fb in range(2):
                    ins = e.activation(lo_sum[:, g, fb], ps[:, 2 * g + fb, TOK:2 * TOK], ACT.Identity,
                                       bias=vec("b_in", self.col + 2 * g + fb))
                ins.then_inc(lo_copied, 1)

            def dve_head(self, e, T, g):
                e.wait_ge(lo_copied, 2 * T + g + 1)
                e.tensor_tensor(sum_sb[:, g], self.bank(g, 0), lo_sum[:, g], ALU.add).then_inc(psum_free, 1)

            def act_tail(self, e, T, g):
                e.wait_ge(psum_free, 2 * T + g + 1)
                for fb in range(2):
                    f = self.col + 2 * g + fb
                    ins = e.activation(u[:, self.part, 2 * g + fb], sum_sb[:, g, fb], ACT.Identity,
                                       bias=vec("conv_b", f), scale=vec("conv_w", 3 * KB + f))
                ins.then_inc(centred, 1)

            def dve_tail(self, e, T, g):
                e.wait_ge(centred, self.n + g + 1)
                for side in range(2):
                    for fb in range(2):
                        o = u[:, self.part, 2 * g + fb]
                        to = o[:, 1:TOK] if side == 0 else o[:, 0:TOK - 1]
                        fr = sum_sb[:, g, fb, 0:TOK - 1] if side == 0 else sum_sb[:, g, fb, 1:TOK]
                        ins = e.scalar_tensor_tensor(to, fr, vec("conv_w", 6 * KB * side + self.col + 2 * g + fb), to,
                                                     ALU.mult, ALU.add)
                    ins.then_inc(tapped, 1)
                    e.wait_ge(tapped, 2 * (self.n + g) + side + 1)

        def act_iter(e, T, prev, cur, norm=None, ctx_chunk=None, stats=None, after_unit=None):
            for n in range(8):
                act_split(e, T, n)
                if norm and n < 4:
                    act_norm_hi(e, norm[0], norm[4], n)
                if ctx_chunk is not None and n == 5:
                    act_norm_hi(e, 1, alt, ctx_chunk)
                if stats is not None and n == 5:
                    act_stats(e, *stats, T - 1)
                if after_unit:
                    after_unit(n)
                if n == 0 and prev:
                    prev.act_tail(e, T - 1, 0)
                if n == 3 and prev:
                    prev.act_head(e, T - 1, 1)
                if n == 4 and prev:
                    prev.act_tail(e, T - 1, 1)
                if n == 7:
                    cur.act_head(e, T, 0)

        def act_flush(e, T, r):
            r.act_tail(e, T, 0)
            r.act_head(e, T, 1)
            r.act_tail(e, T, 1)

        def dve_iter(e, T, prev, cur, i, sl, finish=None, norm=None, ctx_chunk=None, after_unit=None):
            for n in range(8):
                if norm and n < 4:
                    dve_normalise(e, *norm[:4], n)
                if ctx_chunk is not None and n == 5:
                    dve_normalise(e, *NORM_CTX[:4], ctx_chunk)
                dve_split(e, T, n)
                if norm and n < 4:
                    dve_norm_lo(e, norm[0], norm[4], n)
                if ctx_chunk is not None and n == 5:
                    dve_norm_lo(e, 1, alt, ctx_chunk)
                if after_unit:
                    after_unit(n)
                if n == 0 and prev:
                    prev.dve_tail(e, T - 1, 0)
                if n == 3:
                    if finish:
                        dve_finish(e, *finish)
                    if prev:
                        prev.dve_head(e, T - 1, 1)
                if n == 4 and prev:
                    prev.dve_tail(e, T - 1, 1)
                if n >= 4 and sl:
                    r = sl.per // 4
                    dve_slabs(e, sl, i, (n - 4) * r, r)
                if n == 7:
                    cur.dve_head(e, T, 0)

        def dve_flush(e, T, r):
            r.dve_tail(e, T, 0)
            r.dve_head(e, T, 1)
            r.dve_tail(e, T, 1)

        def act_call(e, T, n, prev, kind, norm=None, k=None):
            with_ctx = norm is not None and norm[0] == 0
            act_iter(e, T, prev, kind(0), norm, 0 if with_ctx else None)
            with e.Fori(1, n) as i:
                act_iter(e, T + i, kind(i - 1), kind(i), None, i if with_ctx else None,
                         None if k is None else (k, i - 1))
            return kind(n - 1)

        def dve_call(e, T, n, prev, kind, sl, finish=None, norm=None):
            with_ctx = norm is not None and norm[0] == 0
            dve_iter(e, T, prev, kind(0), 0, sl, finish, norm, 0 if with_ctx else None)
            with e.Fori(1, n) as i:
                dve_iter(e, T + i, kind(i - 1), kind(i), i, sl, None, None, i if with_ctx else None)
            return kind(n - 1)

        def act_stats(e, k, c, T):
            e.wait_ge(psum_free, 2 * T + 2)
            e.wait_ge(square_sums, 4 * k + c)
            e.activation(sq[:, 0], x[:, ds(4 * c, 4), :], ACT.Square).then_inc(squares, 1)

        def pe_stats(e, k, c):
            e.wait_ge(squares, 4 * k + c + 1)
            for kk in range(4):
                mm = e.matmul(ps_all[:, ds(6 * 512 + TOK * c, TOK)], ones[:], sq[:, 0, kk, :],
                              start=(kk == 0), stop=(kk == 3))
            mm.then_inc(square_sums, 1)

        def dve_stats(e, k, r):
            e.wait_ge(square_sums, 4 * k + 4)
            sums = rn[0][:, 0:TOK]
            e.tensor_reduce(sums, ps[:, 6:8, :].rearrange("p a (b t) -> p t (a b)", b=2), AX.X,
                            ALU.add).then_inc(stat_summed, 1)
            e.wait_ge(stat_summed, k - 1)
            dve_rsqrt(e, r, sums, TOK, 1.0 / D, EPS, rs_tok[:, 0:TOK], temps=rn)

        def dve_rsqrt(e, r, sums, n, scale, eps, out, *waits, temps=(rs_a, rs_r, rs_y, rs_t)):
            for w in waits:
                e.wait_ge(*w)
            A, R, Y, Tm = (t[:, 0:n] for t in temps)
            e.tensor_scalar(A, sums, scale, eps, ALU.mult, ALU.add).then_inc(rs_v, 1)
            e.wait_ge(rs_v, 6 * r + 1)
            e.reciprocal(R, A).then_inc(rs_v, 1)
            e.wait_ge(rs_root, r + 1)
            e.tensor_tensor(Tm, Y, Y, ALU.mult).then_inc(rs_v, 1)
            e.wait_ge(rs_v, 6 * r + 3)
            e.tensor_tensor(Tm, Tm, A, ALU.mult).then_inc(rs_v, 1)
            e.wait_ge(rs_v, 6 * r + 4)
            e.tensor_scalar(Tm, Tm, -0.5, 1.5, ALU.mult, ALU.add).then_inc(rs_v, 1)
            e.wait_ge(rs_v, 6 * r + 5)
            e.tensor_tensor(out, Y, Tm, ALU.mult).then_inc(rs_v, 1)
            e.wait_ge(rs_v, 6 * r + 6)

        def act_root(e, r, n, temps=(rs_a, rs_r, rs_y, rs_t)):
            e.wait_ge(rs_v, 6 * r + 2)
            e.activation(temps[2][:, 0:n], temps[1][:, 0:n], ACT.Sqrt).then_inc(rs_root, 1)

        def factors(k):
            at = TOK * (k == 1)
            return rs_tok[:, at:at + TOK].rearrange("p (a t) -> p a t", a=1).to_broadcast([P, 4, TOK])

        def norm_part(k, c):
            return hm[:, 0 if k == 1 else c % 2]

        def dve_normalise(e, k, src, gains_ap, shift_ap, c):
            h = norm_part(k, c)
            if k == 1:
                e.wait_ge(norm_ready, 4 + c)
            elif c >= 2 and shift_ap is not None:
                e.wait_ge(norm_ready, 4 * k + c - 1)
            e.tensor_tensor(h, src[:, ds(4 * c, 4), :], factors(k),
                            ALU.mult).then_inc(normed, 1)
            e.wait_ge(normed, 8 * k + 2 * c + 1)
            for kk in range(4):
                kb = ds(4 * c + kk, 1)
                if shift_ap is None:
                    ins = e.tensor_scalar(h[:, kk], h[:, kk], gains_ap[:, kb], None, ALU.mult)
                else:
                    ins = e.tensor_scalar(h[:, kk], h[:, kk], gains_ap[:, kb], shift_ap[:, kb],
                                          ALU.mult, ALU.add)
            ins.then_inc(normed, 1)

        def dve_norm_lo(e, k, dst, c):
            e.wait_ge(norm_hi, 4 * k + c + 1)
            e.tensor_tensor(dst[:, ds(4 * c, 4), TOK:2 * TOK], norm_part(k, c),
                            dst[:, ds(4 * c, 4), 0:TOK].bitcast(F32), ALU.subtract).then_inc(norm_ready, 1)

        def act_norm_hi(e, k, dst, c):
            e.wait_ge(normed, 8 * k + 2 * c + 2)
            e.activation(dst[:, ds(4 * c, 4), 0:TOK], norm_part(k, c), ACT.Copy).then_inc(norm_hi, 1)

        def dve_gain(e, n, dst, scale_cols, g):
            e.scalar_tensor_tensor(dst, scale_cols, 1.0, g, ALU.add, ALU.mult).then_inc(gains, 1)
            e.wait_ge(gains, n)

        def mods(layer, s_):
            return mod[:, (layer * N_MOD + s_) * KB:(layer * N_MOD + s_ + 1) * KB]

        NORM_X = (0, x, gain[:, 0:KB], mods(0, 0), lat)
        NORM_CTX = (1, xc, gain[:, KB:2 * KB], mod_ctx[:, 0:KB], alt)
        NORM_MLP = ((2, x, gain[:, 0:KB], mods(0, 3), lat), (4, x, gain[:, 0:KB], mods(1, 3), lat))
        NORM_HY = (3, x, gain[:, 0:KB], mods(1, 0), lat)

        def after(n, k):
            return not isinstance(n, int) or n >= k

        def all_steps(e, step):
            for i in range(8):
                step(0, i)
            with e.Fori(1, KV_HEADS - 1) as kv:
                for i in range(8):
                    step(kv, i)
            for i in range(13):
                step(KV_HEADS - 1, i, True)

        SL_Q = Slabs(0, [4], 4, M_Q)
        SL_KV = Slabs(0, [5, 6], 16, M_KV)
        SL_ATT = Slabs(0, [8, 9], 8, M_ATT)
        POOL_HALF = 10
        SL_OUT = Slabs(0, [7], 4, M_OUT)
        SL_UP0 = Slabs(0, [11], 4, M_MLP0)

        def sl_mlp0(q_, down):
            return Slabs(1, [2 * q_ - 1 + down], 4, M_MLP0 + 8 * q_ + 4 * down)

        def sl_hy(c):
            return Slabs(1, [7 + c], 4, M_HY + 4 * c)

        SL_HOUT = Slabs(1, [11], 4, M_HOUT)
        HB = SLAB // P

        def mod_col(layer, half_):
            return layer * N_MOD * KB + half_ * HB

        G1, G2, G3, G4 = (2 * KB, 5 * KB, 8 * KB, 11 * KB)
        OUT_0, OUT_M0, OUT_H, OUT_M1 = 0, 8, 40, 48
        w_ff = D_FF // D

        block = stack.enter_context(nc.Block())

        @block.sync
        def _(e):
            e.dma_start(vecs[:], a["vecs"]).then_inc(in_vecs, 16)
            e.dma_start(f_w[:, :], a["f_w"]).then_inc(in_fw, 16)
            e.dma_start(feats[:], a["feats"]).then_inc(in_feats, 16)
            e.dma_start(const[:], a["const"]).then_inc(in_const, 16)
            e.dma_start(fwd0[:], a["fwd"]).then_inc(in_fwd0, 16)
            e.wait_ge(started, 1)
            with e.Fori(0, 2) as cc:
                for par in range(2):
                    c = 2 * cc + par
                    for j in range(16):
                        e.wait_ge(start_free[j % START_RING], 2 * c + j // START_RING + 1)
                        e.dma_start(start_slot(j), a["mod_w"][0, j * P:(j + 1) * P, ds(c * SLAB, SLAB)]
                                    ).then_inc(start_landed[j % START_RING], 16)
                        if j == 1:
                            e.wait_ge(taps_mm, 2 * c + 2)
                            e.dma_start(w3[:, par], a["w3"][:, :, ds(512 * c, 512)]).then_inc(in_w3[par], 16)
                            e.wait_ge(taps_ready, 2 * c + 2)
                            e.dma_start(decay[:, par], a["decay"][ds(c, 1)].rearrange("a p t n -> (a p) t n")
                                        ).then_inc(in_decay[par], 16)
                        if j in (4, 7):
                            name, dst, signal = (("x", x, in_x), ("ctx", xc, in_ctx))[j // 7]
                            e.dma_start(dst[:, ds(4 * c, 4), :], a[name][:, ds(4 * c, 4), :]).then_inc(signal, 16)
            for j in range(START_RING):
                e.wait_ge(start_free[j], 4 * 2 + 1)
            sp_call(e, T_Q, 4, a["attn_w_in"], 0, 0, SL_Q)
            e.wait_ge(norm_ready, 8)
            e.dma_start(rope[:], a["rope"]).then_inc(in_rope, 16)
            sp_call(e, T_KV, 2, a["attn_w_in"], 0, KV_COL, SL_KV)
            e.wait_ge(split_ready, 8 * (T_KV + 2))
            with e.Fori(0, KV_HEADS) as kv:
                for j in range(RING):
                    sp_slabs(e, SL_ATT, kv, 2 * j, 2)
                    e.wait_ge(pool_used, 4 * kv + j + 1)
                    e.dma_start(pool_slot(j), a["mod_w"][0, ds((4 * kv + j) * P, P), POOL_HALF * SLAB:(POOL_HALF + 1) * SLAB]
                                ).then_inc(pool_landed[j], 16)
            e.wait_ge(pool_used, 4 + KB)
            sp_call(e, T_OUT, 4, a["attn_w_out"], 0, 0, SL_OUT)

            def mlp(layer, T, q_, sl_up, sl_down):
                sp_call(e, T, 4, a[f"mlp_w1_{layer}"], 0, q_ * D, sl_up)
                sp_call(e, T + 4, 4, a[f"mlp_w2_{layer}"], q_ * D, 0, sl_down)

            mlp(0, T_MLP0, 0, SL_UP0, sl_mlp0(0, 1))
            with e.Fori(1, w_ff) as q_:
                mlp(0, T_MLP0 + 8 * q_, q_, sl_mlp0(q_, 0), sl_mlp0(q_, 1))
            e.wait_ge(spec_stored, 9 * 16)

            def sp_filter(s_):
                e.wait_ge(spec_v, 12 * s_ + 6)
                e.dma_start(h_spec[:], spec_dram[ds(s_, 1)].rearrange("a p f c -> (a p) f c")).then_inc(h_landed, 16)

            with e.Fori(0, 4) as c:
                for k, part in enumerate((2, 0, 1)):
                    if k == 2:
                        sp_filter(2 * c)
                    sp_iter(e, T_HY + 3 * c + k, a["hy_w_in"], 0, (c + part * 4) * 512, k, sl_hy(c))
                sp_slabs(e, sl_hy(c), 3, 0, 4)
                sp_filter(2 * c + 1)
            sp_call(e, T_HOUT, 4, a["hy_w_out"], 0, 0, SL_HOUT)
            mlp(1, T_MLP1, 0, None, None)
            with e.Fori(1, w_ff) as q_:
                mlp(1, T_MLP1 + 8 * q_, q_, None, None)
            for c in range(4):
                e.wait_ge(normed, 8 * 5 + 2 * c + 2)
                e.dma_start(a["y"][:, 4 * c:4 * c + 4, :], hm[:, c % 2]).then_inc(stored[c], 16)
            for c in range(4):
                e.wait_ge(stored[c], 16)

        @block.tensor
        def _(e):
            e.sem_inc(units_done, 8)
            e.sem_inc(taps_mm, 4)
            e.sem_inc(mod_cols, 1)
            e.wait_ge(started, 1)
            e.wait_ge(in_fw, 16)
            e.wait_ge(in_feats, 16)
            e.matmul(ps[0:HID, 0, 0:TOK], f_w[0:FILTER_EMB, 0:HID], feats[:], start=True, stop=True).then_inc(hid_mm, 1)
            e.wait_ge(hid_sin, 1)
            e.matmul(ps[0:HID, 1, 0:TOK], f_w[:, HID:2 * HID], hid_1[:], start=True, stop=True).then_inc(hid_mm, 1)
            e.wait_ge(hid_sin, 2)
            e.wait_ge(silu_v, 3)
            e.wait_ge(in_fwd0, 16)
            e.wait_ge(in_const, 16)

            def pe_slab(c, r):
                j = PE_SLABS[r]
                e.wait_ge(start_landed[j % START_RING], 16 * (2 * c + j // START_RING + 1))
                pair = silu[:].rearrange("p (w k) -> p w k", w=2)[:, :, j]
                for b in range(2):
                    mm = e.matmul(ps[0:2, 4 + b, :], pair, start_slot(j)[:, b * 512:(b + 1) * 512],
                                  start=(r == 0), stop=(r == len(PE_SLABS) - 1))
                mm.then_inc(start_free[j % START_RING], 1)

            with e.Fori(0, 2) as cc:
                for par in range(2):
                    c = 2 * cc + par
                    for o in range(2):
                        if o == 0:
                            e.wait_ge(start_summed, c + 1)
                        pe_slab(c, 3 * o)
                        if o == 0:
                            e.wait_ge(in_w3[par], 16 * (cc + 1))
                        e.wait_ge(taps_ready, 2 * c + o + 4)
                        for tb in range(2):
                            mm = e.matmul(ps[:, tb, :], hid_2[:, tb * P:(tb + 1) * P], w3[:, par, o, :],
                                          start=True, stop=True)
                        mm.then_inc(taps_mm, 1)
                        pe_slab(c, 3 * o + 1)
                        if o == 1:
                            pe_slab(c, 5)
                        e.wait_ge(taps_ready, 2 * c + o + 5)
                        e.wait_ge(spec_copied, 4 * (2 * c + o) + 2)
                        for b in range(4):
                            for tb in range(2):
                                e.transpose(ps[:, 6 + b // 2, (b % 2) * TOK + tb * P:(b % 2) * TOK + (tb + 1) * P],
                                            taps[:, o, tb, b * P:(b + 1) * P], ident)
                        for f in range(4):
                            e.wait_ge(spec_copied, 4 * (2 * c + o) + f + 1)
                            for kb in range(2):
                                mm = e.matmul(ps[:, 2 + f % 2, :], fwd0[:, kb, f * P:(f + 1) * P], taps[:, o, kb, :],
                                              start=(kb == 0), stop=(kb == 1))
                            mm.then_inc(spec_mm, 1)
                        if o == 0:
                            pe_slab(c, 2)
                    e.wait_ge(rows_copied, c + 1)
                    e.wait_ge(start_free[15 % START_RING], 2 * c + 3)
                    for w in range(2):
                        for b in range(half):
                            e.transpose(ps[:, 4 + 2 * w + b // 4, (b % 4) * P:(b % 4 + 1) * P],
                                        (acc, acc_odd)[par][:, w, b * P:(b + 1) * P], ident)
                    for b in range(half):
                        mm = e.transpose(ps[:, 0, 2 * b:2 * b + 2], rows[:, b * P:(b + 1) * P], ident[0:2, 0:2])
                    mm.then_inc(start_turned, 1)
            e.wait_ge(sq_summed, 10)
            for c in range(4):
                mm = e.matmul(ps[:, 1, :], ones[:], sum_sq[:, c, :], start=(c == 0), stop=(c == 3))
            mm.then_inc(square_sums, 8)
            e.wait_ge(start_summed, 5)
            with e.Fori(0, 4) as i:
                pe_iter(e, T_Q + i, lat, lambda j: (norm_ready, 1 + j))
            pe_finish(e, M_KV, FIN_Q, 1)
            e.wait_ge(mod_ready, FIN_Q + 2)
            with e.Fori(0, 2) as i:
                pe_iter(e, T_KV + i, lat, lambda j: (norm_ready, 5 + j), alt)
            e.wait_ge(psum_free, 2 * (T_KV + 2))
            pe_finish(e, M_ATT, FIN_KV, 2)
            e.wait_ge(mod_ready, FIN_KV + 2)
            for h in range(KV_HEADS):
                for tb in range(4):
                    mm = e.transpose(ps[:, h, tb * P:(tb + 1) * P], vt[:, h, tb * P:(tb + 1) * P], ident)
                mm.then_inc(vt_turned, 1)
            for pr in range(2):
                e.wait_ge(b_scaled, 1 + pr)
                for h in range(2):
                    mm = e.matmul(ps[:, 4 + pr, h * TOK:(h + 1) * TOK], swap,
                                  kt[:, 2 * pr + h, 0:TOK], start=True, stop=True)
                mm.then_inc(k_swapped, 1)
            for h in range(2):
                for c in range(4):
                    e.wait_ge(k_squared, h + 1)
                    tb = (h * 4 + c) % 8
                    mm = e.matmul(ps[:, 6, tb:tb + 1], k_sq[:, 2 * h + c // 2, (c % 2) * P:(c % 2 + 1) * P],
                                  ones[:, 0:1], start=True, stop=True)
            mm.then_inc(kq_sums, 1)
            for hp in range(4):
                e.wait_ge(k_squared, 3 + hp)
                if hp == 0:
                    e.wait_ge(rs_v, 6 * 2 + 1)
                for h in range(2):
                    for tb in range(2):
                        col = (2 * hp + h) * 2 + tb
                        mm = e.matmul(ps[:, 6, 16 + col:17 + col], k_sq[:, 2 * (hp % 2) + h, tb * P:(tb + 1) * P],
                                      ones[:, 0:1], start=True, stop=True)
                mm.then_inc(kq_sums, 1)
            e.wait_ge(rs_v, 6 * 2 + 6)
            e.wait_ge(v_ready, 4)
            for h in range(2):
                for c in range(4):
                    mm = e.matmul(ps[:, h, c * P:(c + 1) * P], rs_k[:, 4 * h + c:4 * h + c + 1].to_broadcast([P, P]),
                                  ident, start=True, stop=True)
            mm.then_inc(k_spread, 1)
            e.wait_ge(k_v, 6)

            def swap_pair(pair):
                if not isinstance(pair, int) or pair:
                    e.wait_ge(q_v, 3 * pair)
                e.matmul(ps[:, 0, :], swap, q[:, ds(2 * pair, 2), :], start=True, stop=True).then_inc(q_swapped, 1)

            def pe_step(kv, i, last=False):
                n = 8 * kv + i
                if i < 8:
                    if i % 4 == 0:
                        e.wait_ge(q_v, 3 * (2 * kv + i // 4) + 3)
                    if after(n, 2):
                        e.wait_ge(exp_done, n - 1)
                    e.matmul(ps[:, 1 + i % 2, :], q_rot[:, i // 4, i // 2 % 2, (i % 2) * P:(i % 2 + 1) * P],
                             kt[:, ds(kv, 1), :], start=True, stop=True).then_inc(scores, 1)
                    if i == 1:
                        swap_pair(2 * kv + 1)
                    if i == 5 and not last:
                        swap_pair(2 * kv + 2)
                if after(n, 3) and i < 11:
                    e.wait_ge(prob_v, n - 2)
                    if after(n, 5):
                        e.wait_ge(probs_copied, n - 4)
                    for kc in range(4):
                        mm = e.transpose(ps[:, 3 + (i + 1) % 2, kc * P:(kc + 1) * P],
                                         probs[:, (i - 3) % 4, kc * P:(kc + 1) * P], ident)
                    mm.then_inc(probs_turned, 1)
                if after(n, 5) and i % 2 == 1:
                    head = 4 * kv + (i - 5) // 2
                    if i == 5:
                        e.wait_ge(v_copied, kv + 1)
                    e.wait_ge(probs_copied, n - 3)
                    e.wait_ge(head_ready, head + 1)
                    at = (i - 5) // 2 % 2
                    for kc in range(4):
                        mm = e.matmul(ps[:, 5 + at, 0:TOK], v_now[:, kc, :], probs_t[:, at, kc, :],
                                      start=(kc == 0), stop=(kc == 3))
                    mm.then_inc(head_out, 1)

            swap_pair(0)
            all_steps(e, pe_step)
            e.wait_ge(head_ready, 2 + HEADS)
            pe_finish(e, M_OUT, FIN_ATT, 2)
            e.wait_ge(mod_ready, FIN_ATT + 2)
            pe_call(e, T_OUT, 4, alt, lambda i: lambda j: (head_ready, 2 + HEADS), 2)
            e.wait_ge(psum_free, 2 * T_MLP0 - 1)
            e.wait_ge(pool_used, 4 + KB)
            pe_finish(e, M_MLP0, FIN_OUT, 2, acc_pool)
            pe_stats(e, 2, 3)

            def mlp_q(layer, q_, k=None):
                T = (T_MLP0, T_MLP1)[layer] + 8 * q_
                h0 = 32 * layer + 8 * q_
                with e.Fori(0, 4) as i:
                    pe_iter(e, T + i, lat, lambda j: (norm_ready, (9, 17)[layer] + j))
                if layer == 0:
                    pe_finish(e, M_MLP0 + 8 * q_ + 4, FIN_MLP0 + 2 * q_, 1)
                pe_call(e, T + 4, 4, alt, lambda i: lambda j: (hidden_ready, h0 + 2 * j + 2), k)
                if k is not None:
                    pe_stats(e, k, 3)
                if layer == 0:
                    pe_finish(e, M_MLP0 + 8 * q_ + 8, FIN_MLP0 + 2 * q_ + 1, 1)

            e.wait_ge(mod_ready, FIN_OUT + 2)
            with e.Fori(0, w_ff - 1) as q_:
                mlp_q(0, q_)
            mlp_q(0, w_ff - 1, 3)
            with e.Fori(0, 4) as c:

                def turn(o, hf):
                    if o == 0:
                        e.wait_ge(tapped, 4 * (3 * c + 1))
                        e.wait_ge(mod_ready, FIN_HY + c + 1)
                    else:
                        e.wait_ge(psum_free, 2 * (T_HY + 3 * c + 3))
                        e.wait_ge(conv_v[hf], 6 * c + 3 + 1)
                    for tb in range(2):
                        for fb in range(2):
                            mm = e.transpose(ps[:, 4 - 2 * o + hf, tb * 256 + fb * P:tb * 256 + (fb + 1) * P],
                                             u[:, 0, 2 * hf + fb, tb * P:(tb + 1) * P], ident)
                    mm.then_inc(turned, 1)

                def spectrum(o, hf):
                    e.wait_ge(tok_ready, 2 * (2 * c + o) + hf + 1)
                    for f in range(4):
                        for kb in range(2):
                            mm = e.matmul(ps[:, 4 + 2 * hf + f // 2, (f % 2) * 256:(f % 2 + 1) * 256],
                                          fwd[:, kb, f * P:(f + 1) * P], z_tok[:, hf, kb, :],
                                          start=(kb == 0), stop=(kb == 1))
                    mm.then_inc(z_spec, 1)

                def invert(o, hf):
                    e.wait_ge(spec_v, 6 * (2 * (2 * c + o) + hf) + 6 + 6)
                    for fb in range(2):
                        for f in range(4):
                            mm = e.matmul(ps[:, 2 * o + hf, fb * TOK:(fb + 1) * TOK],
                                          y_spec[:, hf, f, fb * P:(fb + 1) * P], back[:, f, :],
                                          start=(f == 0), stop=(f == 3))
                    mm.then_inc(y_back, 1)

                def under_last(n):
                    if n == 0:
                        turn(0, 0)
                        turn(0, 1)
                    if n == 2:
                        e.wait_ge(in_fwd, 16)
                        e.wait_ge(tok_ready, 2 * (2 * c) + 2)
                        spectrum(0, 0)
                    if n == 3:
                        spectrum(0, 1)

                def under_first(n):
                    if n == 4:
                        for hf in range(2):
                            e.wait_ge(conv_v[hf], 6 * c + 1)

                for k in range(3):
                    pe_iter(e, T_HY + 3 * c + k, lat, lambda j: (norm_ready, 13 + j), None, None,
                            (under_first, None, under_last)[k])
                e.wait_ge(in_back, 16)
                e.wait_ge(psum_free, 2 * (T_HY + 3 * c + 2) + 1)
                invert(0, 0)
                invert(0, 1)
                turn(1, 0)
                spectrum(1, 0)
                turn(1, 1)
                spectrum(1, 1)
                invert(1, 0)
                invert(1, 1)
                pe_finish(e, M_HY + 4 * c + 4, FIN_HY + c, 1)
            pe_call(e, T_HOUT, 4, alt, lambda i: lambda j: (z_ready, 8), 4)
            pe_stats(e, 4, 3)
            pe_finish(e, M_END, FIN_HOUT, 1)
            with e.Fori(0, w_ff - 1) as q_:
                mlp_q(1, q_)
            mlp_q(1, w_ff - 1, 5)

        @block.scalar
        def _(e):
            e.sem_inc(hi_ready, 8)
            e.sem_inc(lo_copied, 2)
            e.sem_inc(spec_copied, 2)
            e.wait_ge(in_vecs, 16)
            e.activation(silu_e[:], vec("c", 0, 2 * KB), ACT.Exp, scale=-1.0).then_inc(silu_exp, 1)
            e.wait_ge(hid_v, 7)
            e.activation(hid_1[:], hid_a[:], ACT.Sin).then_inc(hid_sin, 1)
            e.wait_ge(hid_v, 14)
            e.activation(hid_2[:], hid_a[:], ACT.Sin).then_inc(hid_sin, 1)
            with e.Fori(0, 4) as c:
                for o in range(2):
                    e.wait_ge(spec_stored, 16 * (2 * c + o + 1))
                    for f in range(4):
                        e.wait_ge(spec_mm, 4 * (2 * c + o) + f + 1)
                        e.activation(spec[:, f], ps[:, 2 + f % 2, :], ACT.Copy).then_inc(spec_copied, 1)
                        if f == 0:
                            for b in range(4):
                                turned_taps = ps[:, 6 + b // 2, (b % 2) * TOK:(b % 2 + 1) * TOK]
                                e.activation(turned_taps, turned_taps, ACT.Square,
                                             accum_out=tap_sums[:, ds(o * KB + 4 * c + b, 1)])
                    e.wait_ge(spec_copied, 4 * (2 * c + o) + 4 + 2)
                    e.dma_start(spec_dram[ds(2 * c + o, 1)].rearrange("a p f c -> (a p) f c"), spec[:]
                                ).then_inc(spec_stored, 16)
                    if o == 0:
                        e.wait_ge(sq_summed, 2 * c + 2)
                        for k, (src, landed) in enumerate(((x, in_x), (xc, in_ctx))):
                            e.wait_ge(landed, 16 * (c + 1))
                            e.activation(sq[:, k], src[:, ds(4 * c, 4), :], ACT.Square).then_inc(squares, 1)
                e.activation(rows[:].rearrange("w (b n) -> w b n", b=2), ps[0:2, 4:6, :], ACT.Copy).then_inc(rows_copied, 1)
            act_root(e, 0, 2 * TOK, rn)
            act_root(e, 1, 32)
            e.wait_ge(spec_stored, 9 * 16)
            r = act_call(e, T_Q, 4, None, Queries, NORM_X)
            act_iter(e, T_KV, r, KeysValues(kt))
            act_iter(e, T_KV + 1, KeysValues(kt), KeysValues(vt))
            act_flush(e, T_KV + 1, KeysValues(vt))
            for h in range(2):
                e.wait_ge(psum_free, 2 * (T_KV + 2))
                e.activation(k_sq[:, 2 * h:2 * h + 2, :].rearrange("p a t -> p (a t)"), kt[:, 2 + h, :],
                             ACT.Square).then_inc(k_squared, 1)
            for hp in range(4):
                e.wait_ge(kq_sums, 1 if hp < 2 else hp)
                e.activation(k_sq[:, 2 * (hp % 2):2 * (hp % 2) + 2, :], q[:, A_HEADS + 2 * hp:A_HEADS + 2 * hp + 2, :],
                             ACT.Square).then_inc(k_squared, 1)
            for h in range(KV_HEADS):
                e.wait_ge(vt_turned, h + 1)
                e.activation(v[:, h].rearrange("p a d -> p (a d)"), ps[:, h, :], ACT.Copy).then_inc(v_ready, 1)
            act_root(e, 2, 8)
            act_root(e, 3, 16)

            def act_step(kv, i, last=False):
                n = 8 * kv + i
                if after(n, 3) and i < 11:
                    e.wait_ge(probs_turned, n - 2)
                    head = 4 * kv + (i - 3) // 2
                    if i % 2 == 1 and after(head, 2):
                        e.wait_ge(head_out, head - 1)
                    q_at = (i + 1) % 2
                    e.activation(probs_t[:, (i - 3) // 2 % 2, :, q_at * P:(q_at + 1) * P],
                                 ps[:, 3 + q_at, :].rearrange("p (k t) -> p k t", k=4), ACT.Copy).then_inc(probs_copied, 1)
                if after(n, 6) and i % 2 == 0:
                    head, at = 4 * kv + (i - 6) // 2, (i - 6) // 2 % 2
                    e.wait_ge(head_out, head + 1)
                    e.activation(alt[:, ds(head, 1), 0:TOK], ps[:, 5 + at:6 + at, 0:TOK], ACT.Copy).then_inc(head_hi, 1)
                if i < 8:
                    e.wait_ge(row_max, n + 1)
                    if after(n, 4):
                        e.wait_ge(probs_turned, n - 3)
                    m = sm[:, i % 2]
                    e.activation(probs[:, i % 4, :], ps[:, 1 + i % 2, :], ACT.Exp, bias=m[:, 0:1],
                                 scale=rs_q[:, ds(n, 1)], accum_out=m[:, 1:2])
                    e.activation(m[:, 2:3], vec("sink", 4 * kv + i // 2), ACT.Exp, bias=m[:, 0:1]).then_inc(exp_done, 1)
                if after(n, 1) and i < 9:
                    e.wait_ge(recip_v, n)
                    p_ = probs[:, (i - 1) % 4, :]
                    e.activation(p_, p_, ACT.Identity, scale=sm[:, (i - 1) % 2, 3:4]).then_inc(prob_v, 1)
                if i == 4:
                    if after(kv, 1):
                        e.wait_ge(head_out, 4 * kv)
                    e.activation(v_now[:], v[:, ds(kv, 1)].rearrange("p a k d -> p (a k) d"), ACT.Copy).then_inc(v_copied, 1)

            all_steps(e, act_step)

            def mlp(layer, q_, prev, k=None):
                T = (T_MLP0, T_MLP1)[layer] + 8 * q_
                h0, n_out = 32 * layer + 8 * q_, (OUT_M0, OUT_M1)[layer] + 8 * q_
                norm = NORM_MLP[layer] if prev is None else None
                r = act_call(e, T, 4, prev, lambda i: Hidden(i, h0), norm)
                return act_call(e, T + 4, 4, r, lambda i: Gated((G2, G4)[layer], i, n_out), None, k)

            def mlps(layer, k):
                mlp(layer, 0, None)

                def before(q_):
                    return Gated((G2, G4)[layer], 3, (OUT_M0, OUT_M1)[layer] + 8 * (q_ - 1))

                with e.Fori(1, w_ff - 1) as q_:
                    mlp(layer, q_, before(q_))
                mlp(layer, w_ff - 1, before(w_ff - 1), k)
                T = (T_MLP0, T_MLP1)[layer]
                act_flush(e, T + 31, before(w_ff))
                act_stats(e, k, 3, T + 31)

            r = act_call(e, T_OUT, 4, None, lambda i: Gated(G1, i, OUT_0), None, 2)
            act_flush(e, T_OUT + 3, r)
            act_stats(e, 2, 3, T_OUT + 3)
            act_root(e, 4, TOK, rn)
            mlps(0, 3)
            act_root(e, 5, TOK, rn)

            def hyena(c, norm=None):
                prev = None

                def copy_turned(o, hf):
                    e.wait_ge(turned, 2 * (2 * c + o) + hf + 1)
                    e.activation(z_tok[:, hf].rearrange("p a n -> p (a n)"), ps[:, 4 - 2 * o + hf, :],
                                 ACT.Copy).then_inc(tok_ready, 1)

                def under_last(n):
                    if n == 1:
                        copy_turned(0, 0)
                        copy_turned(0, 1)

                for k, part in enumerate((2, 0, 1)):
                    cur = ShortConv(k, part * KB + 4 * c, 6 * c + 2 * k)
                    act_iter(e, T_HY + 3 * c + k, prev, cur, norm if k == 0 else None, None, None,
                             under_last if k == 2 else None)
                    if norm and k == 0:
                        e.wait_ge(norm_ready, 16)
                        e.dma_start(fwd[:], a["fwd"]).then_inc(in_fwd, 16)
                        e.dma_start(back[:], a["back"]).then_inc(in_back, 16)
                    prev = cur
                act_flush(e, T_HY + 3 * c + 2, prev)
                for hf in range(2):
                    copy_turned(1, hf)
                for hf in range(2):
                    e.wait_ge(conv_v[hf], 6 * c + 6 + 1)
                    e.activation(alt[:, ds(4 * c + 2 * hf, 2), 0:TOK], u[:, 0, 2 * hf:2 * hf + 2], ACT.Copy).then_inc(z_hi, 1)
            hyena(0, NORM_HY)
            with e.Fori(1, 4) as c:
                hyena(c)
            e.wait_ge(gains, 4)
            r = act_call(e, T_HOUT, 4, None, lambda i: Gated(G3, i, OUT_H, bias=True), None, 4)
            act_flush(e, T_HOUT + 3, r)
            act_stats(e, 4, 3, T_HOUT + 3)
            act_root(e, 6, TOK, rn)
            mlps(1, 5)
            act_root(e, 7, TOK, rn)

        @block.gpsimd
        def _(e):
            e.sem_inc(pool_used, 4)
            e.wait_ge(silu_v, 3)
            e.wait_ge(vt_turned, KV_HEADS)
            for j in range(KB):
                s_ = pool_slot(j)
                e.wait_ge(pool_landed[j % RING], 16 * (j // RING + 1))
                if j == 0:
                    e.tensor_scalar(acc_pool, s_, silu[:, 0:1], None, ALU.mult).then_inc(pool_used, 1)
                else:
                    e.tensor_scalar(s_, s_, silu[:, j:j + 1], None, ALU.mult).then_inc(pool_scaled, 1)
                    e.wait_ge(pool_scaled, j)
                    e.wait_ge(pool_used, 4 + j)
                    e.tensor_tensor(acc_pool, acc_pool, s_, ALU.add).then_inc(pool_used, 1)

        @block.vector
        def _(e):
            e.sem_inc(split_ready, 8)
            e.sem_inc(psum_free, 2)
            e.sem_inc(slabs_used, 4)
            for j in range(START_RING):
                e.sem_inc(start_free[j], 1)
            e.sem_inc(mod_ready, 1)
            e.sem_inc(taps_ready, 4)
            e.sem_inc(sq_summed, 2)
            e.sem_inc(start_summed, 1)
            e.sem_inc(spec_stored, 16)
            e.sem_inc(head_ready, 2)
            e.sem_inc(spec_v, 6)
            for hf in range(2):
                e.sem_inc(conv_v[hf], 1)
            e.memset(ones[:], 1.0).then_inc(started, 1)
            e.wait_ge(silu_exp, 1)
            e.tensor_scalar(silu_e[:], silu_e[:], 1.0, None, ALU.add).then_inc(silu_v, 1)
            e.wait_ge(silu_v, 1)
            e.reciprocal(silu[:], silu_e[:]).then_inc(silu_v, 1)
            e.wait_ge(silu_v, 2)
            e.tensor_tensor(silu[:], silu[:], vec("c", 0, 2 * KB), ALU.mult).then_inc(silu_v, 1)

            def hidden_arg(n, b, fr):
                e.wait_ge(hid_mm, n + 1)
                e.tensor_scalar(hid_a[:], ps[0:HID, n, 0:TOK], b, fr, ALU.add, ALU.mult).then_inc(hid_v, 1)
                e.wait_ge(hid_v, 7 * n + 1)
                e.tensor_scalar(hid_k[:], hid_a[:], 1.0 / (2.0 * math.pi), MAGIC, ALU.mult, ALU.add).then_inc(hid_v, 1)
                e.wait_ge(hid_v, 7 * n + 2)
                e.tensor_scalar(hid_k[:], hid_k[:], MAGIC, None, ALU.subtract).then_inc(hid_v, 1)
                parts = [6.28125, 0.0019340515136718750]
                parts.append(2.0 * math.pi - sum(parts))
                for m, part in enumerate(parts):
                    e.wait_ge(hid_v, 7 * n + 3 + m)
                    e.scalar_tensor_tensor(hid_a[:], hid_k[:], -part, hid_a[:], ALU.mult, ALU.add).then_inc(hid_v, 1)
                e.wait_ge(hid_v, 7 * n + 6)
                e.tensor_scalar(hid_a[:], hid_a[:], 3.1415925, -3.1415925, ALU.min, ALU.max).then_inc(hid_v, 1)

            e.wait_ge(in_fw, 16)
            b1, fr1, b2, fr2 = (f_w[:, 2 * HID + n:2 * HID + n + 1] for n in range(4))
            hidden_arg(0, b1, fr1)
            hidden_arg(1, b2, fr2)
            with e.Fori(0, 2) as cc:
                for par in range(2):
                    c = 2 * cc + par
                    sums = (acc, acc_odd)[par]
                    mine = [j for j in range(16) if j not in PE_SLABS]
                    for r, j in enumerate(mine):
                        if r in (1, 6):
                            o = r // 6
                            e.wait_ge(taps_mm, 2 * c + o + 5)
                            e.wait_ge(in_decay[par], 16 * (cc + 1))
                            e.tensor_tensor(taps[:, o], ps[:, 0:2, :], decay[:, par], ALU.mult).then_inc(taps_ready, 1)
                        e.wait_ge(start_landed[j % START_RING], 16 * (2 * c + j // START_RING + 1))
                        s_ = start_slot(j)
                        if r == 0:
                            e.tensor_scalar(sums[:, 0], s_, silu[:, 0:1], None, ALU.mult).then_inc(acc_ready, 1)
                            e.tensor_scalar(sums[:, 1], s_, silu[:, KB:KB + 1], None,
                                            ALU.mult).then_inc(start_free[j % START_RING], 1)
                        else:
                            before = mine[r - 1]
                            e.wait_ge(acc_ready, len(mine) * c + r)
                            e.scalar_tensor_tensor(sums[:, 0], s_, silu[:, j:j + 1], sums[:, 0],
                                                   ALU.mult, ALU.add).then_inc(acc_ready, 1)
                            e.wait_ge(start_free[before % START_RING], 2 * c + before // START_RING + 2)
                            e.scalar_tensor_tensor(sums[:, 1], s_, silu[:, KB + j:KB + j + 1], sums[:, 1],
                                                   ALU.mult, ALU.add).then_inc(start_free[j % START_RING], 1)
                    for k in range(2):
                        e.wait_ge(squares, 2 * c + k + 1)
                        e.tensor_reduce(sum_sq[:, ds(c, 1), k * TOK:(k + 1) * TOK].rearrange("p a t -> p (a t)"),
                                        sq[:, k].rearrange("p k t -> p t k"), AX.X, ALU.add).then_inc(sq_summed, 1)
                    e.wait_ge(start_turned, c + 1)
                    for w in range(2):
                        ins = e.tensor_reduce(mod_part[:, w], ps[:, 4 + 2 * w:6 + 2 * w, :].rearrange(
                            "p a (b k) -> p (a b) k", k=P), AX.X, ALU.add)
                    ins.then_inc(silu_v, 1)
                    e.wait_ge(silu_v, 4 + c)
                    e.tensor_tensor(start_part[:, :, ds(half * c, half)], mod_part[:],
                                    ps[:, 0, 0:2 * half].rearrange("p (b w) -> p w b", w=2), ALU.add).then_inc(start_summed, 1)
            e.wait_ge(start_summed, 5)
            for w, dst in enumerate((mod, mod_ctx)):
                ins = e.tensor_tensor(dst[:, 0:2 * KB], start_part[:, w], vec("mod_b", 0, 2 * KB), ALU.add)
            ins.then_inc(mod_ready, 1)
            e.sem_inc(mod_summed, 1)
            dve_rsqrt(e, 0, ps[:, 1, :], 2 * TOK, 1.0 / D, EPS, rs_tok[:], (square_sums, 8), temps=rn)
            dve_rsqrt(e, 1, tap_sums[:], 32, 1.0, EPS, rs_filter[:], (rows_copied, 4))
            e.wait_ge(mod_ready, 2)
            dve_gain(e, 1, gain[:, 0:KB], mods(0, 1), vec("mix_g", 0, KB))
            dve_gain(e, 2, gain[:, KB:2 * KB], mod_ctx[:, KB:2 * KB], vec("mix_g", 0, KB))
            r = dve_call(e, T_Q, 4, None, Queries, SL_Q, None, NORM_X)
            dve_finish(e, FIN_Q, [mod_col(0, 4)])
            dve_iter(e, T_KV, r, KeysValues(kt), 0, SL_KV)
            dve_iter(e, T_KV + 1, KeysValues(kt), KeysValues(vt), 1, SL_KV)
            dve_flush(e, T_KV + 1, KeysValues(vt))
            dve_finish(e, FIN_KV, [mod_col(0, 5), mod_col(0, 6)])
            e.wait_ge(in_rope, 16)
            qn, kn = vec("q_norm"), vec("k_norm")
            e.tensor_scalar(neg_sink[:], vec("sink", 0, HEADS), -1.0, None, ALU.mult)
            e.memset(rs_q[:, 0:2 * A_HEADS], 1.0).then_inc(b_scaled, 1)
            e.wait_ge(k_squared, 2)
            e.tensor_scalar(kt[:, 2:4, :], kt[:, 2:4, :], kn, None, ALU.mult).then_inc(b_scaled, 1)
            sin_b = sin.rearrange("p (a t) -> p a t", a=1).to_broadcast([P, 2, TOK])

            def rotate(dst, src, bank, done, n):
                tb_ = cos.rearrange("p (a t) -> p a t", a=1).to_broadcast([P, 2, TOK])
                e.tensor_tensor(q_sin[:], ps[:, bank, :].rearrange("p (a t) -> p a t", a=2), sin_b, ALU.mult)
                e.tensor_tensor(dst, src, tb_, ALU.mult).then_inc(done, 1)
                e.wait_ge(done, n + 1)
                e.tensor_tensor(dst, dst, q_sin[:], ALU.add).then_inc(done, 1)
                e.wait_ge(done, n + 2)

            e.wait_ge(k_swapped, 1)
            rotate(kt[:, 0:2, 0:TOK], kt[:, 0:2, 0:TOK], 4, k_v, 0)
            dve_rsqrt(e, 2, ps[:, 6, 0:8], 8, 1.0 / HEAD, EPS, rs_k[:], (kq_sums, 1))
            e.wait_ge(k_swapped, 2)
            rotate(kt[:, 2:4, 0:TOK], kt[:, 2:4, 0:TOK], 5, k_v, 2)
            e.wait_ge(k_squared, 6)
            e.tensor_scalar(q[:, A_HEADS:HEADS, :], q[:, A_HEADS:HEADS, :], qn, None, ALU.mult).then_inc(b_scaled, 1)
            dve_rsqrt(e, 3, ps[:, 6, 16:32], 16, 1.0 / HEAD, EPS * QSCALE * QSCALE, rs_q[:, 2 * A_HEADS:], (kq_sums, 5))
            e.wait_ge(rs_v, 6 * 3 + 6)
            e.tensor_scalar(rs_q[:, 2 * A_HEADS:], rs_q[:, 2 * A_HEADS:], QSCALE, None, ALU.mult).then_inc(k_v, 1)
            e.wait_ge(k_spread, 1)
            for h in range(2):
                kl, kc = kt[:, 2 + h, 0:TOK], kt[:, 2 + h, TOK:2 * TOK]
                e.tensor_tensor(kl, kl, ps[:, h, 0:TOK], ALU.mult)
                ins = e.tensor_tensor(kc, kc, ps[:, h, TOK:2 * TOK], ALU.mult)
            ins.then_inc(k_v, 1)
            e.wait_ge(k_v, 6)
            def rotate_pair(pair, at):
                e.wait_ge(q_swapped, pair + 1)
                hq = q[:, ds(2 * pair, 2), :]
                cos_b = cos.rearrange("p (a t) -> p a t", a=1).to_broadcast([P, 2, TOK])
                e.tensor_tensor(q_sin[:], ps[:, 0, :].rearrange("p (a t) -> p a t", a=2), sin_b, ALU.mult).then_inc(q_v, 1)
                e.tensor_tensor(q_rot[:, at], hq, cos_b, ALU.mult).then_inc(q_v, 1)
                e.wait_ge(q_v, 3 * pair + 2)
                e.tensor_tensor(q_rot[:, at], q_rot[:, at], q_sin[:], ALU.add).then_inc(q_v, 1)
                e.wait_ge(q_v, 3 * pair + 3)

            def dve_step(kv, i, last=False):
                n = 8 * kv + i
                if i < 8:
                    m, s_ = sm[:, i % 2], ps[:, 1 + i % 2, :]
                    e.wait_ge(scores, n + 1)
                    if after(n, 2):
                        e.wait_ge(prob_v, n - 1)
                    part = s_[:, (1 - i % 2) * P:(2 - i % 2) * P]
                    e.tensor_tensor(part, part, mask[:, ds(kv, 1), i % 2, :], ALU.add).then_inc(scored_v, 1)
                    e.wait_ge(scored_v, 2 * n + 1)
                    e.tensor_reduce(m[:, 3:4], s_, AX.X, ALU.max, negate=True).then_inc(scored_v, 1)
                    e.wait_ge(scored_v, 2 * n + 2)
                    e.scalar_tensor_tensor(m[:, 0:1], m[:, 3:4], rs_q[:, ds(n, 1)], neg_sink[:, ds(4 * kv + i // 2, 1)],
                                           ALU.mult, ALU.min).then_inc(row_max, 1)
                if after(n, 1) and i < 9:
                    m = sm[:, (i - 1) % 2]
                    e.wait_ge(exp_done, n)
                    e.tensor_tensor(m[:, 1:2], m[:, 1:2], m[:, 2:3], ALU.add).then_inc(scored_w, 1)
                    e.wait_ge(scored_w, n)
                    e.reciprocal(m[:, 3:4], m[:, 1:2]).then_inc(recip_v, 1)
                if i == 2:
                    rotate_pair(2 * kv + 1, 1)
                if i == 6 and not last:
                    rotate_pair(2 * kv + 2, 0)
                if i < 8:
                    dve_slabs(e, SL_ATT, kv, i, 1)
                if after(n, 6) and i % 2 == 0:
                    head, at = 4 * kv + (i - 6) // 2, (i - 6) // 2 % 2
                    e.wait_ge(head_hi, head + 1)
                    e.tensor_tensor(alt[:, ds(head, 1), TOK:2 * TOK], ps[:, 5 + at:6 + at, 0:TOK],
                                    alt[:, ds(head, 1), 0:TOK].bitcast(F32), ALU.subtract).then_inc(head_ready, 1)

            rotate_pair(0, 0)
            all_steps(e, dve_step)
            r = dve_call(e, T_OUT, 4, None, lambda i: Gated(G1, i, OUT_0), SL_OUT,
                         (FIN_ATT, [mod_col(0, 8), mod_col(0, 9)]))
            dve_flush(e, T_OUT + 3, r)
            dve_finish(e, FIN_OUT, [mod_col(0, 7), mod_col(0, 10)])
            dve_stats(e, 2, 4)
            e.wait_ge(mod_ready, FIN_OUT + 2)
            dve_gain(e, 3, gain[:, 0:KB], mods(0, 4), vec("mlp_g", 0, KB))

            def mlp(layer, q_, prev, sl_up, sl_down, fin_before, fin_mid):
                T = (T_MLP0, T_MLP1)[layer] + 8 * q_
                h0, n_out = 32 * layer + 8 * q_, (OUT_M0, OUT_M1)[layer] + 8 * q_
                norm = NORM_MLP[layer] if prev is None else None
                r = dve_call(e, T, 4, prev, lambda i: Hidden(i, h0), sl_up, fin_before, norm)
                return dve_call(e, T + 4, 4, r, lambda i: Gated((G2, G4)[layer], i, n_out), sl_down, fin_mid)

            mlp(0, 0, None, SL_UP0, sl_mlp0(0, 1), None, (FIN_MLP0, [mod_col(0, 11)]))
            with e.Fori(1, w_ff) as q_:
                mlp(0, q_, Gated(G2, 3, OUT_M0 + 8 * (q_ - 1)), sl_mlp0(q_, 0), sl_mlp0(q_, 1),
                    (FIN_MLP0 + 2 * q_ - 1, [mod_col(1, 2 * q_ - 2)]), (FIN_MLP0 + 2 * q_, [mod_col(1, 2 * q_ - 1)]))
            dve_flush(e, T_MLP0 + 31, Gated(G2, 3, OUT_M0 + 24))
            dve_stats(e, 3, 5)
            e.wait_ge(mod_ready, FIN_HY)
            e.tensor_tensor(gate_bias[:], mods(1, 2), vec("b_out", 0, KB), ALU.mult)
            dve_gain(e, 4, gain[:, 0:KB], mods(1, 1), vec("mix_g", KB, KB))

            def hyena(c, before, norm=None):
                prev = None

                def multiply(o, hf):
                    m = 2 * (2 * c + o) + hf
                    e.wait_ge(z_spec, m + 1)
                    e.wait_ge(h_landed, 16 * (2 * c + o + 1))
                    zr, zi = (ps[:, 4 + 2 * hf + n, :].rearrange("p (f n) -> p f n", f=2) for n in range(2))
                    hr, hi = (h_spec[:, 2 * n:2 * n + 2, hf * 256:(hf + 1) * 256] for n in range(2))
                    yr, yi, tmp = y_spec[:, hf, 0:2], y_spec[:, hf, 2:4], z_tok[:, hf]
                    n0 = 6 * m + 6
                    e.tensor_tensor(yr, zr, hr, ALU.mult).then_inc(spec_v, 1)
                    e.tensor_tensor(tmp, zi, hi, ALU.mult).then_inc(spec_v, 1)
                    e.wait_ge(spec_v, n0 + 2)
                    e.tensor_tensor(yr, yr, tmp, ALU.subtract).then_inc(spec_v, 1)
                    e.tensor_tensor(yi, zr, hi, ALU.mult).then_inc(spec_v, 1)
                    e.wait_ge(spec_v, n0 + 4)
                    e.tensor_tensor(tmp, zi, hr, ALU.mult).then_inc(spec_v, 1)
                    e.wait_ge(spec_v, n0 + 5)
                    e.tensor_tensor(yi, yi, tmp, ALU.add).then_inc(spec_v, 1)

                def skip(o, hf):
                    for fb in range(2 * hf, 2 * hf + 2):
                        ins = e.tensor_scalar(u[:, 0, fb], u[:, 0, fb], vec("skip", o * KB + 4 * c + fb), None, ALU.mult)
                    ins.then_inc(conv_v[hf], 1)

                def under_last(n):
                    if n in (5, 7):
                        multiply(0, (n - 5) // 2)
                        skip(0, (n - 5) // 2)

                for k, part in enumerate((2, 0, 1)):
                    cur = ShortConv(k, part * KB + 4 * c, 6 * c + 2 * k)
                    dve_iter(e, T_HY + 3 * c + k, prev, cur, k, sl_hy(c),
                             before if k == 0 else None, norm if k == 0 else None,
                             None, under_last if k == 2 else None)
                    prev = cur
                dve_flush(e, T_HY + 3 * c + 2, prev)

                def combine(o, hf):
                    e.wait_ge(conv_v[hf], 6 * c + 3 * o + 1 + 1)
                    e.wait_ge(y_back, 2 * (2 * c + o) + hf + 1)
                    for fb in range(2):
                        z = u[:, 0, 2 * hf + fb]
                        ins = e.scalar_tensor_tensor(z, ps[:, 2 * o + hf, fb * TOK:(fb + 1) * TOK],
                                                     rs_filter[:, ds(o * KB + 4 * c + 2 * hf + fb, 1)], z,
                                                     ALU.mult, ALU.add)
                    ins.then_inc(conv_v[hf], 1)
                    e.wait_ge(conv_v[hf], 6 * c + 3 * o + 2 + 1)
                    z = u[:, 0, 2 * hf:2 * hf + 2]
                    e.tensor_tensor(z, z, u[:, 1 + o, 2 * hf:2 * hf + 2], ALU.mult).then_inc(conv_v[hf], 1)

                combine(0, 0)
                combine(0, 1)
                dve_slabs(e, sl_hy(c), 3, 0, 1)
                multiply(1, 0)
                skip(1, 0)
                multiply(1, 1)
                skip(1, 1)
                dve_slabs(e, sl_hy(c), 3, 1, 1)
                combine(1, 0)
                dve_slabs(e, sl_hy(c), 3, 2, 1)
                combine(1, 1)
                dve_slabs(e, sl_hy(c), 3, 3, 1)
                for hf in range(2):
                    e.wait_ge(z_hi, 2 * c + hf + 1)
                    e.tensor_tensor(alt[:, ds(4 * c + 2 * hf, 2), TOK:2 * TOK], u[:, 0, 2 * hf:2 * hf + 2],
                                    alt[:, ds(4 * c + 2 * hf, 2), 0:TOK].bitcast(F32),
                                    ALU.subtract).then_inc(z_ready, 1)

            hyena(0, (FIN_MLP0 + 7, [mod_col(1, 6)]), NORM_HY)
            with e.Fori(1, 4) as c:
                hyena(c, (FIN_HY + c - 1, [mod_col(1, 6 + c)]))
            dve_finish(e, FIN_HY + 3, [mod_col(1, 10)])
            r = dve_call(e, T_HOUT, 4, None, lambda i: Gated(G3, i, OUT_H), SL_HOUT)
            dve_flush(e, T_HOUT + 3, r)
            dve_stats(e, 4, 6)
            e.wait_ge(mod_ready, FIN_HOUT + 1)
            dve_gain(e, 5, gain[:, 0:KB], mods(1, 4), vec("mlp_g", KB, KB))
            mlp(1, 0, None, None, None, (FIN_HOUT, [mod_col(1, 11)]), None)
            with e.Fori(1, w_ff) as q_:
                mlp(1, q_, Gated(G4, 3, OUT_M1 + 8 * (q_ - 1)), None, None, None, None)
            dve_flush(e, T_MLP1 + 31, Gated(G4, 3, OUT_M1 + 24))
            dve_stats(e, 5, 7)
            for c in range(4):
                if c >= 2:
                    e.wait_ge(stored[c - 2], 16)
                dve_normalise(e, 5, x, vec("final_g", 0, KB), None, c)


def columns(v):
    return v.reshape(-1, P).T


def kernel(**inputs):
    import concourse.bacc as bacc
    from concourse.bass_utils import run_bass_kernel_spmd

    i = {k: np.asarray(v_) for k, v_ in inputs.items()}
    arrays = constants()
    feature_major = lambda t: np.ascontiguousarray(t.T.reshape(KB, P, TOK).transpose(1, 0, 2))
    arrays["x"] = feature_major(i["x"][0])
    arrays["ctx"] = feature_major(i["ctx"][0])
    arrays["vecs"] = np.ascontiguousarray(np.concatenate([
        columns(i["c"]), columns(i["c_ctx"]), columns(i["mod_b"]), columns(i["norm_mix_g"]), columns(i["norm_mlp_g"]),
        columns(i["final_g"]), columns(i["hy_b_in"]), columns(i["hy_conv_w"]), columns(i["hy_conv_b"]),
        columns(i["hy_skip"]), columns(i["hy_b_out"]), columns(i["attn_q_norm"]), columns(i["attn_k_norm"]),
        np.broadcast_to(i["attn_sink"], (P, A_HEADS)), np.full((P, HEADS - A_HEADS), NO_SINK, np.float32)], 1))
    f_w1 = np.zeros((HID, HID), np.float32)
    f_w1[:FILTER_EMB] = i["hy_f_w1"][0]
    arrays["f_w"] = np.ascontiguousarray(np.concatenate([
        f_w1, i["hy_f_w2"][0], i["hy_f_b1"].T, i["hy_f_freq1"].T, i["hy_f_b2"].T, i["hy_f_freq2"].T], 1))
    arrays["w3"] = i["hy_f_w3"][0].reshape(HID, 2, D)
    arrays["mod_w"] = i["mod_w"]
    for name in ("attn_w_in", "attn_w_out", "hy_w_in", "hy_w_out"):
        arrays[name] = i[name][0]
    for layer in range(2):
        arrays[f"mlp_w1_{layer}"] = i["mlp_w1"][layer]
        arrays[f"mlp_w2_{layer}"] = i["mlp_w2"][layer]
    nc = bacc.Bacc("TRN2", target_bir_lowering=False, num_devices=1)
    a = {k: nc.dram_tensor(f"in_{k}", v_.shape, F32, kind="ExternalInput").ap() for k, v_ in arrays.items()}
    a["y"] = nc.dram_tensor("out_y", (P, KB, TOK), F32, kind="ExternalOutput").ap()
    build(nc, a)
    r = run_bass_kernel_spmd(nc, [{f"in_{k}": v_ for k, v_ in arrays.items()}], core_ids=[0])
    y = r.results[0]["out_y"]
    return np.ascontiguousarray(y.transpose(1, 0, 2).reshape(D, TOK).T)[None]
```
